# Optimizing a Trainium2 kernel written in Bass

```python
import math
import jax, jax.numpy as jnp
from jax import lax
import numpy as np
import jax
import jax.numpy as jnp

D_MODEL = 1024
BATCH = 1
SEQ = 512
DEPTH = 2

N_A = DEPTH // 2
N_B = DEPTH - N_A
N_HEADS = 16
HEAD_DIM = D_MODEL // N_HEADS
CONV_W = 31
FFN_DIM = 2816
FFN_CONV_W = 3
PLE_DIM = 256
Q_BLOCK = 128
LN_EPS = 1e-5
DN_ALPHA = (2.0 * DEPTH) ** 0.25
DN_BETA = (8.0 * DEPTH) ** -0.25


def layer_norm(x, g, b):
    xf = x.astype(jnp.float32)
    mu = jnp.mean(xf, axis=-1, keepdims=True)
    var = jnp.mean(jnp.square(xf - mu), axis=-1, keepdims=True)
    y = (xf - mu) * lax.rsqrt(var + LN_EPS)
    return (y * g.astype(jnp.float32) + b.astype(jnp.float32)).astype(x.dtype)

def causal_dwconv(x, w, b):
    k = w.shape[0]
    y = lax.conv_general_dilated(
        x, w[:, None, :].astype(x.dtype), window_strides=(1,), padding=[(k - 1, 0)],
        dimension_numbers=("NWC", "WIO", "NWC"), feature_group_count=x.shape[-1])
    return y + b

def conformer_conv(x, pw1_w, pw1_b, dw_w, dw_b, ln_g, ln_b, pw2_w, pw2_b):
    h = x @ pw1_w + pw1_b
    a, g = jnp.split(h, 2, axis=-1)
    h = a * jax.nn.sigmoid(g)
    h = causal_dwconv(h, dw_w, dw_b)
    h = layer_norm(h, ln_g, ln_b)
    h = jax.nn.silu(h)
    return h @ pw2_w + pw2_b

def stick_breaking_attention(q, k, v):
    b, s, h, dh = q.shape
    nb = s // Q_BLOCK
    scale = 1.0 / math.sqrt(dh)
    kh = jnp.transpose(k, (0, 2, 1, 3))
    vh = jnp.transpose(v, (0, 2, 1, 3))
    qb = jnp.transpose(q.reshape(b, nb, Q_BLOCK, h, dh), (1, 0, 3, 2, 4))
    t0s = jnp.arange(nb, dtype=jnp.int32) * Q_BLOCK
    ts = jnp.arange(s, dtype=jnp.int32)

    def block(args):
        qblk, t0 = args
        z = jnp.einsum('bhqd,bhkd->bhqk', qblk, kh).astype(jnp.float32) * scale
        tq = t0 + jnp.arange(Q_BLOCK, dtype=jnp.int32)
        mask = ts[None, :] < tq[:, None]
        log_1m = jnp.where(mask, jax.nn.log_sigmoid(-z), 0.0)
        rev = lax.cumsum(log_1m, axis=3, reverse=True)
        log_a = jax.nn.log_sigmoid(z) + (rev - log_1m)
        a = jnp.where(mask, jnp.exp(log_a), 0.0)
        return jnp.einsum('bhqk,bhkd->bhqd', a.astype(vh.dtype), vh)

    out = lax.map(block, (qb, t0s))
    return jnp.transpose(out, (1, 0, 3, 2, 4)).reshape(b, s, h * dh)

def conv_gated_ffn(x, w_up, w_gate, conv_w, conv_b, w_down):
    u = x @ w_up
    g = causal_dwconv(x @ w_gate, conv_w, conv_b)
    return (jax.nn.silu(g) * u) @ w_down

def first_inputs(seed: int = 0) -> dict:
    key = jax.random.key(seed)
    ks = jax.random.split(key, 32)
    D, F = D_MODEL, FFN_DIM

    def nrm(k, shape, scale):
        return jax.random.normal(k, shape, jnp.float32) * scale

    return {
        "x": nrm(ks[0], (BATCH, SEQ, D), 1.0),
        "p": nrm(ks[1], (DEPTH, BATCH, SEQ, PLE_DIM), 1.0),
        "a_pw1_w": nrm(ks[2], (N_A, D, 2 * D), D ** -0.5),
        "a_pw1_b": nrm(ks[3], (N_A, 2 * D), 0.02),
        "a_dw_w": nrm(ks[4], (N_A, CONV_W, D), CONV_W ** -0.5),
        "a_dw_b": nrm(ks[5], (N_A, D), 0.02),
        "a_ln_g": 1.0 + nrm(ks[6], (N_A, D), 0.02),
        "a_ln_b": nrm(ks[7], (N_A, D), 0.02),
        "a_pw2_w": nrm(ks[8], (N_A, D, D), D ** -0.5 * DN_BETA),
        "a_pw2_b": nrm(ks[9], (N_A, D), 0.02),
        "b_wq": nrm(ks[10], (N_B, D, D), D ** -0.5),
        "kv_wk": nrm(ks[11], (D, D), D ** -0.5),
        "kv_wv": nrm(ks[12], (D, D), D ** -0.5 * DN_BETA),
        "b_wo": nrm(ks[13], (N_B, D, D), D ** -0.5 * DN_BETA),
        "ln_mix_g": 1.0 + nrm(ks[14], (DEPTH, D), 0.02),
        "ln_mix_b": nrm(ks[15], (DEPTH, D), 0.02),
        "ffn_w_up": nrm(ks[16], (DEPTH, D, F), D ** -0.5),
        "ffn_w_gate": nrm(ks[17], (DEPTH, D, F), D ** -0.5),
        "ffn_conv_w": nrm(ks[18], (DEPTH, FFN_CONV_W, F), FFN_CONV_W ** -0.5),
        "ffn_conv_b": nrm(ks[19], (DEPTH, F), 0.02),
        "ffn_w_down": nrm(ks[20], (DEPTH, F, D), F ** -0.5 * DN_BETA),
        "ple_w_gate": nrm(ks[21], (DEPTH, D, D), D ** -0.5),
        "ple_w_proj": nrm(ks[22], (DEPTH, PLE_DIM, D), PLE_DIM ** -0.5 * DN_BETA),
        "ln_ffn_g": 1.0 + nrm(ks[23], (DEPTH, D), 0.02),
        "ln_ffn_b": nrm(ks[24], (DEPTH, D), 0.02),
    }

def first_block(x, p, a_pw1_w, a_pw1_b, a_dw_w, a_dw_b, a_ln_g, a_ln_b, a_pw2_w, a_pw2_b,
              b_wq, kv_wk, kv_wv, b_wo, ln_mix_g, ln_mix_b,
              ffn_w_up, ffn_w_gate, ffn_conv_w, ffn_conv_b, ffn_w_down,
              ple_w_gate, ple_w_proj, ln_ffn_g, ln_ffn_b):
    b, s, d = x.shape
    k_shared = None
    v_shared = None
    for i in range(DEPTH):
        if i < N_A:
            mix = conformer_conv(x, a_pw1_w[i], a_pw1_b[i], a_dw_w[i], a_dw_b[i],
                                 a_ln_g[i], a_ln_b[i], a_pw2_w[i], a_pw2_b[i])
        else:
            j = i - N_A
            if k_shared is None:
                k_shared = (x @ kv_wk).reshape(b, s, N_HEADS, HEAD_DIM)
                v_shared = (x @ kv_wv).reshape(b, s, N_HEADS, HEAD_DIM)
            q = (x @ b_wq[j]).reshape(b, s, N_HEADS, HEAD_DIM)
            mix = stick_breaking_attention(q, k_shared, v_shared) @ b_wo[j]
        x = layer_norm(DN_ALPHA * x + mix, ln_mix_g[i], ln_mix_b[i])
        ffn = conv_gated_ffn(x, ffn_w_up[i], ffn_w_gate[i], ffn_conv_w[i], ffn_conv_b[i], ffn_w_down[i])
        ple = jax.nn.sigmoid(x @ ple_w_gate[i]) * (p[i] @ ple_w_proj[i])
        x = layer_norm(DN_ALPHA * x + ffn + ple, ln_ffn_g[i], ln_ffn_b[i])
    return x


DEPTH_2 = 1

HEAD_DIM_2 = 64
ROPE_DIM = HEAD_DIM_2 // 4
ROPE_THETA = 500000.0
DIFF_HEADS = 4
DIFF_V_DIM = 2 * HEAD_DIM_2
NSA_HEADS = 8
NSA_KV_HEADS = 2
NSA_GROUP = NSA_HEADS // NSA_KV_HEADS
N_BRANCH = 3
CMP_BLOCK = 32
CMP_STRIDE = 16
CMP_HIDDEN = 4 * HEAD_DIM_2
SEL_BLOCK = 64
SEL_TOP_N = 16
WINDOW = 512
D_FF = 2816
SEL_Q_CHUNK = 64
MIX_WIDTH = DIFF_HEADS * DIFF_V_DIM + NSA_HEADS * HEAD_DIM_2
IN_SIZES = (DIFF_HEADS * 2 * HEAD_DIM_2, DIFF_HEADS * 2 * HEAD_DIM_2, DIFF_HEADS * DIFF_V_DIM,
            NSA_HEADS * HEAD_DIM_2) + (NSA_KV_HEADS * HEAD_DIM_2,) * 6 + (NSA_HEADS * N_BRANCH,)
IN_WIDTH = sum(IN_SIZES)
EPS = 1e-6
NEG_INF = -1e30
FORCE_SCORE = 1e9


def rms_norm(x, g):
    xf = x.astype(jnp.float32)
    y = xf * lax.rsqrt(jnp.mean(xf * xf, axis=-1, keepdims=True) + EPS)
    return (y * g.astype(jnp.float32)).astype(x.dtype)

def rope_tables(S):
    pos = jnp.arange(S, dtype=jnp.float32)
    inv = ROPE_THETA ** (-jnp.arange(0, ROPE_DIM, 2, dtype=jnp.float32) / ROPE_DIM)
    ang = pos[:, None] * inv[None, :]
    return jnp.cos(ang), jnp.sin(ang)

def partial_rope(x, cos, sin):
    xr = x[..., :ROPE_DIM].astype(jnp.float32)
    x1, x2 = xr[..., :ROPE_DIM // 2], xr[..., ROPE_DIM // 2:]
    rot = jnp.concatenate([x1 * cos - x2 * sin, x2 * cos + x1 * sin], axis=-1)
    return jnp.concatenate([rot.astype(x.dtype), x[..., ROPE_DIM:]], axis=-1)

def swiglu(h, w_gate, w_up, w_down):
    return (jax.nn.silu(h @ w_gate) * (h @ w_up)) @ w_down

def diff_attention(q, k, v, lam, subln_g, lambda_init):
    B, Hd, _, S, dh = q.shape
    nb = S // Q_BLOCK
    scale = dh ** -0.5
    qb = q.reshape(B, Hd, 2, nb, Q_BLOCK, dh).transpose(3, 0, 1, 2, 4, 5)
    kpos = jnp.arange(S)

    def block(args):
        qi, i = args
        s = jnp.einsum('bhmqd,bhmkd->bhmqk', qi, k).astype(jnp.float32) * scale
        qpos = i * Q_BLOCK + jnp.arange(Q_BLOCK)
        s = jnp.where(kpos[None, :] <= qpos[:, None], s, NEG_INF)
        p = jax.nn.softmax(s, axis=-1)
        a = p[:, :, 0] - lam * p[:, :, 1]
        return jnp.einsum('bhqk,bhkd->bhqd', a.astype(v.dtype), v)

    o = lax.map(block, (qb, jnp.arange(nb)))
    o = o.transpose(1, 2, 0, 3, 4).reshape(B, Hd, S, 2 * dh)
    o = rms_norm(o, subln_g) * (1.0 - lambda_init)
    return o.transpose(0, 2, 1, 3).reshape(B, S, Hd * 2 * dh)

def compress(x, pe, w1, w2):
    B, G, S, dh = x.shape
    r = CMP_BLOCK // CMP_STRIDE
    nc = S // CMP_STRIDE - r + 1
    sub = x.reshape(B, G, S // CMP_STRIDE, CMP_STRIDE, dh)
    blocks = jnp.concatenate([sub[:, :, j:j + nc] for j in range(r)], axis=3)
    blocks = (blocks + pe).reshape(B, G, nc, CMP_BLOCK * dh)
    return jax.nn.gelu(blocks @ w1) @ w2

def sel_overlap(nc, n_sel):
    cs = np.arange(nc)[:, None] * CMP_STRIDE
    ss = np.arange(n_sel)[None, :] * SEL_BLOCK
    ov = np.minimum(cs + CMP_BLOCK, ss + SEL_BLOCK) - np.maximum(cs, ss)
    return jnp.asarray(np.clip(ov, 0, None) / CMP_BLOCK, dtype=jnp.float32)

def nsa_attention(q, k_cmp, v_cmp, k_sel, v_sel, k_win, v_win, gates,
                  pe_k, wk1, wk2, pe_v, wv1, wv2):
    B, H, S, dh = q.shape
    G, Hg = NSA_KV_HEADS, NSA_GROUP
    scale = dh ** -0.5
    qg = q.reshape(B, G, Hg, S, dh)
    t = jnp.arange(S)

    kc = compress(k_cmp, pe_k, wk1, wk2)
    vc = compress(v_cmp, pe_v, wv1, wv2)
    nc = kc.shape[2]
    cend = jnp.arange(nc) * CMP_STRIDE + CMP_BLOCK - 1
    cvalid = cend[None, :] <= t[:, None]
    s = jnp.einsum('bghsd,bgcd->bghsc', qg, kc).astype(jnp.float32) * scale
    p_cmp = jnp.where(cvalid, jax.nn.softmax(jnp.where(cvalid, s, NEG_INF), axis=-1), 0.0)
    o_cmp = jnp.einsum('bghsc,bgcd->bghsd', p_cmp.astype(vc.dtype), vc)

    n_sel = S // SEL_BLOCK
    top_n = min(SEL_TOP_N, n_sel)
    imp = jnp.einsum('bghsc,cj->bgsj', p_cmp, sel_overlap(nc, n_sel))
    blk = jnp.arange(n_sel)[None, :]
    cur = (t // SEL_BLOCK)[:, None]
    causal_blk = blk * SEL_BLOCK <= t[:, None]
    forced = (blk == 0) | ((blk <= cur) & (blk >= cur - 1))
    imp = jnp.where(forced, FORCE_SCORE, jnp.where(causal_blk, imp, -1.0))
    _, idx = lax.top_k(imp, top_n)

    kb = k_sel.reshape(B, G, n_sel, SEL_BLOCK, dh)
    vb = v_sel.reshape(B, G, n_sel, SEL_BLOCK, dh)
    C = SEL_Q_CHUNK
    nq = S // C
    q_c = qg.reshape(B, G, Hg, nq, C, dh).transpose(3, 0, 1, 2, 4, 5)
    idx_c = idx.reshape(B, G, nq, C, top_n).transpose(2, 0, 1, 3, 4)
    bi = jnp.arange(B)[:, None, None, None]
    gi = jnp.arange(G)[None, :, None, None]

    def sel_chunk(args):
        qi, ii, c = args
        ks = kb[bi, gi, ii]
        vs = vb[bi, gi, ii]
        s = jnp.einsum('bghqd,bgqnld->bghqnl', qi, ks).astype(jnp.float32) * scale
        kpos = ii[..., None] * SEL_BLOCK + jnp.arange(SEL_BLOCK)
        qpos = c * C + jnp.arange(C)
        mask = kpos <= qpos[None, None, :, None, None]
        s = jnp.where(mask[:, :, None], s, NEG_INF).reshape(B, G, Hg, C, top_n * SEL_BLOCK)
        p = jax.nn.softmax(s, axis=-1).reshape(B, G, Hg, C, top_n, SEL_BLOCK)
        return jnp.einsum('bghqnl,bgqnld->bghqd', p.astype(vs.dtype), vs)

    o_sel = lax.map(sel_chunk, (q_c, idx_c, jnp.arange(nq)))
    o_sel = o_sel.transpose(1, 2, 3, 0, 4, 5).reshape(B, G, Hg, S, dh)

    nb = S // Q_BLOCK
    span = WINDOW + Q_BLOCK
    kp = jnp.pad(k_win, ((0, 0), (0, 0), (WINDOW, 0), (0, 0)))
    vp = jnp.pad(v_win, ((0, 0), (0, 0), (WINDOW, 0), (0, 0)))
    q_w = qg.reshape(B, G, Hg, nb, Q_BLOCK, dh).transpose(3, 0, 1, 2, 4, 5)

    def win_block(args):
        qi, i = args
        start = i * Q_BLOCK
        ks = lax.dynamic_slice_in_dim(kp, start, span, axis=2)
        vs = lax.dynamic_slice_in_dim(vp, start, span, axis=2)
        s = jnp.einsum('bghqd,bgkd->bghqk', qi, ks).astype(jnp.float32) * scale
        qpos = start + jnp.arange(Q_BLOCK)
        kpos = start - WINDOW + jnp.arange(span)
        d = qpos[:, None] - kpos[None, :]
        mask = (d >= 0) & (d < WINDOW) & (kpos[None, :] >= 0)
        p = jax.nn.softmax(jnp.where(mask, s, NEG_INF), axis=-1)
        return jnp.einsum('bghqk,bgkd->bghqd', p.astype(vs.dtype), vs)

    o_win = lax.map(win_block, (q_w, jnp.arange(nb)))
    o_win = o_win.transpose(1, 2, 3, 0, 4, 5).reshape(B, G, Hg, S, dh)

    o = gates[..., 0:1] * o_cmp + gates[..., 1:2] * o_sel + gates[..., 2:3] * o_win
    return o.transpose(0, 3, 1, 2, 4).reshape(B, S, H * dh)

def hybrid_mixer(h, w_in, lambda_q1, lambda_k1, lambda_q2, lambda_k2, diff_subln,
                 cmp_pe_k, cmp_k_w1, cmp_k_w2, cmp_pe_v, cmp_v_w1, cmp_v_w2, w_out, lambda_init):
    B, S, _ = h.shape
    dh = HEAD_DIM_2
    cos, sin = rope_tables(S)
    pts = [int(v) for v in np.cumsum(IN_SIZES)[:-1]]
    dq, dk, dv, nq, kc, vc, ks, vs, kw, vw, gl = jnp.split(h @ w_in, pts, axis=-1)

    dq = partial_rope(dq.reshape(B, S, DIFF_HEADS, 2, dh).transpose(0, 2, 3, 1, 4), cos, sin)
    dk = partial_rope(dk.reshape(B, S, DIFF_HEADS, 2, dh).transpose(0, 2, 3, 1, 4), cos, sin)
    dv = dv.reshape(B, S, DIFF_HEADS, DIFF_V_DIM).transpose(0, 2, 1, 3)
    lq1, lk1 = lambda_q1.astype(jnp.float32), lambda_k1.astype(jnp.float32)
    lq2, lk2 = lambda_q2.astype(jnp.float32), lambda_k2.astype(jnp.float32)
    lam = jnp.exp(jnp.sum(lq1 * lk1)) - jnp.exp(jnp.sum(lq2 * lk2)) + lambda_init
    o_diff = diff_attention(dq, dk, dv, lam, diff_subln, lambda_init)

    def kv_heads(a):
        return a.reshape(B, S, NSA_KV_HEADS, dh).transpose(0, 2, 1, 3)
    nq = partial_rope(nq.reshape(B, S, NSA_HEADS, dh).transpose(0, 2, 1, 3), cos, sin)
    gates = jax.nn.sigmoid(gl.reshape(B, S, NSA_HEADS, N_BRANCH)).transpose(0, 2, 1, 3)
    gates = gates.reshape(B, NSA_KV_HEADS, NSA_GROUP, S, N_BRANCH)
    o_nsa = nsa_attention(nq, kv_heads(kc), kv_heads(vc),
                          partial_rope(kv_heads(ks), cos, sin), kv_heads(vs),
                          partial_rope(kv_heads(kw), cos, sin), kv_heads(vw), gates,
                          cmp_pe_k, cmp_k_w1, cmp_k_w2, cmp_pe_v, cmp_v_w1, cmp_v_w2)

    return jnp.concatenate([o_diff, o_nsa], axis=-1) @ w_out

def second_inputs(seed: int = 0) -> dict:
    key = jax.random.key(seed)
    ks = jax.random.split(key, 26)
    f32 = jnp.float32
    L = DEPTH_2

    def w(k, shape, fan_in):
        return jax.random.normal(k, shape, f32) * fan_in ** -0.5

    def gain(k, n):
        return 1.0 + 0.1 * jax.random.normal(k, (L, n), f32)

    return {
        'x': jax.random.normal(ks[0], (BATCH, SEQ, D_MODEL), f32),
        'ff1_norm_pre': gain(ks[1], D_MODEL),
        'ff1_w_gate': w(ks[2], (L, D_MODEL, D_FF), D_MODEL),
        'ff1_w_up': w(ks[3], (L, D_MODEL, D_FF), D_MODEL),
        'ff1_w_down': w(ks[4], (L, D_FF, D_MODEL), D_FF),
        'ff1_norm_post': gain(ks[5], D_MODEL),
        'mix_norm_pre': gain(ks[6], D_MODEL),
        'w_in': w(ks[7], (L, D_MODEL, IN_WIDTH), D_MODEL),
        'lambda_q1': 0.1 * jax.random.normal(ks[8], (L, HEAD_DIM_2), f32),
        'lambda_k1': 0.1 * jax.random.normal(ks[9], (L, HEAD_DIM_2), f32),
        'lambda_q2': 0.1 * jax.random.normal(ks[10], (L, HEAD_DIM_2), f32),
        'lambda_k2': 0.1 * jax.random.normal(ks[11], (L, HEAD_DIM_2), f32),
        'diff_subln': gain(ks[12], DIFF_V_DIM),
        'cmp_pe_k': 0.1 * jax.random.normal(ks[13], (L, CMP_BLOCK, HEAD_DIM_2), f32),
        'cmp_k_w1': w(ks[14], (L, CMP_BLOCK * HEAD_DIM_2, CMP_HIDDEN), CMP_BLOCK * HEAD_DIM_2),
        'cmp_k_w2': w(ks[15], (L, CMP_HIDDEN, HEAD_DIM_2), CMP_HIDDEN),
        'cmp_pe_v': 0.1 * jax.random.normal(ks[16], (L, CMP_BLOCK, HEAD_DIM_2), f32),
        'cmp_v_w1': w(ks[17], (L, CMP_BLOCK * HEAD_DIM_2, CMP_HIDDEN), CMP_BLOCK * HEAD_DIM_2),
        'cmp_v_w2': w(ks[18], (L, CMP_HIDDEN, HEAD_DIM_2), CMP_HIDDEN),
        'w_out': w(ks[19], (L, MIX_WIDTH, D_MODEL), MIX_WIDTH),
        'mix_norm_post': gain(ks[20], D_MODEL),
        'ff2_norm_pre': gain(ks[21], D_MODEL),
        'ff2_w_gate': w(ks[22], (L, D_MODEL, D_FF), D_MODEL),
        'ff2_w_up': w(ks[23], (L, D_MODEL, D_FF), D_MODEL),
        'ff2_w_down': w(ks[24], (L, D_FF, D_MODEL), D_FF),
        'ff2_norm_post': gain(ks[25], D_MODEL),
    }

def second_block(x, ff1_norm_pre, ff1_w_gate, ff1_w_up, ff1_w_down, ff1_norm_post,
              mix_norm_pre, w_in, lambda_q1, lambda_k1, lambda_q2, lambda_k2, diff_subln,
              cmp_pe_k, cmp_k_w1, cmp_k_w2, cmp_pe_v, cmp_v_w1, cmp_v_w2, w_out, mix_norm_post,
              ff2_norm_pre, ff2_w_gate, ff2_w_up, ff2_w_down, ff2_norm_post):
    for l in range(DEPTH_2):
        lambda_init = 0.8 - 0.6 * math.exp(-0.3 * l)
        h = swiglu(rms_norm(x, ff1_norm_pre[l]), ff1_w_gate[l], ff1_w_up[l], ff1_w_down[l])
        x = x + 0.5 * rms_norm(h, ff1_norm_post[l])
        h = hybrid_mixer(rms_norm(x, mix_norm_pre[l]), w_in[l], lambda_q1[l], lambda_k1[l],
                         lambda_q2[l], lambda_k2[l], diff_subln[l], cmp_pe_k[l], cmp_k_w1[l],
                         cmp_k_w2[l], cmp_pe_v[l], cmp_v_w1[l], cmp_v_w2[l], w_out[l], lambda_init)
        x = x + rms_norm(h, mix_norm_post[l])
        h = swiglu(rms_norm(x, ff2_norm_pre[l]), ff2_w_gate[l], ff2_w_up[l], ff2_w_down[l])
        x = x + 0.5 * rms_norm(h, ff2_norm_post[l])
    return x


def setup_inputs(seed=0):
    out = dict(first_inputs(seed))
    for name, value in second_inputs(seed + 1).items():
        if name != "x":
            out[name + "_2"] = value
    return out


def reference(
    x, p, a_pw1_w, a_pw1_b, a_dw_w, a_dw_b, a_ln_g, a_ln_b, a_pw2_w, a_pw2_b, b_wq, kv_wk,
    kv_wv, b_wo, ln_mix_g, ln_mix_b, ffn_w_up, ffn_w_gate, ffn_conv_w, ffn_conv_b, ffn_w_down,
    ple_w_gate, ple_w_proj, ln_ffn_g, ln_ffn_b, ff1_norm_pre_2, ff1_w_gate_2, ff1_w_up_2,
    ff1_w_down_2, ff1_norm_post_2, mix_norm_pre_2, w_in_2, lambda_q1_2, lambda_k1_2,
    lambda_q2_2, lambda_k2_2, diff_subln_2, cmp_pe_k_2, cmp_k_w1_2, cmp_k_w2_2, cmp_pe_v_2,
    cmp_v_w1_2, cmp_v_w2_2, w_out_2, mix_norm_post_2, ff2_norm_pre_2, ff2_w_gate_2, ff2_w_up_2,
    ff2_w_down_2, ff2_norm_post_2,
):
    x = first_block(
        x, p, a_pw1_w, a_pw1_b, a_dw_w, a_dw_b, a_ln_g, a_ln_b, a_pw2_w, a_pw2_b, b_wq, kv_wk,
        kv_wv, b_wo, ln_mix_g, ln_mix_b, ffn_w_up, ffn_w_gate, ffn_conv_w, ffn_conv_b,
        ffn_w_down, ple_w_gate, ple_w_proj, ln_ffn_g, ln_ffn_b,
    )
    return second_block(
        x, ff1_norm_pre_2, ff1_w_gate_2, ff1_w_up_2, ff1_w_down_2, ff1_norm_post_2,
        mix_norm_pre_2, w_in_2, lambda_q1_2, lambda_k1_2, lambda_q2_2, lambda_k2_2,
        diff_subln_2, cmp_pe_k_2, cmp_k_w1_2, cmp_k_w2_2, cmp_pe_v_2, cmp_v_w1_2, cmp_v_w2_2,
        w_out_2, mix_norm_post_2, ff2_norm_pre_2, ff2_w_gate_2, ff2_w_up_2, ff2_w_down_2,
        ff2_norm_post_2,
    )


_drawn_inputs = setup_inputs


def setup_inputs(seed=0):
    import zlib

    import numpy as np

    out = dict(_drawn_inputs(seed))
    spreads = {}
    factors = {'a_pw1_b': 4.302,
     'a_ln_g': 4.801,
     'a_ln_b': 4.452,
     'ffn_conv_b': 6.452,
     'lambda_k2_2': 40.875,
     'cmp_pe_k_2': 25.554,
     'a_pw2_b': 3.458}
    for name, (base, spread) in spreads.items():
        noise = np.random.default_rng([zlib.crc32(name.encode()), seed]).standard_normal(out[name].shape)
        drawn = base * np.exp(spread * noise) if base else spread * noise
        out[name] = jnp.asarray(drawn.astype(out[name].dtype))
    for name, factor in factors.items():
        out[name] = (out[name] * factor).astype(out[name].dtype)
    return out
```

```python
from contextlib import ExitStack

import concourse.bass as bass
from concourse import mybir

F32 = mybir.dt.float32
F32R = mybir.dt.float32r
BF16 = mybir.dt.bfloat16
ACT = mybir.ActivationFunctionType
ALU = mybir.AluOpType
AX_X = mybir.AxisListType.X

P = 128
S = 512
D = 1024
KT = D // P
F = 2816
FT = F // P
CONV_W = 31
FCONV_W = 3
QT = S // P
DH = 64
LN_EPS = 1e-5
RMS_EPS = 1e-6
ALPHA = 4.0 ** 0.25
NEG = -1e30
RAW = 4
CMP_BLOCK = 32
CMP_STRIDE = 16
NC = S // CMP_STRIDE - 1
CMP_HID = 256
NSA_HEADS = 8
DIFF_HEADS = 4

COUNTS = [("pw1", 2 * KT), ("pw2", KT)]
for _l in range(2):
    if _l == 1:
        COUNTS += [("qkv", 3 * KT), ("wo", KT)]
    COUNTS += [(f"pleproj{_l}", 2), (f"plegate{_l}", KT), (f"gateup{_l}", 2 * FT), (f"down{_l}", FT)]
COUNTS += [("gateup2", 2 * FT), ("down2", FT), ("hybrid", 7 + 3 * DIFF_HEADS + 4), ("wout", KT), ("gateup3", 2 * FT),
           ("down3", FT)]
CHUNK = {}
NCHUNKS = 0
for _n, _k in COUNTS:
    CHUNK[_n] = NCHUNKS
    NCHUNKS += _k

PARAMS = [("pw1_ba", KT), ("pw1_bg", KT), ("dw_w", KT * CONV_W), ("dw_b", KT), ("aln_g", KT), ("aln_b", KT),
          ("pw2_b", KT), ("mix_g0", KT), ("mix_b0", KT), ("mix_g1", KT), ("mix_b1", KT),
          ("fcw0", FT * FCONV_W), ("fcb0", FT), ("fcw1", FT * FCONV_W), ("fcb1", FT),
          ("ffn_g0", KT), ("ffn_b0", KT), ("ffn_g1", KT), ("ffn_b1", KT),
          ("ff1_pre", KT), ("ff1_post", KT), ("mix_pre", KT), ("mix_post", KT), ("ff2_pre", KT), ("ff2_post", KT),
          ("subln", 1), ("pe_k", CMP_BLOCK), ("pe_v", CMP_BLOCK), ("w2_k", 2 * DH), ("w2_v", 2 * DH),
          ("lams", 4 * DH)]
PCOL = {}
NPAR = 0
for _n, _k in PARAMS:
    PCOL[_n] = NPAR
    NPAR += _k

CONSTS = [("ident", P), ("mean", P), ("negtri", P), ("negone", P), ("perm", P), ("maskS", P), ("maskC", P),
          ("eps", 2), ("cadd", QT * NC), ("cmul", QT * NC)]
CCOL = {}
NCON = 0
for _n, _k in CONSTS:
    CCOL[_n] = NCON
    NCON += _k

TILE_W = [512, 384, 256, 128]
TILE_BANK = [0, 1, 2, 1]
TILE_COL = [0, 0, 0, 384]
TILE_OFF = [0, 512, 1024, 896]
SCORE_COLS = 1280
BANKS3 = [(0, 0, 512), (1, 512, 512), (2, 1024, 256)]

ITEMS = [("copy", "kc", 0), ("copy", "vc", 0), ("rope", "ks", 0), ("turn", "vs", 0), ("rope", "kw", 0),
         ("turn", "vw", 0), ("gate", "gates", 0)]
for _h in range(DIFF_HEADS):
    ITEMS += [("rope", "dq", _h), ("rope", "dk", _h), ("turn", "dv", _h)]
ITEMS += [("rope", "nq", _j) for _j in range(4)]
USE = {}


def _use(*key):
    USE[key] = len(USE)


def _use_item(i):
    _use("item", i)
    if ITEMS[i][0] != "copy":
        _use("second", i)


for _i in range(7):
    _use_item(_i)
_use("compressed")
for _i in range(7, 10):
    _use_item(_i)
for _h in range(DIFF_HEADS):
    for _i in (range(10 + 3 * _h, 13 + 3 * _h) if _h < 3 else [19]):
        _use_item(_i)
for _j in range(4):
    _use("cmp_scores", _j)
    if _j < 3:
        _use_item(20 + _j)
    _use("cmp_turn", _j, 0)
    _use("cmp_turn", _j, 1)
ROPES = [i for i, it in enumerate(ITEMS) if it[0] == "rope"]
SECONDS = [k for k in USE if k[0] not in ("item",)]
LAMBDA_INIT = 0.2


def build_block(nc, ws, xT, pT, params, consts, rope, w1, out, stop=None):
    with ExitStack() as ctx:
        def sb(name, shape, dt=F32):
            return ctx.enter_context(nc.sbuf_tensor(name, shape, dt))

        def sem(name):
            return ctx.enter_context(nc.semaphore(name))

        raw = sb("raw", [P, RAW, 1024])
        wH = sb("wH", [P, 2, 1024], F32R)
        wL = sb("wL", [P, 2, 1024], F32R)
        xf = sb("xf", [P, KT, S])
        xH = sb("xH", [P, KT, S], F32R)
        xL = sb("xL", [P, KT, S], F32R)
        tmp = sb("tmp", [P, 10, S])
        rstd = sb("rstd", [P, S])
        par = sb("par", [P, NPAR])
        con = sb("con", [P, NCON])
        bcon = sb("bcon", [P, 3 * P], BF16)
        one = sb("one", [P, 1])
        vturn0 = sb("vturn0", [P, S])
        st = sb("st", [P, 160])
        sq = [tmp[:, 8, :], tmp[:, 9, :]]

        def overlay(specs):
            with ExitStack() as sub:
                return [sub.enter_context(nc.sbuf_tensor(n, s, d)) for n, s, d in specs]

        hH, hL = overlay([("hH", [P, FT, S], F32R), ("hL", [P, FT, S], F32R)])
        cH, cL, gpad = overlay([("cH", [P, KT, S], F32R), ("cL", [P, KT, S], F32R),
                                ("gpad", [P, 2, CONV_W - 1 + S], F32)])
        (mH, mL, qT, kT, vT, vN, lg, sp, aT) = overlay([
            ("mH", [P, KT, S], F32R), ("mL", [P, KT, S], F32R), ("qT", [P, 2, S], F32), ("kT", [P, 2, S], F32),
            ("vT", [P, S], F32), ("vN", [P, 2, QT, P], F32),
            ("lg", [P, 2, SCORE_COLS], F32), ("sp", [P, 2, SCORE_COLS], F32), ("aT", [P, 2, SCORE_COLS], F32)])
        _, pf, pH, pL = overlay([("pgap", [P, 18944], F32), ("pf", [P, 2, S], F32), ("pH", [P, 2, S], F32R),
                                 ("pL", [P, 2, S], F32R)])

        common = [("ropeT", [P, 2, S], F32), ("ksT", [P, S], F32), ("kwT", [P, S], F32), ("vsN", [P, QT, P], F32),
                  ("vwN", [P, QT, P], F32), ("gN", [P, QT, 24], F32), ("kcC", [P, 32], F32), ("vcC", [P, P], F32)]
        (ropeT, ksT, kwT, vsN, vwN, gN, kcC, vcC, w1b, kcvc, blk_v, hid) = overlay(common + [
            ("w1b", [P, 2, CMP_BLOCK * CMP_HID], F32), ("kcvc", [P, 2, S], F32), ("blk_v", [P, NC, CMP_BLOCK], F32),
            ("hid", [P, 8, 32], F32)])
        (dqT, dkT, dvN, AT, pcT, pc_n, oN, nqT) = overlay(
            [(n + "_", s, d) for n, s, d in common] + [
                ("dqT", [P, 2, S], F32), ("dkT", [P, 2, S], F32), ("dvN", [P, 2, QT, P], F32), ("AT", [P, 2, SCORE_COLS], F32), ("pcT", [P, QT, P], F32), ("pc_n", [P, 2, QT, NC], F32),
                ("oN", [P, QT, D], F32), ("nqT", [P, 2, S], F32)])[8:]
        flat = tmp[:].rearrange("p a b -> p (a b)")
        prob = flat[:, 0:2 * SCORE_COLS].rearrange("p (m c) -> p m c", m=2)
        pre = flat[:, 2560:3584].rearrange("p (a b) -> p a b", a=2)
        rot = flat[:, 3584:4096]
        blk_k = flat[:, 4096:4096 + NC * CMP_BLOCK].rearrange("p (c s) -> p c s", c=NC)

        ps = [ctx.enter_context(nc.psum_tensor(f"ps{i}", [P, 512], F32)) for i in range(8)]

        def pc(name, n=0, w=1):
            return par[:, bass.ds(PCOL[name] + n, w)]

        def cc(name, w=P):
            return con[:, CCOL[name]:CCOL[name] + w]

        identB, maskSB, maskCB = bcon[:, 0:P], bcon[:, P:2 * P], bcon[:, 2 * P:3 * P]

        in_loaded = sem("in_loaded")
        raw_loaded = [sem(f"raw_loaded{j}") for j in range(RAW)]
        high_ready = sem("high_ready")
        low_ready = sem("low_ready")
        chunk_done = sem("chunk_done")
        bank_done = sem("bank_done")
        one_ready = sem("one_ready")
        const_ready = sem("const_ready")
        x_high = sem("x_high")
        x_ready = sem("x_ready")
        src_ready = sem("src_ready")
        mean_ready = sem("mean_ready")
        centered = sem("centered")
        squared = sem("squared")
        sumsq = sem("sumsq")
        std_ready = sem("std_ready")
        rstd_ready = sem("rstd_ready")
        normed = sem("normed")
        affine = sem("affine")
        glu_sig = sem("glu_sig")
        glu_pad = sem("glu_pad")
        glu_banks_free = sem("glu_banks_free")
        taps = sem("taps")
        c_act = sem("c_act")
        c_ready = sem("c_ready")
        res_scaled = sem("res_scaled")
        p_loaded = sem("p_loaded")
        p_high = sem("p_high")
        p_ready = sem("p_ready")
        proj_copied = sem("proj_copied")
        ple_sig = sem("ple_sig")
        ple_mul = sem("ple_mul")
        ple_free = sem("ple_free")
        tap2 = sem("tap2")
        tap10 = sem("tap10")
        gate_act = sem("gate_act")
        h_made = sem("h_made")
        h_high = sem("h_high")
        h_ready = sem("h_ready")
        q_free = sem("q_free")
        qkv_copied = sem("qkv_copied")
        z_ready = sem("z_ready")
        abs_ready = sem("abs_ready")
        e_ready = sem("e_ready")
        ln_ready = sem("ln_ready")
        sp_ready = sem("sp_ready")
        cum_ready = sem("cum_ready")
        a_ready = sem("a_ready")
        av_ready = sem("av_ready")
        vt_ready = sem("vt_ready")
        m_high = sem("m_high")
        m_ready = sem("m_ready")
        updated = sem("updated")
        w1_loaded = sem("w1_loaded")
        rope_loaded = sem("rope_loaded")
        b7_read = sem("b7_read")
        second_done = sem("second_done")
        roped = sem("roped")
        rot_ready = sem("rot_ready")
        blocks_ready = sem("blocks_ready")
        hid_psum = sem("hid_psum")
        hid_ready = sem("hid_ready")
        lam_steps = sem("lam_steps")
        s_ready = sem("s_ready")
        max_ready = sem("max_ready")
        p_exp = sem("p_exp")
        coef_ready = sem("coef_ready")
        scaled = sem("scaled")
        p_ready2 = sem("p_ready2")
        turned = sem("turned")
        at_ready = sem("at_ready")
        at2_ready = sem("at2_ready")
        o_ready = sem("o_ready")
        o_copied = sem("o_copied")
        cmp_steps = sem("cmp_steps")
        cmp_sum = sem("cmp_sum")
        cmp_exp = sem("cmp_exp")
        cmp_ready = sem("cmp_ready")
        head_sq = sem("head_sq")
        head_std = sem("head_std")
        head_done = sem("head_done")
        o_turned = sem("o_turned")
        out_done = sem("out_done")

        block = ctx.enter_context(nc.Block())

        def fp(ap):
            return ap.bitcast(F32)

        @block.sync
        def _(sp_e):
            sp_e.dma_start(par[:], params).then_inc(in_loaded, 16)
            sp_e.dma_start(con[:], consts).then_inc(in_loaded, 16)
            sp_e.dma_start(xf[:], xT.rearrange("(k p) t -> p k t", p=P)).then_inc(in_loaded, 16)
            for c in range(RAW):
                sp_e.dma_start(raw[:, c, :], ws[c]).then_inc(raw_loaded[c], 16)

            def load(t, j):
                c = t * RAW + j
                sp_e.wait_ge(low_ready, c - RAW + 1)
                sp_e.dma_start(raw[:, j, :], ws[bass.ds(c, 1)].rearrange("o p n -> (o p) n"))\
                    .then_inc(raw_loaded[j], 16)

            with sp_e.Fori(1, NCHUNKS // RAW) as t:
                for j in range(RAW):
                    load(t, j)
            for j in range(NCHUNKS % RAW):
                load(NCHUNKS // RAW, j)

        @block.gpsimd
        def _(pool):
            pool.memset(one[:], 1.0).then_inc(one_ready, 1)
            pool.wait_ge(one_ready, 1)

            def split(t, j, slot_used=True):
                c = t * RAW + j
                pool.wait_ge(raw_loaded[j], 16 * t + 16)
                if slot_used:
                    pool.wait_ge(chunk_done, c - 1)
                pool.tensor_tensor(wH[:, j % 2, :], raw[:, j, :], one[:, 0:1].broadcast_to([P, 1024]),
                                   ALU.mult).then_inc(high_ready, 1)
                pool.wait_ge(high_ready, c + 1)
                pool.tensor_tensor(wL[:, j % 2, :], raw[:, j, :], fp(wH[:, j % 2, :]),
                                   ALU.subtract).then_inc(low_ready, 1)

            for j in range(RAW):
                split(0, j, slot_used=j >= 2)
            with pool.Fori(1, NCHUNKS // RAW) as t:
                for j in range(RAW):
                    split(t, j)
            for j in range(NCHUNKS % RAW):
                split(NCHUNKS // RAW, j)

        NORM = {n: i for i, n in enumerate(["conf", "mix0", "ffn0", "mix1", "ffn1", "ff1_pre", "ff1_post",
                                            "mix_pre", "mix_post", "ff2_pre", "ff2_post"])}
        LNORM = ["conf", "mix0", "ffn0", "mix1", "ffn1"]
        FULL = {n: i for i, n in enumerate(["pw2", "pleproj0", "down0", "wo", "pleproj1", "down1", "down2",
                                            "wout", "down3"])}
        XV = {n: i for i, n in enumerate(["in", "mix0", "ffn0", "mix1", "ff1_pre", "mix_pre", "mixer",
                                          "ff2_pre"])}
        XH = {n: i for i, n in enumerate(["in", "ff1_pre", "mix_pre", "mixer", "ff2_pre"])}
        NUNITS = DIFF_HEADS + NSA_HEADS
        SRC = {n: i for i, n in enumerate(["conf", "mix0", "ffn0", "mix1", "ffn1", "ff1_post", "mix_post",
                                           "ff2_post"])}

        @block.tensor
        def _(pe):
            def three(bank, w, rh, rl, start, stop, c=None):
                slot, cols = w
                pe.matmul(bank, wH[:, slot, cols], rh, start=start, stop=False)
                pe.matmul(bank, wH[:, slot, cols], rl, start=False, stop=False)
                return pe.matmul(bank, wL[:, slot, cols], rh, start=False, stop=stop)

            def tile_product(bank, c, slot, rH=xH, rL=xL):
                pe.wait_ge(low_ready, c + 1)
                for k in range(KT):
                    mm = three(bank, (slot, slice(k * P, k * P + P)), rH[:, k, :], rL[:, k, :],
                               k == 0, k == KT - 1)
                mm.then_inc(chunk_done, 1)

            def full_product(name, nk, rH, rL, ready, ready_base, banks_free):
                c0 = CHUNK[name]

                def one_k(k, j, first=False, last=False):
                    pe.wait_ge(low_ready, c0 + k + 1)
                    pe.wait_ge(ready, ready_base + k + 1)
                    slot = (c0 + j) % 2
                    rh = rH[:, bass.ds(k, 1), :].rearrange("p o t -> p (o t)")
                    rl = rL[:, bass.ds(k, 1), :].rearrange("p o t -> p (o t)")
                    for n in range(8):
                        if first:
                            banks_free(n)
                        mm = three(ps[n][:], (slot, slice(n * P, n * P + P)), rh, rl, first, last)
                        if last and n < 7:
                            mm.then_inc(bank_done, 1)
                    mm.then_inc(chunk_done, 1)

                one_k(0, 0, first=True, last=nk == 1)
                if nk > 2:
                    one_k(1, 1)
                    if nk > 4:
                        with pe.Fori(1, nk // 2 - 1) as t:
                            for j in range(2):
                                one_k(t * 2 + j, j)
                    one_k(nk - 2, 0)
                one_k(nk - 1, 1, last=True)

            def mean_product(name, src):
                i = SRC[name]
                for n in range(KT):
                    pe.wait_ge(src_ready, 8 * i + n + 1)
                    mm = pe.matmul(ps[0][:], cc("mean"), src[:, n, :], start=n == 0, stop=n == KT - 1)
                mm.then_inc(mean_ready, 1)

            def sumsq_product(name, bank):
                i = NORM[name]
                if name.endswith("post"):
                    pe.wait_ge(src_ready, 8 * SRC[name] + 2)
                for n in range(KT):
                    pe.wait_ge(squared, 8 * i + n + 1)
                    pe.matmul(ps[bank][:], cc("mean"), sq[n % 2], start=n == 0, stop=n == KT - 1)\
                        .then_inc(sumsq, 1)

            def x_wait(name):
                pe.wait_ge(x_ready, 8 * XV[name] + 8)

            def ffn(inst, xname):
                c0 = CHUNK[f"gateup{inst}"]
                x_wait(xname)
                with pe.Fori(0, FT // 2) as t:
                    for j in range(2):
                        c = t * 4 + (c0 + 2 * j)
                        pe.wait_ge(h_made, t * 2 + (24 * inst + j + 1))
                        tile_product(ps[2 * j][:], c, c0 % 2)
                        tile_product(ps[2 * j + 1][:], c + 1, (c0 + 1) % 2)

                def banks_free(n):
                    if n == 0:
                        pe.wait_ge(h_made, 24 * inst + 24)
                full_product(f"down{inst}", FT, hH, hL, h_ready, FT * inst, banks_free)

            def ple(layer, xname):
                pe.wait_ge(p_ready, layer + 1)
                x_wait(xname)
                full_product(f"pleproj{layer}", 2, pH, pL, p_ready, layer - 1, lambda n: None)
                c0 = CHUNK[f"plegate{layer}"]
                pe.wait_ge(proj_copied, KT * (layer + 1))
                with pe.Fori(0, KT // 2) as t:
                    for j in range(2):
                        pe.wait_ge(ple_free, t * 2 + (10 * layer + j + 1))
                        tile_product(ps[j][:], t * 2 + (c0 + j), (c0 + j) % 2)

            x_wait("in")
            with pe.Fori(0, KT // 2) as t:
                for j in range(2):
                    pe.wait_ge(glu_banks_free, t * 2 + (j + 1))
                    tile_product(ps[2 * j][:], t * 4 + 2 * j, 0)
                    tile_product(ps[2 * j + 1][:], t * 4 + (2 * j + 1), 1)
            pe.wait_ge(glu_banks_free, 10)
            mean_product("conf", tmp)
            sumsq_product("conf", 1)
            full_product("pw2", KT, cH, cL, c_ready, 0, lambda n: None)
            mean_product("mix0", xf)
            sumsq_product("mix0", 1)
            ple(0, "mix0")
            pe.wait_ge(ple_free, 10)
            ffn(0, "mix0")
            mean_product("ffn0", xf)
            sumsq_product("ffn0", 1)

            c0 = CHUNK["qkv"]

            def project(p, j, which):
                pe.wait_ge(q_free, p * 4 + (which + 1))
                tile_product(ps[7][:], p * 3 + (c0 + which), (c0 + 3 * j + which) % 2)

            def turn_values(p, j):
                pe.wait_ge(qkv_copied, p * 4 + 3)
                for kt in range(QT):
                    mm = pe.transpose(ps[7][:, kt * P:kt * P + P], vT[:, kt * P:kt * P + P], cc("ident"))
                mm.then_inc(vt_ready, 1)

            def scores(p, j, h):
                pe.wait_ge(qkv_copied, p * 4 + 2)
                r = slice(DH * h, DH * h + DH)
                for kt in range(QT):
                    b = ps[3 * h + TILE_BANK[kt]]
                    o = TILE_COL[kt]
                    pe.matmul(b[:, o:o + TILE_W[kt]], kT[r, j, kt * P:kt * P + P], qT[r, j, kt * P:S],
                              start=kt != 3, stop=False, skip_group_check=True)
                    mm = pe.matmul(b[:, o:o + P], identB, maskSB, start=False, stop=False, skip_group_check=True)
                mm.then_inc(z_ready, 1)

            def cumulate(p, h):
                pe.wait_ge(sp_ready, p * 6 + (3 * h + 3))
                for kt in range(QT):
                    b = ps[3 * h + TILE_BANK[kt]]
                    o = TILE_COL[kt]
                    for k2 in range(kt, QT):
                        m = pe.matmul(b[:, o + (k2 - kt) * P:o + TILE_W[kt]], cc("negtri" if k2 == kt else "negone"),
                                      sp[:, h, TILE_OFF[k2]:TILE_OFF[k2] + TILE_W[k2]],
                                      start=False, stop=False, skip_group_check=True)
                m.then_inc(cum_ready, 1)

            def values(p, j, h):
                pe.wait_ge(a_ready, p * 6 + (3 * h + 3))
                r = slice(DH * h, DH * h + DH)
                for kt in range(QT):
                    m = pe.matmul(ps[6][r, kt * P:S], vN[:, j, kt, r], aT[:, h, TILE_OFF[kt]:TILE_OFF[kt] + TILE_W[kt]],
                                  start=kt == 0, stop=kt == QT - 1, skip_group_check=True)
                m.then_inc(av_ready, 1)

            def pair(p, j, more, first=False):
                if not first:
                    pe.wait_ge(a_ready, p * 6)
                scores(p, j, 0)
                scores(p, j, 1)
                if more:
                    project(p + 1, 1 - j, 0)
                cumulate(p, 0)
                if more:
                    project(p + 1, 1 - j, 1)
                cumulate(p, 1)
                if more:
                    project(p + 1, 1 - j, 2)
                if not first:
                    pe.wait_ge(m_ready, p)
                pe.wait_ge(qkv_copied, p * 4 + 4)
                values(p, j, 0)
                values(p, j, 1)
                if more:
                    turn_values(p + 1, 1 - j)

            x_wait("ffn0")
            for which in range(3):
                project(0, 0, which)
            turn_values(0, 0)
            pair(0, 0, True, first=True)
            pair(1, 1, True)
            with pe.Fori(1, KT // 2 - 1) as t:
                pair(t * 2, 0, True)
                pair(t * 2 + 1, 1, True)
            pair(KT - 2, 0, True)
            pair(KT - 1, 1, False)
            pe.wait_ge(a_ready, 6 * KT)
            pe.wait_ge(qkv_copied, 4 * KT)

            def wo_free(n):
                if n == 6:
                    pe.wait_ge(m_ready, KT)
            full_product("wo", KT, mH, mL, m_ready, 0, wo_free)
            mean_product("mix1", xf)
            sumsq_product("mix1", 1)
            ple(1, "mix1")
            pe.wait_ge(ple_free, 20)
            ffn(1, "mix1")
            mean_product("ffn1", xf)
            sumsq_product("ffn1", 1)

            sumsq_product("ff1_pre", 2)
            ffn(2, "ff1_pre")
            sumsq_product("ff1_post", 1)
            sumsq_product("mix_pre", 2)

            c0 = CHUNK["hybrid"]
            q_of = {"dq": dqT, "nq": nqT}

            def item(i):
                kind, name, h = ITEMS[i]
                if USE["item", i]:
                    pe.wait_ge(b7_read, USE["item", i])
                tile_product(ps[7][:], c0 + i, (c0 + i) % 2)
                if kind == "copy":
                    return
                pe.wait_ge(b7_read, USE["second", i])
                if kind == "rope":
                    mm = pe.matmul(ps[7][:], cc("perm"), pre[:, ROPES.index(i) % 2, :], start=True, stop=True)
                else:
                    for t in range(QT):
                        mm = pe.transpose(ps[7][:, t * P:t * P + P], vturn0[:, t * P:t * P + P], cc("ident"))
                mm.then_inc(second_done, 1)

            x_wait("mix_pre")
            for i in range(7):
                item(i)

            pe.wait_ge(blocks_ready, 4)
            pe.wait_ge(w1_loaded, 32)
            for kv, blk in ((0, blk_k), (1, blk_v)):
                for m in range(2):
                    for g in range(2):
                        r = slice(DH * g, DH * g + DH)
                        col = (2 * kv + m) * 32
                        for pos in range(CMP_BLOCK):
                            w = w1b[r, kv, pos * CMP_HID + m * P:pos * CMP_HID + m * P + P]
                            mm = pe.matmul(ps[3 + g][:, col:col + NC], w, blk[r, :, pos], start=pos == 0,
                                           stop=pos == CMP_BLOCK - 1, skip_group_check=True)
            mm.then_inc(hid_psum, 1)
            pe.wait_ge(hid_ready, 2)
            pe.wait_ge(b7_read, USE[("compressed",)])
            for g in range(2):
                for m in range(2):
                    pe.matmul(ps[7][DH * g:DH * g + DH, 0:NC], pc("w2_k", DH * m, DH), hid[:, 4 * g + m, 0:NC],
                              start=m == 0, stop=m == 1, skip_group_check=True)
            for g in range(2):
                for m in range(2):
                    mm = pe.matmul(ps[5][0:NC, DH * g:DH * g + DH], hid[:, 4 * g + 2 + m, 0:NC],
                                   pc("w2_v", DH * m, DH), start=m == 0, stop=m == 1, skip_group_check=True)
            mm.then_inc(second_done, 1)

            def scores2(m, q, k, r):
                for t in range(QT):
                    qt = QT - 1 - t
                    b = ps[3 * (m % 2) + TILE_BANK[t]]
                    o = TILE_COL[t]
                    pe.matmul(b[:, o:o + TILE_W[t]], q[r, qt * P:qt * P + P], k[r, 0:TILE_W[t]],
                              start=t != 3, stop=False, skip_group_check=True)
                    mm = pe.matmul(b[:, o + qt * P:o + qt * P + P], identB, maskCB, start=False, stop=False,
                                   skip_group_check=True)
                mm.then_inc(s_ready, 1)

            def turn_map(m, src):
                for kt in range(QT):
                    b = ps[3 * (m % 2) + TILE_BANK[kt]]
                    for qt in range(kt, QT):
                        o = TILE_COL[kt] + (qt - kt) * P
                        f = TILE_OFF[QT - 1 - qt] + kt * P
                        mm = pe.transpose(b[:, o:o + P], prob[:, src, f:f + P], cc("ident"))
                mm.then_inc(turned, 1)

            def weigh(m, v, w, first):
                for qt in range(QT):
                    for kt in range(qt + 1):
                        f = TILE_OFF[kt] + (qt - kt) * P
                        mm = pe.matmul(ps[6][:, qt * w:qt * w + w], AT[:, m % 2, f:f + P], v[:, kt, :],
                                       start=first and qt == 0 and kt == 0, stop=False, skip_group_check=True)
                return mm

            for i in range(7, 10):
                item(i)
            for h in range(DIFF_HEADS):
                j = h % 2
                pe.wait_ge(b7_read, USE["second", 9 + 3 * h] + 1)
                pe.wait_ge(roped, 2 + 2 * h + 2)
                if h:
                    pe.wait_ge(at_ready, 3 * h)
                    pe.wait_ge(p_exp, 8 * h)
                scores2(2 * h, dqT[:, j, :], dkT[:, j, :], slice(0, DH))
                scores2(2 * h + 1, dqT[:, j, :], dkT[:, j, :], slice(DH, P))
                nxt = list(range(10 + 3 * h, 13 + 3 * h)) if h < 3 else [19]
                for i in nxt[:2]:
                    item(i)
                pe.wait_ge(p_ready2, QT * (h + 1))
                turn_map(0, 0)
                for i in nxt[2:]:
                    item(i)
                pe.wait_ge(at_ready, 3 * (h + 1))
                if h:
                    pe.wait_ge(o_copied, h)
                weigh(0, dvN[:, j, :, :], P, True).then_inc(o_ready, 1)

            for j in range(4):
                pe.wait_ge(roped, 10 + j + 1)
                pe.wait_ge(b7_read, USE["cmp_scores", j])
                pe.wait_ge(o_copied, DIFF_HEADS + 2 * j)
                for g in range(2):
                    for qt in range(QT):
                        r = slice(DH * g, DH * g + DH)
                        mm = pe.matmul(ps[7 - g][:, qt * NC:qt * NC + NC], nqT[r, j % 2, qt * P:qt * P + P],
                                       kcC[r, 0:NC], start=qt == 0, stop=False, skip_group_check=True)
                mm.then_inc(second_done, 1)
                for g in range(2):
                    u = DIFF_HEADS + 2 * j + g
                    r = slice(DH * g, DH * g + DH)
                    pe.wait_ge(at_ready, 3 * u)
                    if u > DIFF_HEADS:
                        pe.wait_ge(at2_ready, 3 * (u - DIFF_HEADS))
                    pe.wait_ge(p_exp, 8 * u)
                    scores2(0, nqT[:, j % 2, :], ksT, r)
                    scores2(1, nqT[:, j % 2, :], kwT, r)
                    if g == 0 and j < 3:
                        item(20 + j)
                    pe.wait_ge(cmp_ready, j + 1)
                    pe.wait_ge(b7_read, USE["cmp_turn", j, g])
                    for qt in range(QT):
                        mm = pe.transpose(ps[7][0:NC, qt * P:qt * P + P], pc_n[:, g, qt, :], cc("ident"))
                    mm.then_inc(second_done, 1)
                    n0 = QT * DIFF_HEADS + 8 * (u - DIFF_HEADS)
                    pe.wait_ge(p_ready2, n0 + QT)
                    turn_map(0, 0)
                    pe.wait_ge(p_ready2, n0 + 2 * QT)
                    turn_map(1, 1)
                    pe.wait_ge(o_copied, u)
                    pe.wait_ge(b7_read, USE["cmp_turn", j, g] + 1)
                    for qt in range(QT):
                        pe.matmul(ps[6][:, qt * DH:qt * DH + DH], pcT[0:NC, qt, :], vcC[0:NC, r],
                                  start=qt == 0, stop=False, skip_group_check=True)
                    pe.wait_ge(at_ready, 3 * u + 3)
                    weigh(0, vsN[:, :, r], DH, False)
                    pe.wait_ge(at2_ready, 3 * (u - DIFF_HEADS) + 3)
                    weigh(1, vwN[:, :, r], DH, False).then_inc(o_ready, 1)

            pe.wait_ge(o_copied, NUNITS)
            pe.wait_ge(head_done, QT * DIFF_HEADS)
            for n in range(KT):
                for qt in range(QT):
                    mm = pe.transpose(ps[n][:, qt * P:qt * P + P], oN[:, qt, n * P:n * P + P], cc("ident"))
                mm.then_inc(o_turned, 1)
            full_product("wout", KT, xH, xL, x_ready, 8 * XV["mixer"],
                         lambda n: pe.wait_ge(x_ready, 8 * XV["mixer"] + n + 1))
            sumsq_product("mix_post", 1)
            sumsq_product("ff2_pre", 2)
            ffn(3, "ff2_pre")
            sumsq_product("ff2_post", 1)

        @block.scalar
        def _(act):
            def load_p(layer):
                act.dma_start(pf[:], pT[layer].rearrange("(k p) t -> p k t", p=P)).then_inc(p_loaded, 16)

            load_p(0)
            act.wait_ge(in_loaded, 48)
            act.activation(identB, cc("ident"), ACT.Copy).then_inc(const_ready, 1)
            act.activation(maskSB, cc("maskS"), ACT.Copy).then_inc(const_ready, 1)
            act.activation(maskCB, cc("maskC"), ACT.Copy).then_inc(const_ready, 1)
            for n, f in (("ff1_post", 0.5), ("ff2_post", 0.5), ("subln", 1.0 - LAMBDA_INIT)):
                w = dict(PARAMS)[n]
                act.activation(pc(n, 0, w), pc(n, 0, w), ACT.Copy, scale=f).then_inc(const_ready, 1)
            for n in range(KT):
                act.activation(xH[:, n, :], xf[:, n, :], ACT.Copy).then_inc(x_high, 1)

            def squares(name, src, ready, base, step=1):
                i = NORM[name]
                for n in range(KT):
                    act.wait_ge(ready, base + step * (n + 1))
                    if 8 * i + n - 1 > 0:
                        act.wait_ge(sumsq, 8 * i + n - 1)
                    act.activation(sq[n % 2], src[:, n, :], ACT.Square).then_inc(squared, 1)

            def std(name, bank, eps):
                i = NORM[name]
                act.wait_ge(sumsq, 8 * i + 8)
                if i:
                    act.wait_ge(rstd_ready, i)
                act.activation(rstd[:], ps[bank][:], ACT.Sqrt, bias=cc("eps", 2)[:, eps:eps + 1])\
                    .then_inc(std_ready, 1)

            def layer_norm(name, src, g, b):
                li = LNORM.index(name)
                squares(name, src, centered, 8 * li)
                std(name, 1, 0)
                for n in range(KT):
                    act.wait_ge(normed, 8 * NORM[name] + n + 1)
                    if name == "conf":
                        act.activation(src[:, n, :], src[:, n, :], ACT.Silu, scale=pc(g, n), bias=pc(b, n))\
                            .then_inc(affine, 1)
                        act.wait_ge(affine, 2 * n + 1)
                        act.activation(cH[:, n, :], src[:, n, :], ACT.Copy).then_inc(affine, 1)
                    elif name == "ffn1":
                        act.activation(src[:, n, :], src[:, n, :], ACT.Identity, scale=pc(g, n), bias=pc(b, n))\
                            .then_inc(affine, 2)
                    else:
                        act.activation(xH[:, n, :], src[:, n, :], ACT.Identity, scale=pc(g, n), bias=pc(b, n))\
                            .then_inc(affine, 1)
                        act.wait_ge(affine, 16 * li + 2 * n + 1)
                        act.activation(src[:, n, :], src[:, n, :], ACT.Identity, scale=pc(g, n), bias=pc(b, n))\
                            .then_inc(affine, 1)

            def ple(layer):
                act.wait_ge(p_loaded, 16 * layer + 16)
                for k in range(2):
                    act.activation(pH[:, k, :], pf[:, k, :], ACT.Copy).then_inc(p_high, 1)
                for n in range(KT):
                    if n < 7:
                        act.wait_ge(bank_done, 7 * FULL[f"pleproj{layer}"] + n + 1)
                    else:
                        act.wait_ge(chunk_done, CHUNK[f"pleproj{layer}"] + 2)
                    act.activation(tmp[:, n, :], ps[n][:], ACT.Copy).then_inc(proj_copied, 1)
                c0 = CHUNK[f"plegate{layer}"]
                with act.Fori(0, KT // 2) as t:
                    for j in range(2):
                        act.wait_ge(chunk_done, t * 2 + (c0 + j + 1))
                        act.wait_ge(ple_free, t * 2 + (10 * layer + j + 1))
                        act.activation(sq[j], ps[j][:], ACT.Sigmoid).then_inc(ple_sig, 1)

            def ffn(inst):
                c0 = CHUNK[f"gateup{inst}"]
                with act.Fori(0, FT // 2) as t:
                    for j in range(2):
                        f = t * 2 + j
                        act.wait_ge(chunk_done, t * 4 + (c0 + 2 * j + 1))
                        act.wait_ge(h_made, t * 2 + (24 * inst + j + 1))
                        if inst < 2:
                            act.activation(tmp[:, j, :], ps[2 * j][:], ACT.Identity,
                                           scale=pc(f"fcw{inst}", f * FCONV_W + 2), bias=pc(f"fcb{inst}", f))\
                                .then_inc(tap2, 1)
                            act.wait_ge(tap10, t * 4 + (2 * FT * inst + 2 * j + 2))
                            act.activation(tmp[:, j, :], tmp[:, j, :], ACT.Silu).then_inc(gate_act, 1)
                        else:
                            act.activation(tmp[:, j, :], ps[2 * j][:], ACT.Silu).then_inc(gate_act, 1)
                        act.wait_ge(h_made, t * 2 + (24 * inst + 2 + j + 1))
                        act.activation(hH[:, bass.ds(f, 1), :].rearrange("p o t -> p (o t)"), tmp[:, 2 + j, :],
                                       ACT.Copy).then_inc(h_high, 1)

            with act.Fori(0, KT // 2) as t:
                for j in range(2):
                    act.wait_ge(chunk_done, t * 4 + (2 * j + 1))
                    act.wait_ge(glu_banks_free, t * 2 + (j + 1))
                    act.activation(sq[j], ps[2 * j][:], ACT.Sigmoid, bias=pc("pw1_bg", t * 2 + j)).then_inc(glu_sig, 1)
            layer_norm("conf", tmp, "aln_g", "aln_b")
            layer_norm("mix0", xf, "mix_g0", "mix_b0")
            ple(0)
            ffn(0)
            layer_norm("ffn0", xf, "ffn_g0", "ffn_b0")

            def copy_qkv(p, j, which):
                act.wait_ge(chunk_done, p * 3 + (CHUNK["qkv"] + which + 1))
                if which == 0:
                    act.activation(qT[:, j, :], ps[7][:], ACT.Copy, scale=DH ** -0.5).then_inc(qkv_copied, 1)
                elif which == 1:
                    act.activation(kT[:, j, :], ps[7][:], ACT.Copy).then_inc(qkv_copied, 1)
                else:
                    act.activation(vT[:], ps[7][:], ACT.Copy).then_inc(qkv_copied, 1)
                act.wait_ge(qkv_copied, p * 4 + (which + 1))
                act.sem_inc(q_free, 1)

            def copy_values(p, j):
                act.wait_ge(vt_ready, p + 1)
                act.activation(vN[:, j, :, :].rearrange("p a b -> p (a b)"), ps[7][:], ACT.Copy).then_inc(qkv_copied, 1)
                act.wait_ge(qkv_copied, p * 4 + 4)
                act.sem_inc(q_free, 1)

            def softplus_log(p, h, first):
                act.wait_ge(z_ready, p * 2 + (h + 1))
                if not first:
                    act.wait_ge(sp_ready, p * 6 + (3 * h - 3))
                for b, off, w in BANKS3:
                    act.activation(lg[:, h, off:off + w], ps[3 * h + b][:, 0:w], ACT.Abs).then_inc(abs_ready, 1)
                act.wait_ge(abs_ready, p * 6 + (3 * h + 3))
                act.activation(lg[:, h, :], lg[:, h, :], ACT.Exp, scale=-1.0).then_inc(e_ready, 1)
                act.wait_ge(e_ready, p * 2 + (h + 1))
                act.activation(lg[:, h, :], lg[:, h, :], ACT.Ln, bias=1.0).then_inc(ln_ready, 1)

            def probabilities(p, h, first):
                act.wait_ge(cum_ready, p * 2 + (h + 1))
                if not first:
                    act.wait_ge(av_ready, p * 2 + (h - 1))
                for b, off, w in BANKS3:
                    act.activation(aT[:, h, off:off + w], ps[3 * h + b][:, 0:w], ACT.Exp).then_inc(a_ready, 1)

            def pair(p, j, more, first=False):
                softplus_log(p, 0, first)
                softplus_log(p, 1, first)
                if more:
                    copy_qkv(p + 1, 1 - j, 0)
                probabilities(p, 0, first)
                if more:
                    copy_qkv(p + 1, 1 - j, 1)
                probabilities(p, 1, first)
                if more:
                    copy_qkv(p + 1, 1 - j, 2)
                act.wait_ge(av_ready, p * 2 + 2)
                act.activation(mH[:, bass.ds(p, 1), :].rearrange("p o t -> p (o t)"), ps[6][:], ACT.Copy)\
                    .then_inc(m_high, 1)
                if more:
                    copy_values(p + 1, 1 - j)

            act.sem_inc(q_free, 1)
            for which in range(3):
                copy_qkv(0, 0, which)
            copy_values(0, 0)
            pair(0, 0, True, first=True)
            pair(1, 1, True)
            with act.Fori(1, KT // 2 - 1) as t:
                pair(t * 2, 0, True)
                pair(t * 2 + 1, 1, True)
            pair(KT - 2, 0, True)
            pair(KT - 1, 1, False)

            act.wait_ge(m_ready, KT)
            load_p(1)
            layer_norm("mix1", xf, "mix_g1", "mix_b1")
            ple(1)
            ffn(1)
            layer_norm("ffn1", xf, "ffn_g1", "ffn_b1")

            def pre_norm(name, ready, base, step=1):
                squares(name, xf, ready, base, step)
                std(name, 2, 1)
                for n in range(KT):
                    act.wait_ge(normed, 8 * NORM[name] + n + 1)
                    act.activation(xH[:, n, :], tmp[:, n, :], ACT.Copy, scale=pc(name, n)).then_inc(x_high, 1)

            def post_norm(name):
                squares(name, tmp, src_ready, 8 * SRC[name])
                std(name, 1, 1)

            pre_norm("ff1_pre", affine, 64, 2)
            ffn(2)
            act.wait_ge(chunk_done, CHUNK["down2"] + FT)
            act.dma_start(ropeT[:].rearrange("p a t -> p (a t)"), rope).then_inc(rope_loaded, 16)
            for kv in range(2):
                act.dma_start(w1b[:, kv, :], w1[kv]).then_inc(w1_loaded, 16)
            post_norm("ff1_post")
            pre_norm("mix_pre", updated, 0)

            c0 = CHUNK["hybrid"]

            def item(i):
                kind, name, h = ITEMS[i]
                act.wait_ge(chunk_done, c0 + i + 1)
                if kind == "copy":
                    act.activation(kcvc[:, i, :], ps[7][:], ACT.Copy).then_inc(b7_read, 1)
                elif kind == "rope":
                    r = ROPES.index(i)
                    if r >= 2:
                        act.wait_ge(roped, r - 1)
                    act.activation(pre[:, r % 2, :], ps[7][:], ACT.Copy,
                                   scale=DH ** -0.5 if name in ("dq", "nq") else 1.0).then_inc(b7_read, 1)
                else:
                    act.activation(vturn0[:], ps[7][:], ACT.Sigmoid if kind == "gate" else ACT.Copy)\
                        .then_inc(b7_read, 1)
                    act.wait_ge(second_done, SECONDS.index(("second", i)) + 1)
                    if kind == "gate":
                        act.activation(gN[:], ps[7][:].rearrange("p (q g) -> p q g", q=QT)[:, :, 0:24], ACT.Copy)\
                            .then_inc(b7_read, 1)
                    else:
                        dst = {"vs": vsN[:], "vw": vwN[:], "dv": dvN[:, h % 2, :, :]}[name]
                        act.activation(dst, ps[7][:].rearrange("p (q g) -> p q g", q=QT), ACT.Copy)\
                            .then_inc(b7_read, 1)

            for i in range(7):
                item(i)
            act.wait_ge(lam_steps, 2)
            act.activation(st[:, 130:132], st[:, 128:130], ACT.Exp).then_inc(lam_steps, 1)
            act.wait_ge(hid_psum, 1)
            for g in range(2):
                act.activation(hid[:, 4 * g:4 * g + 4, 0:NC],
                               ps[3 + g][:, 0:P].rearrange("p (k c) -> p k c", k=4)[:, :, 0:NC],
                               ACT.Gelu_apprx_tanh).then_inc(hid_ready, 1)
            act.wait_ge(second_done, SECONDS.index(("compressed",)) + 1)
            act.activation(vcC[0:NC, :], ps[5][0:NC, 0:P], ACT.Copy).then_inc(hid_ready, 1)
            act.activation(kcC[:, 0:NC], ps[7][:, 0:NC], ACT.Copy).then_inc(b7_read, 1)
            act.wait_ge(hid_ready, 3)
            for i in range(7, 10):
                item(i)

            def exps(u, m):
                act.wait_ge(max_ready, 8 * u + 4 * m + 4)
                for t in range(QT):
                    qt = QT - 1 - t
                    o, f = TILE_COL[t], TILE_OFF[t]
                    act.activation(prob[:, m, f:f + TILE_W[t]], ps[3 * m + TILE_BANK[t]][:, o:o + TILE_W[t]], ACT.Exp,
                                   bias=st[:, 4 * m + qt:4 * m + qt + 1],
                                   accum_out=st[:, 8 + 4 * m + qt:9 + 4 * m + qt]).then_inc(p_exp, 1)

            def copy_turned(m, n):
                act.wait_ge(turned, n)
                for b, off, w in BANKS3:
                    act.activation(AT[:, m, off:off + w], ps[3 * m + b][:, 0:w], ACT.Copy).then_inc(at_ready, 1)

            for h in range(DIFF_HEADS):
                if h:
                    act.wait_ge(turned, h)
                exps(h, 0)
                exps(h, 1)
                nxt = list(range(10 + 3 * h, 13 + 3 * h)) if h < 3 else [19]
                for i in nxt[:2]:
                    item(i)
                copy_turned(0, h + 1)
                for i in nxt[2:]:
                    item(i)
                act.wait_ge(o_ready, h + 1)
                act.activation(oN[:, :, h * P:h * P + P], ps[6][:].rearrange("p (q d) -> p q d", q=QT), ACT.Copy)\
                    .then_inc(o_copied, 1)
            for j in range(4):
                act.wait_ge(cmp_steps, 4 * j + 3)
                act.activation(pc_n[:], pc_n[:], ACT.Exp).then_inc(cmp_exp, 1)
                for g in range(2):
                    u = DIFF_HEADS + 2 * j + g
                    v = u - DIFF_HEADS
                    act.wait_ge(turned, DIFF_HEADS + 2 * v)
                    exps(u, 0)
                    exps(u, 1)
                    if g == 0 and j < 3:
                        item(20 + j)
                    act.wait_ge(second_done, SECONDS.index(("cmp_turn", j, g)) + 1)
                    act.activation(pcT[0:NC, :, :].rearrange("p q d -> p (q d)"), ps[7][0:NC, :], ACT.Copy)\
                        .then_inc(b7_read, 1)
                    copy_turned(0, DIFF_HEADS + 2 * v + 1)
                    act.wait_ge(o_ready, u + 1)
                    c = (DIFF_HEADS + j) * P + g * DH
                    act.activation(oN[:, :, c:c + DH], ps[6][:, 0:QT * DH].rearrange("p (q d) -> p q d", q=QT),
                                   ACT.Copy).then_inc(o_copied, 1)
            act.wait_ge(head_sq, 2)
            act.activation(st[:, 48:64], st[:, 32:48], ACT.Sqrt, scale=1.0 / P, bias=cc("eps", 2)[:, 1:2])\
                .then_inc(head_std, 1)
            for n in range(KT):
                act.wait_ge(o_turned, n + 1)
                act.activation(xH[:, n, :], ps[n][:], ACT.Copy, scale=pc("subln") if n < DIFF_HEADS else 1.0)\
                    .then_inc(x_high, 1)
            post_norm("mix_post")
            pre_norm("ff2_pre", updated, 8)
            ffn(3)
            post_norm("ff2_post")
            act.wait_ge(updated, 24)
            act.dma_start(out.rearrange("(k p) t -> p k t", p=P), xf[:]).then_inc(out_done, 16)
            act.wait_ge(out_done, 16)

        @block.vector
        def _(dve):
            def low_part(n):
                dve.tensor_tensor(xL[:, n, :], xf[:, n, :], fp(xH[:, n, :]), ALU.subtract).then_inc(x_ready, 1)

            dve.memset(gpad[:, :, 0:CONV_W - 1], 0.0).then_inc(glu_pad, 1)
            dve.wait_ge(in_loaded, 48)
            for n in range(KT):
                dve.wait_ge(x_high, n + 1)
                low_part(n)
            dve.sem_inc(glu_banks_free, 2)

            def take_banks(name, fn):
                for n in range(KT):
                    if n < 7:
                        dve.wait_ge(bank_done, 7 * FULL[name] + n + 1)
                    else:
                        dve.wait_ge(chunk_done, CHUNK[name] + dict(COUNTS)[name])
                    fn(n)

            def add_residual(n):
                dve.tensor_tensor(xf[:, n, :], ps[n][:], xf[:, n, :], ALU.add).then_inc(src_ready, 1)

            def reciprocal(name):
                i = NORM[name]
                dve.wait_ge(std_ready, i + 1)
                dve.reciprocal(rstd[:], rstd[:]).then_inc(rstd_ready, 1)
                dve.wait_ge(rstd_ready, i + 1)

            def layer_norm(name, src):
                li = LNORM.index(name)
                dve.wait_ge(mean_ready, li + 1)
                for n in range(KT):
                    dve.tensor_tensor(src[:, n, :], src[:, n, :], ps[0][:], ALU.subtract).then_inc(centered, 1)
                reciprocal(name)
                for n in range(KT):
                    dve.tensor_tensor(src[:, n, :], src[:, n, :], rstd[:], ALU.mult).then_inc(normed, 1)
                if name == "ffn1":
                    return
                for n in range(KT):
                    dve.wait_ge(affine, 16 * li + 2 * n + 2)
                    if name == "conf":
                        dve.tensor_tensor(cL[:, n, :], src[:, n, :], fp(cH[:, n, :]), ALU.subtract).then_inc(c_ready, 1)
                    else:
                        low_part(n)

            def ple(layer):
                for k in range(2):
                    dve.wait_ge(p_high, 2 * layer + k + 1)
                    i = dve.tensor_tensor(pL[:, k, :], pf[:, k, :], fp(pH[:, k, :]), ALU.subtract)
                    if k == 1:
                        i.then_inc(p_ready, 1)
                dve.wait_ge(proj_copied, KT * (layer + 1))
                dve.sem_inc(ple_free, 2)
                with dve.Fori(0, KT // 2) as t:
                    for j in range(2):
                        n = t * 2 + j
                        dve.wait_ge(ple_sig, t * 2 + (KT * layer + j + 1))
                        proj = tmp[:, bass.ds(n, 1), :].rearrange("p o t -> p (o t)")
                        x_n = xf[:, bass.ds(n, 1), :].rearrange("p o t -> p (o t)")
                        dve.tensor_tensor(proj, sq[j], proj, ALU.mult).then_inc(ple_mul, 1)
                        dve.wait_ge(ple_mul, t * 2 + (KT * layer + j + 1))
                        dve.scalar_tensor_tensor(x_n, x_n, ALPHA, proj, ALU.mult, ALU.add).then_inc(ple_free, 1)
                dve.wait_ge(ple_free, 10 * layer + 10)

            def ffn(inst):
                c0 = CHUNK[f"gateup{inst}"]
                dve.sem_inc(h_made, 2)
                with dve.Fori(0, FT // 2) as t:
                    for j in range(2):
                        f = t * 2 + j
                        if inst < 2:
                            dve.wait_ge(tap2, t * 2 + (FT * inst + j + 1))
                            for tap in (1, 0):
                                back = FCONV_W - 1 - tap
                                dve.scalar_tensor_tensor(tmp[:, j, back:S], ps[2 * j][:, 0:S - back],
                                                         pc(f"fcw{inst}", f * FCONV_W + tap), tmp[:, j, back:S],
                                                         ALU.mult, ALU.add).then_inc(tap10, 1)
                                if tap == 1:
                                    dve.wait_ge(tap10, t * 4 + (2 * FT * inst + 2 * j + 1))
                        dve.wait_ge(gate_act, t * 2 + (FT * inst + j + 1))
                        dve.wait_ge(chunk_done, t * 4 + (c0 + 2 * j + 2))
                        dve.tensor_tensor(tmp[:, 2 + j, :], ps[2 * j + 1][:], tmp[:, j, :], ALU.mult).then_inc(h_made, 1)
                        dve.wait_ge(h_high, t * 2 + (FT * inst + j + 1))
                        dve.tensor_tensor(hL[:, bass.ds(f, 1), :].rearrange("p o t -> p (o t)"), tmp[:, 2 + j, :],
                                          fp(hH[:, bass.ds(f, 1), :].rearrange("p o t -> p (o t)")), ALU.subtract)\
                            .then_inc(h_ready, 1)

            dve.wait_ge(glu_pad, 1)
            with dve.Fori(0, KT // 2) as t:
                for j in range(2):
                    n = t * 2 + j
                    conv = tmp[:, bass.ds(n, 1), :].rearrange("p o t -> p (o t)")
                    dve.wait_ge(glu_sig, t * 2 + (j + 1))
                    dve.wait_ge(chunk_done, t * 4 + (2 * j + 2))
                    dve.scalar_tensor_tensor(gpad[:, j, CONV_W - 1:], ps[2 * j + 1][:], pc("pw1_ba", n), sq[j],
                                             ALU.add, ALU.mult).then_inc(glu_banks_free, 1)
                    dve.wait_ge(glu_banks_free, t * 2 + (j + 3))
                    for tap in range(CONV_W):
                        w = pc("dw_w", n * CONV_W + tap)
                        if tap == 0:
                            i = dve.tensor_scalar(conv, gpad[:, j, 0:S], w, pc("dw_b", n), ALU.mult, ALU.add)
                        else:
                            i = dve.scalar_tensor_tensor(conv, gpad[:, j, tap:tap + S], w, conv, ALU.mult, ALU.add)
                        i.then_inc(taps, 1)
                        dve.wait_ge(taps, t * (2 * CONV_W) + (CONV_W * j + tap + 1))
                    dve.sem_inc(src_ready, 1)
            layer_norm("conf", tmp)
            for n in range(KT):
                dve.tensor_scalar(xf[:, n, :], xf[:, n, :], ALPHA, pc("pw2_b", n), ALU.mult, ALU.add).then_inc(res_scaled, 1)
            dve.wait_ge(res_scaled, KT)
            take_banks("pw2", add_residual)
            layer_norm("mix0", xf)
            ple(0)
            ffn(0)
            take_banks("down0", add_residual)
            layer_norm("ffn0", xf)

            for n in range(KT):
                dve.tensor_scalar(xf[:, n, :], xf[:, n, :], ALPHA, None, ALU.mult).then_inc(res_scaled, 1)

            def softplus(p, h):
                dve.wait_ge(ln_ready, p * 2 + (h + 1))
                for b, off, w in BANKS3:
                    dve.scalar_tensor_tensor(sp[:, h, off:off + w], ps[3 * h + b][:, 0:w], 0.0, lg[:, h, off:off + w],
                                             ALU.max, ALU.add).then_inc(sp_ready, 1)

            def pair(p):
                softplus(p, 0)
                softplus(p, 1)
                dve.wait_ge(m_high, p + 1)
                m = bass.ds(p, 1)
                dve.tensor_tensor(mL[:, m, :].rearrange("p o t -> p (o t)"), ps[6][:],
                                  fp(mH[:, m, :].rearrange("p o t -> p (o t)")), ALU.subtract).then_inc(m_ready, 1)

            with dve.Fori(0, KT) as p:
                pair(p)
            dve.wait_ge(res_scaled, 2 * KT)
            take_banks("wo", add_residual)
            layer_norm("mix1", xf)
            ple(1)
            ffn(1)
            take_banks("down1", add_residual)
            layer_norm("ffn1", xf)

            def copy_product(n):
                dve.tensor_copy(tmp[:, n, :], ps[n][:]).then_inc(src_ready, 1)

            def pre_norm(name):
                reciprocal(name)
                for n in range(KT):
                    dve.tensor_tensor(tmp[:, n, :], xf[:, n, :], rstd[:], ALU.mult).then_inc(normed, 1)
                for n in range(KT):
                    dve.wait_ge(x_high, 8 * XH[name] + n + 1)
                    dve.scalar_tensor_tensor(xL[:, n, :], tmp[:, n, :], pc(name, n), fp(xH[:, n, :]), ALU.mult,
                                             ALU.subtract).then_inc(x_ready, 1)

            def post_norm(name):
                reciprocal(name)
                for n in range(KT):
                    dve.tensor_tensor(tmp[:, n, :], tmp[:, n, :], rstd[:], ALU.mult).then_inc(normed, 1)
                for n in range(KT):
                    dve.wait_ge(normed, 8 * NORM[name] + n + 1)
                    dve.scalar_tensor_tensor(xf[:, n, :], tmp[:, n, :], pc(name, n), xf[:, n, :], ALU.mult, ALU.add)\
                        .then_inc(updated, 1)

            dve.wait_ge(affine, 80)
            pre_norm("ff1_pre")
            ffn(2)
            take_banks("down2", copy_product)
            post_norm("ff1_post")
            dve.wait_ge(updated, 8)
            pre_norm("mix_pre")

            lam = pc("lams", 0, 4 * DH).rearrange("p (a b d) -> p a b d", a=2, b=2)
            dve.tensor_tensor(st[:, 0:2 * DH].rearrange("p (a d) -> p a d", a=2), lam[:, :, 0, :], lam[:, :, 1, :],
                              ALU.mult).then_inc(lam_steps, 1)
            dve.wait_ge(lam_steps, 1)
            dve.tensor_reduce(st[:, 128:130], st[:, 0:2 * DH].rearrange("p (a d) -> p a d", a=2), AX_X, ALU.add)\
                .then_inc(lam_steps, 1)

            def item(i):
                kind, name, h = ITEMS[i]
                if kind == "copy":
                    dve.wait_ge(b7_read, USE["item", i] + 1)
                    blk = (blk_k, blk_v)[i]
                    for half in range(2):
                        src = kcvc[:, i, 16 * half:16 * half + NC * 16].rearrange("p (c s) -> p c s", s=16)
                        pe_ = pc(("pe_k", "pe_v")[i], 16 * half, 16).unsqueeze(1).broadcast_to([P, NC, 16])
                        dve.tensor_tensor(blk[:, :, 16 * half:16 * half + 16], src, pe_, ALU.add)\
                            .then_inc(blocks_ready, 1)
                elif kind == "rope":
                    r = ROPES.index(i)
                    dst = {"ks": ksT[:], "kw": kwT[:], "dq": dqT[:, h % 2, :], "dk": dkT[:, h % 2, :],
                           "nq": nqT[:, h % 2, :]}[name]
                    if r == 0:
                        dve.wait_ge(rope_loaded, 16)
                    else:
                        dve.wait_ge(roped, r)
                    dve.wait_ge(second_done, SECONDS.index(("second", i)) + 1)
                    dve.tensor_tensor(rot, ps[7][:], ropeT[:, 1, :], ALU.mult).then_inc(b7_read, 1)
                    dve.tensor_tensor(pre[:, r % 2, :], pre[:, r % 2, :], ropeT[:, 0, :], ALU.mult)\
                        .then_inc(rot_ready, 1)
                    dve.wait_ge(rot_ready, r + 1)
                    dve.wait_ge(b7_read, USE["second", i] + 1)
                    dve.tensor_tensor(dst, pre[:, r % 2, :], rot, ALU.add).then_inc(roped, 1)

            for i in range(7):
                item(i)
            dve.wait_ge(lam_steps, 3)
            dve.scalar_tensor_tensor(st[:, 132:133], st[:, 131:132], -LAMBDA_INIT, st[:, 130:131], ALU.add,
                                     ALU.subtract).then_inc(lam_steps, 1)
            for i in range(7, 10):
                item(i)

            def maxima(u, m):
                dve.wait_ge(s_ready, 2 * u + m + 1)
                for t in range(QT):
                    qt = QT - 1 - t
                    o = TILE_COL[t]
                    dve.tensor_reduce(st[:, 4 * m + qt:4 * m + qt + 1], ps[3 * m + TILE_BANK[t]][:, o:o + TILE_W[t]],
                                      AX_X, ALU.max, negate=True).then_inc(max_ready, 1)

            for h in range(DIFF_HEADS):
                if h:
                    dve.wait_ge(p_exp, 8 * h)
                maxima(h, 0)
                maxima(h, 1)
                nxt = list(range(10 + 3 * h, 13 + 3 * h)) if h < 3 else [19]
                dve.wait_ge(p_exp, 8 * h + 8)
                if h:
                    dve.wait_ge(p_ready2, QT * h)
                dve.reciprocal(st[:, 16:24], st[:, 8:16]).then_inc(coef_ready, 1)
                if h == 0:
                    dve.wait_ge(lam_steps, 4)
                dve.wait_ge(coef_ready, 2 * h + 1)
                dve.tensor_scalar(st[:, 24:28], st[:, 20:24], st[:, 132:133], None, ALU.mult).then_inc(coef_ready, 1)
                dve.wait_ge(coef_ready, 2 * h + 2)
                for t in range(QT):
                    qt = QT - 1 - t
                    f = slice(TILE_OFF[t], TILE_OFF[t] + TILE_W[t])
                    dve.tensor_scalar(prob[:, 1, f], prob[:, 1, f], st[:, 24 + qt:25 + qt], None, ALU.mult)\
                        .then_inc(scaled, 1)
                for t in range(QT):
                    qt = QT - 1 - t
                    f = slice(TILE_OFF[t], TILE_OFF[t] + TILE_W[t])
                    dve.wait_ge(scaled, QT * h + t + 1)
                    dve.scalar_tensor_tensor(prob[:, 0, f], prob[:, 0, f], st[:, 16 + qt:17 + qt], prob[:, 1, f],
                                             ALU.mult, ALU.add).then_inc(p_ready2, 1)
                for i in nxt:
                    item(i)
            dve.wait_ge(o_copied, DIFF_HEADS)
            for j in range(4):
                dve.wait_ge(second_done, SECONDS.index(("cmp_scores", j)) + 1)
                if j:
                    dve.wait_ge(second_done, SECONDS.index(("cmp_turn", j - 1, 1)) + 1)
                cadd = cc("cadd", QT * NC).rearrange("p (q c) -> p q c", q=QT)
                cmul = cc("cmul", QT * NC).rearrange("p (q c) -> p q c", q=QT)
                base = 4 * j
                for g in range(2):
                    i = dve.tensor_tensor(pc_n[:, g, :, :], ps[7 - g][:, 0:QT * NC]
                                          .rearrange("p (q c) -> p q c", q=QT), cadd, ALU.add)
                    i.then_inc(b7_read if g == 0 else cmp_steps, 1)
                dve.wait_ge(b7_read, USE["cmp_scores", j] + 1)
                dve.wait_ge(cmp_steps, base + 1)
                flatc = pc_n[:].rearrange("p g q c -> p (g q) c")
                dve.tensor_reduce(st[:, 64:72], flatc, AX_X, ALU.max).then_inc(cmp_steps, 1)
                dve.wait_ge(cmp_steps, base + 2)
                dve.tensor_tensor(flatc, flatc, st[:, 64:72].unsqueeze(2).broadcast_to([P, 8, NC]), ALU.subtract)\
                    .then_inc(cmp_steps, 1)
                dve.wait_ge(cmp_exp, j + 1)
                dve.tensor_reduce(st[:, 72:80], flatc, AX_X, ALU.add).then_inc(cmp_sum, 1)
                dve.wait_ge(cmp_sum, 3 * j + 1)
                dve.reciprocal(st[:, 80:88], st[:, 72:80]).then_inc(cmp_sum, 1)
                dve.wait_ge(cmp_sum, 3 * j + 2)
                for g in range(2):
                    gate = gN[:, :, 3 * (4 * g + j)]
                    i = dve.tensor_tensor(st[:, 88 + 4 * g:92 + 4 * g], gate, st[:, 80 + 4 * g:84 + 4 * g], ALU.mult)
                    if g == 1:
                        i.then_inc(cmp_sum, 1)
                dve.wait_ge(cmp_sum, 3 * j + 3)
                for g in range(2):
                    i = dve.tensor_tensor(pc_n[:, g, :, :], pc_n[:, g, :, :], cmul, ALU.mult)
                    if g == 1:
                        i.then_inc(cmp_steps, 1)
                dve.wait_ge(cmp_steps, base + 4)
                dve.tensor_tensor(flatc, flatc, st[:, 88:96].unsqueeze(2).broadcast_to([P, 8, NC]), ALU.mult)\
                    .then_inc(cmp_ready, 1)
                for g in range(2):
                    u = DIFF_HEADS + 2 * j + g
                    v = u - DIFF_HEADS
                    dve.wait_ge(p_exp, 8 * u)
                    maxima(u, 0)
                    maxima(u, 1)
                    dve.wait_ge(p_exp, 8 * u + 8)
                    dve.wait_ge(p_ready2, QT * DIFF_HEADS + 8 * v)
                    dve.reciprocal(st[:, 16:24], st[:, 8:16]).then_inc(coef_ready, 1)
                    c = 2 * DIFF_HEADS + 2 * v
                    dve.wait_ge(coef_ready, c + 1)
                    for m in range(2):
                        i = dve.tensor_tensor(st[:, 24 + 4 * m:28 + 4 * m], gN[:, :, 3 * (4 * g + j) + 1 + m],
                                              st[:, 16 + 4 * m:20 + 4 * m], ALU.mult)
                    i.then_inc(coef_ready, 1)
                    dve.wait_ge(coef_ready, c + 2)
                    for m in range(2):
                        for t in range(QT):
                            qt = QT - 1 - t
                            f = slice(TILE_OFF[t], TILE_OFF[t] + TILE_W[t])
                            dve.tensor_scalar(prob[:, m, f], prob[:, m, f], st[:, 24 + 4 * m + qt:25 + 4 * m + qt],
                                              None, ALU.mult).then_inc(p_ready2, 1)
                    if g == 0 and j < 3:
                        item(20 + j)
                    dve.wait_ge(turned, DIFF_HEADS + 2 * v + 2)
                    for b, off, w in BANKS3:
                        dve.tensor_copy(AT[:, 1, off:off + w], ps[3 + b][:, 0:w]).then_inc(at2_ready, 1)
            heads = oN[:, :, 0:DIFF_HEADS * P].rearrange("p q (h d) -> p q h d", h=DIFF_HEADS)
            sqs = flat[:, 0:QT * DIFF_HEADS * P].rearrange("p (q h d) -> p q h d", q=QT, h=DIFF_HEADS)
            dve.wait_ge(turned, DIFF_HEADS + 16)
            for q in range(QT):
                i = dve.tensor_tensor(sqs[:, q], heads[:, q], heads[:, q], ALU.mult)
            i.then_inc(head_sq, 1)
            dve.wait_ge(head_sq, 1)
            dve.tensor_reduce(st[:, 32:48], flat[:, 0:QT * DIFF_HEADS * P].rearrange("p (a d) -> p a d", d=P), AX_X,
                              ALU.add).then_inc(head_sq, 1)
            dve.wait_ge(head_std, 1)
            dve.reciprocal(st[:, 96:112], st[:, 48:64]).then_inc(head_sq, 1)
            dve.wait_ge(head_sq, 3)
            for q in range(QT):
                for h in range(DIFF_HEADS):
                    k = 96 + q * DIFF_HEADS + h
                    dve.tensor_scalar(heads[:, q, h, :], heads[:, q, h, :], st[:, k:k + 1], None, ALU.mult)\
                        .then_inc(head_done, 1)
            for n in range(KT):
                dve.wait_ge(x_high, 8 * XH["mixer"] + n + 1)
                if n < DIFF_HEADS:
                    dve.scalar_tensor_tensor(xL[:, n, :], ps[n][:], pc("subln"), fp(xH[:, n, :]), ALU.mult,
                                             ALU.subtract).then_inc(x_ready, 1)
                else:
                    dve.tensor_tensor(xL[:, n, :], ps[n][:], fp(xH[:, n, :]), ALU.subtract).then_inc(x_ready, 1)
            take_banks("wout", copy_product)
            post_norm("mix_post")
            dve.wait_ge(updated, 16)
            pre_norm("ff2_pre")
            ffn(3)
            take_banks("down3", copy_product)
            post_norm("ff2_post")


def lay_out(inputs):
    import numpy as np
    a = {k: np.asarray(v) for k, v in inputs.items()}

    def by_output(w):
        n = w.shape[1] // P
        return w.reshape(KT, P, n, P).transpose(2, 1, 0, 3).reshape(n, P, KT * P)

    def by_k(w):
        return w.reshape(w.shape[0] // P, P, D)

    def mixed(*ws):
        return np.stack([by_output(w) for w in ws], axis=1).reshape(-1, P, KT * P)

    w_in = a["w_in_2"][0]
    sizes = [512, 512, 512, 512] + [128] * 6 + [24]
    at = np.concatenate([[0], np.cumsum(sizes)])
    dq, dk, dv, nq, kc, vc, ks, vs, kw, vw, gl = [w_in[:, at[i]:at[i + 1]] for i in range(11)]
    nq = nq.reshape(D, 2, 4, DH).transpose(0, 2, 1, 3).reshape(D, 512)
    gl = np.concatenate([gl, np.zeros((D, P - 24), np.float32)], axis=1)
    wo2 = a["w_out_2"][0]
    wo2 = np.concatenate([wo2[:512], wo2[512:].reshape(2, 4, DH, D).transpose(1, 0, 2, 3).reshape(512, D)], axis=0)
    parts = [mixed(a["a_pw1_w"][0][:, D:], a["a_pw1_w"][0][:, :D]), by_k(a["a_pw2_w"][0])]
    for l in range(2):
        if l == 1:
            parts += [mixed(a["b_wq"][0], a["kv_wk"], a["kv_wv"]), by_k(a["b_wo"][0])]
        parts += [by_k(a["ple_w_proj"][l]), by_output(a["ple_w_gate"][l]),
                  mixed(a["ffn_w_gate"][l], a["ffn_w_up"][l]), by_k(a["ffn_w_down"][l])]
    parts += [mixed(a["ff1_w_gate_2"][0], a["ff1_w_up_2"][0]), by_k(a["ff1_w_down_2"][0]), 
              *[by_output(w) for w in (kc, vc, ks, vs, kw, vw, gl)], mixed(dq, dk, dv), by_output(nq), by_k(wo2)]
    parts += [mixed(a["ff2_w_gate_2"][0], a["ff2_w_up_2"][0]), by_k(a["ff2_w_down_2"][0])]
    ws = np.concatenate(parts, axis=0)
    assert ws.shape[0] == NCHUNKS

    def col(v):
        return v.reshape(-1, P).T

    def taps(w):
        return w.reshape(w.shape[0], -1, P).transpose(2, 1, 0).reshape(P, -1)

    v = {"pw1_ba": col(a["a_pw1_b"][0][:D]), "pw1_bg": col(a["a_pw1_b"][0][D:]), "dw_w": taps(a["a_dw_w"][0]),
         "dw_b": col(a["a_dw_b"][0]), "aln_g": col(a["a_ln_g"][0]), "aln_b": col(a["a_ln_b"][0]),
         "pw2_b": col(a["a_pw2_b"][0])}
    for l in range(2):
        v[f"mix_g{l}"] = col(a["ln_mix_g"][l])
        v[f"mix_b{l}"] = col(a["ln_mix_b"][l])
        v[f"fcw{l}"] = taps(a["ffn_conv_w"][l])
        v[f"fcb{l}"] = col(a["ffn_conv_b"][l])
        v[f"ffn_g{l}"] = col(a["ln_ffn_g"][l])
        v[f"ffn_b{l}"] = col(a["ln_ffn_b"][l])
    for n, m in (("ff1_pre", "ff1_norm_pre_2"), ("ff1_post", "ff1_norm_post_2"), ("mix_pre", "mix_norm_pre_2"),
                 ("mix_post", "mix_norm_post_2"), ("ff2_pre", "ff2_norm_pre_2"), ("ff2_post", "ff2_norm_post_2")):
        v[n] = col(a[m][0])
    v["subln"] = col(a["diff_subln_2"][0])
    v["pe_k"] = np.tile(a["cmp_pe_k_2"][0].T, (2, 1))
    v["pe_v"] = np.tile(a["cmp_pe_v_2"][0].T, (2, 1))
    v["w2_k"] = a["cmp_k_w2_2"][0].reshape(2, P, DH).transpose(1, 0, 2).reshape(P, 2 * DH)
    v["w2_v"] = a["cmp_v_w2_2"][0].reshape(2, P, DH).transpose(1, 0, 2).reshape(P, 2 * DH)
    v["lams"] = np.tile(np.concatenate([a[f"lambda_{n}_2"][0] for n in ("q1", "k1", "q2", "k2")])[None], (P, 1))
    params = np.concatenate([v[n] for n, _ in PARAMS], axis=1)
    w1 = np.stack([np.tile(a[f"cmp_{n}_w1_2"][0].reshape(CMP_BLOCK, DH, CMP_HID).transpose(1, 0, 2), (2, 1, 1))
                   for n in "kv"])
    return {"ws": ws, "xT": np.ascontiguousarray(a["x"][0].T),
            "pT": np.ascontiguousarray(a["p"][:, 0].transpose(0, 2, 1)), "params": params, "w1": w1}


def constants():
    import numpy as np
    i = np.arange(P)
    later = i[None, :] > i[:, None]
    c = {"ident": np.eye(P), "mean": np.full((P, P), 1.0 / D), "negtri": -(i[:, None] >= i[None, :]).astype(float),
         "negone": -np.ones((P, P)), "maskS": np.where(later, 0.0, NEG), "maskC": np.where(later, NEG, 0.0),
         "eps": np.tile(np.array([[LN_EPS, RMS_EPS]]), (P, 1))}
    d = i % DH
    partner = np.where(d < 8, i + 8, np.where(d < 16, i - 8, i))
    c["perm"] = (i[:, None] == partner[None, :]).astype(float)
    t = np.arange(S).reshape(QT, P)
    cend = np.arange(NC) * CMP_STRIDE + CMP_BLOCK - 1
    valid = cend[None, None, :] <= t.T[:, :, None]
    c["cadd"] = np.where(valid, 0.0, NEG).reshape(P, -1)
    c["cmul"] = valid.astype(float).reshape(P, -1)
    consts = np.concatenate([c[n] for n, _ in CONSTS], axis=1).astype(np.float32)
    inv = (500000.0 ** (-np.arange(0, 16, 2) / 16.0)).astype(np.float32)
    ang = (np.arange(S, dtype=np.float32)[None, :] * inv[:, None]).astype(np.float64)
    cos, sin = np.cos(ang), np.sin(ang)
    table = np.zeros((P, 2, S))
    table[:, 0] = 1.0
    for base in (0, DH):
        table[base:base + 8, 0] = cos
        table[base + 8:base + 16, 0] = cos
        table[base:base + 8, 1] = -sin
        table[base + 8:base + 16, 1] = sin
    return consts, table.reshape(P, 2 * S).astype(np.float32)


def kernel(**inputs):
    import numpy as np
    import concourse.bacc as bacc
    from concourse.bass_utils import run_bass_kernel_spmd as run

    arrays = lay_out(inputs)
    arrays["consts"], arrays["rope"] = constants()
    nc = bacc.Bacc("TRN2", target_bir_lowering=False, num_devices=1)
    names = ["ws", "xT", "pT", "params", "consts", "rope", "w1"]
    arrays = {n: np.ascontiguousarray(arrays[n]) for n in names}
    args = [nc.dram_tensor(n, arrays[n].shape, mybir.dt.from_np(arrays[n].dtype), kind="ExternalInput").ap()
            for n in names]
    out = nc.dram_tensor("out", (D, S), F32, kind="ExternalOutput").ap()
    build_block(nc, *args, out)
    r = run(nc, [arrays], core_ids=[0])
    return np.ascontiguousarray(r.results[0]["out"].T)[None]
```

```python
from contextlib import ExitStack

import concourse.bass as bass
from concourse import mybir

F32 = mybir.dt.float32
F32R = mybir.dt.float32r
BF16 = mybir.dt.bfloat16
ACT = mybir.ActivationFunctionType
ALU = mybir.AluOpType
AX_X = mybir.AxisListType.X

P = 128
S = 512
D = 1024
KT = D // P
F = 2816
FT = F // P
CONV_W = 31
PE_TAPS = 9
DVE_STEPS = CONV_W - PE_TAPS + 1
FCONV_W = 3
QT = S // P
DH = 64
LN_EPS = 1e-5
RMS_EPS = 1e-6
ALPHA = 4.0 ** 0.25
NEG = -1e30
RAW = 4
CMP_BLOCK = 32
CMP_STRIDE = 16
NC = S // CMP_STRIDE - 1
CMP_HID = 256
PAIRS = CMP_BLOCK // 2
NSA_HEADS = 8
DIFF_HEADS = 4

COUNTS = [("pw1", 2 * KT), ("pw2", KT)]
for _l in range(2):
    if _l == 1:
        COUNTS += [("qkv", 3 * KT), ("wo", KT)]
    COUNTS += [(f"ple{_l}", KT + 2), (f"gateup{_l}", 2 * FT), (f"down{_l}", FT)]
COUNTS += [("gateup2", 2 * FT), ("down2", FT), ("hybrid", 7 + 3 * DIFF_HEADS + 4), ("wout", KT), ("gateup3", 2 * FT),
           ("down3", FT)]
PLE_ORDER = [("gate", 0), ("gate", 1), ("proj", 0), ("gate", 2), ("gate", 3), ("gate", 4), ("gate", 5), ("proj", 1),
             ("gate", 6), ("gate", 7)]
CHUNK = {}
NCHUNKS = 0
for _n, _k in COUNTS:
    CHUNK[_n] = NCHUNKS
    NCHUNKS += _k

PARAMS = [("pw1_ba", KT), ("pw1_bg", KT), ("dw_w", KT * CONV_W), ("dw_b", KT), ("aln_g", KT), ("aln_b", KT),
          ("pw2_b", KT), ("mix_g0", KT), ("mix_b0", KT), ("mix_g1", KT), ("mix_b1", KT),
          ("fcw0", FT * FCONV_W), ("fcb0", FT), ("fcw1", FT * FCONV_W), ("fcb1", FT),
          ("ffn_g0", KT), ("ffn_b0", KT), ("ffn_g1", KT), ("ffn_b1", KT),
          ("ff1_pre", KT), ("ff1_post", KT), ("mix_pre", KT), ("mix_post", KT), ("ff2_pre", KT), ("ff2_post", KT),
          ("subln", 1), ("pe_k", PAIRS), ("pe_v", PAIRS), ("w2_k", 2 * DH), ("w2_v", 2 * DH),
          ("lams", 4 * DH)]
PCOL = {}
NPAR = 0
for _n, _k in PARAMS:
    PCOL[_n] = NPAR
    NPAR += _k

CONSTS = [("ident", P), ("mean", P), ("negtri", P), ("negone", P), ("perm", P), ("swap", P), ("maskS", P), ("maskC", P),
          ("eps", 2), ("cadd", QT * NC), ("cmul", QT * NC)]
CCOL = {}
NCON = 0
for _n, _k in CONSTS:
    CCOL[_n] = NCON
    NCON += _k

TILE_W = [512, 384, 256, 128]
TILE_BANK = [0, 1, 2, 1]
TILE_COL = [0, 0, 0, 384]
TILE_OFF = [0, 512, 1024, 896]
SCORE_COLS = 1280
BANKS3 = [(0, 0, 512), (1, 512, 512), (2, 1024, 256)]

ITEMS = [("copy", "kc", 0), ("copy", "vc", 0), ("rope", "ks", 0), ("turn", "vs", 0), ("rope", "kw", 0),
         ("turn", "vw", 0), ("gate", "gates", 0)]
for _h in range(DIFF_HEADS):
    ITEMS += [("rope", "dq", _h), ("rope", "dk", _h), ("turn", "dv", _h)]
ITEMS += [("rope", "nq", _j) for _j in range(4)]
USE = {}


def _use(*key):
    USE[key] = len(USE)


def _use_item(i):
    _use("item", i)
    if ITEMS[i][0] != "copy":
        _use("second", i)


for _i in range(7):
    _use_item(_i)
for _i in range(7, 10):
    _use_item(_i)
BESIDE = [list(range(10 + 3 * _h, 13 + 3 * _h)) if _h < 3 else [19, 20] for _h in range(DIFF_HEADS)]
for _h in range(DIFF_HEADS):
    for _i in BESIDE[_h]:
        _use_item(_i)
for _j in range(4):
    _use("cmp_scores", _j)
    if _j in (1, 2):
        _use_item(20 + _j)
    _use("cmp_turn", _j, 0)
    _use("cmp_turn", _j, 1)
ROPES = [i for i, it in enumerate(ITEMS) if it[0] == "rope"]
SECONDS = [k for k in USE if k[0] not in ("item",)]
LAMBDA_INIT = 0.2


def build_block(nc, ws, xT, pT, params, consts, rope, w1, out, stop=None):
    with ExitStack() as ctx:
        def sb(name, shape, dt=F32):
            return ctx.enter_context(nc.sbuf_tensor(name, shape, dt))

        def sem(name):
            return ctx.enter_context(nc.semaphore(name))

        raw = sb("raw", [P, RAW, 1024])
        wH = sb("wH", [P, 2, 1024], F32R)
        wL = sb("wL", [P, 2, 1024], F32R)
        xf = sb("xf", [P, KT, S])
        xH = sb("xH", [P, KT, S], F32R)
        xL = sb("xL", [P, KT, S], F32R)
        tmp = sb("tmp", [P, 10, S])
        rstd = sb("rstd", [P, S])
        par = sb("par", [P, NPAR])
        con = sb("con", [P, NCON])
        bcon = sb("bcon", [P, 3 * P], BF16)
        vturn0 = sb("vturn0", [P, S])
        st = sb("st", [P, 160])
        sq = [tmp[:, 8, :], tmp[:, 9, :]]

        def overlay(specs):
            with ExitStack() as sub:
                return [sub.enter_context(nc.sbuf_tensor(n, s, d)) for n, s, d in specs]

        hH, hL = overlay([("hH", [P, FT, S], F32R), ("hL", [P, FT, S], F32R)])
        cH, cL, gpad, diag = overlay([("cH", [P, KT, S], F32R), ("cL", [P, KT, S], F32R),
                                      ("gpad", [P, 2, CONV_W - 1 + S], F32),
                                      ("diag", [P, 2, PE_TAPS, P], F32)])
        (mH, mL, qT, kT, vT, vN, lg, sp, aT) = overlay([
            ("mH", [P, KT, S], F32R), ("mL", [P, KT, S], F32R), ("qT", [P, 2, S], F32), ("kT", [P, 2, S], F32),
            ("vT", [P, S], F32), ("vN", [P, 2, QT, P], F32),
            ("lg", [P, 2, SCORE_COLS], F32), ("sp", [P, 2, SCORE_COLS], F32), ("aT", [P, 2, SCORE_COLS], F32)])
        _, pf, pH, pL = overlay([("pgap", [P, 18944], F32), ("pf", [P, 2, S], F32), ("pH", [P, 2, S], F32R),
                                 ("pL", [P, 2, S], F32R)])

        common = [("ropeT", [P, 2, S], F32), ("ksT", [P, S], F32), ("kwT", [P, S], F32), ("vsN", [P, QT, P], F32),
                  ("vwN", [P, QT, P], F32), ("gN", [P, QT, 24], F32), ("kcC", [P, 32], F32), ("vcC", [P, P], F32)]
        (ropeT, ksT, kwT, vsN, vwN, gN, kcC, vcC, w1b, kcvc, blk_v, hid, hidT) = overlay(common + [
            ("w1b", [P, 2, PAIRS * CMP_HID], F32), ("kcvc", [P, 2, S], F32), ("blk_v", [P, PAIRS, 2, NC], F32),
            ("hid", [P, 2 * CMP_HID], F32), ("hidT", [P, 4, 2 * NC], F32)])
        (dqT, dkT, dvN, AT, pcT, pc_n, oN, nqT) = overlay(
            [(n + "_", s, d) for n, s, d in common] + [
                ("dqT", [P, 2, S], F32), ("dkT", [P, 2, S], F32), ("dvN", [P, 2, QT, P], F32), ("AT", [P, 2, SCORE_COLS], F32), ("pcT", [P, QT, P], F32), ("pc_n", [P, 2, QT, NC], F32),
                ("oN", [P, QT, D], F32), ("nqT", [P, 2, S], F32)])[8:]
        flat = tmp[:].rearrange("p a b -> p (a b)")
        prob = flat[:, 0:2 * SCORE_COLS].rearrange("p (m c) -> p m c", m=2)
        pre = flat[:, 2560:3584].rearrange("p (a b) -> p a b", a=2)
        rot = flat[:, 3584:4096]
        blk_k = flat[:, 4096:4096 + NC * CMP_BLOCK].rearrange("p (s g c) -> p s g c", s=PAIRS, g=2)

        ps = [ctx.enter_context(nc.psum_tensor(f"ps{i}", [P, 512], F32)) for i in range(8)]

        def pc(name, n=0, w=1):
            return par[:, bass.ds(PCOL[name] + n, w)]

        def cc(name, w=P):
            return con[:, CCOL[name]:CCOL[name] + w]

        identB, maskSB, maskCB = bcon[:, 0:P], bcon[:, P:2 * P], bcon[:, 2 * P:3 * P]

        in_loaded = sem("in_loaded")
        x_loaded = [sem(f"x_loaded{k}") for k in range(KT)]
        raw_loaded = [sem(f"raw_loaded{j}") for j in range(RAW)]
        high_ready = sem("high_ready")
        low_ready = sem("low_ready")
        chunk_done = sem("chunk_done")
        bank_done = sem("bank_done")
        const_ready = sem("const_ready")
        x_high = sem("x_high")
        x_ready = sem("x_ready")
        src_ready = sem("src_ready")
        mean_ready = sem("mean_ready")
        centered = sem("centered")
        squared = sem("squared")
        sumsq = sem("sumsq")
        log_ready = sem("log_ready")
        rstd_ready = sem("rstd_ready")
        normed = sem("normed")
        affine = sem("affine")
        glu_sig = sem("glu_sig")
        glu_pad = sem("glu_pad")
        glu_banks_free = sem("glu_banks_free")
        taps = sem("taps")
        diag_ready = sem("diag_ready")
        conv_done = sem("conv_done")
        conv_free = sem("conv_free")
        c_act = sem("c_act")
        c_ready = sem("c_ready")
        res_scaled = sem("res_scaled")
        p_loaded = sem("p_loaded")
        p_high = sem("p_high")
        p_ready = sem("p_ready")
        ple_sig = sem("ple_sig")
        ple_mul = sem("ple_mul")
        ple_free = sem("ple_free")
        tap2 = sem("tap2")
        tap10 = sem("tap10")
        gate_act = sem("gate_act")
        h_made = sem("h_made")
        h_high = sem("h_high")
        h_ready = sem("h_ready")
        q_free = sem("q_free")
        qkv_copied = sem("qkv_copied")
        z_ready = sem("z_ready")
        abs_ready = sem("abs_ready")
        e_ready = sem("e_ready")
        ln_ready = sem("ln_ready")
        sp_ready = sem("sp_ready")
        cum_ready = sem("cum_ready")
        a_ready = sem("a_ready")
        av_ready = sem("av_ready")
        vt_ready = sem("vt_ready")
        m_high = sem("m_high")
        m_ready = sem("m_ready")
        updated = sem("updated")
        w1_loaded = sem("w1_loaded")
        rope_loaded = sem("rope_loaded")
        b7_read = sem("b7_read")
        second_done = sem("second_done")
        roped = sem("roped")
        rot_ready = sem("rot_ready")
        blocks_ready = sem("blocks_ready")
        swapped = sem("swapped")
        hid_psum = sem("hid_psum")
        hid_ready = sem("hid_ready")
        lam_steps = sem("lam_steps")
        s_ready = sem("s_ready")
        max_ready = sem("max_ready")
        p_exp = sem("p_exp")
        coef_ready = sem("coef_ready")
        scaled = sem("scaled")
        p_ready2 = sem("p_ready2")
        turned = sem("turned")
        at_ready = sem("at_ready")
        at2_ready = sem("at2_ready")
        o_ready = sem("o_ready")
        o_copied = sem("o_copied")
        cmp_steps = sem("cmp_steps")
        cmp_sum = sem("cmp_sum")
        cmp_exp = sem("cmp_exp")
        cmp_ready = sem("cmp_ready")
        head_sq = sem("head_sq")
        head_std = sem("head_std")
        head_done = sem("head_done")
        o_turned = sem("o_turned")
        out_done = sem("out_done")

        block = ctx.enter_context(nc.Block())

        def fp(ap):
            return ap.bitcast(F32)

        @block.sync
        def _(sp_e):
            for c in range(2):
                sp_e.dma_start(raw[:, c, :], ws[c]).then_inc(raw_loaded[c], 16)
            for k in range(KT):
                sp_e.dma_start(xf[:, k, :], xT[k * P:k * P + P, :]).then_inc(x_loaded[k], 16)
            for c in range(2, RAW):
                sp_e.dma_start(raw[:, c, :], ws[c]).then_inc(raw_loaded[c], 16)

            def load(t, j):
                c = t * RAW + j
                sp_e.wait_ge(low_ready, c - RAW + 1)
                sp_e.dma_start(raw[:, j, :], ws[bass.ds(c, 1)].rearrange("o p n -> (o p) n"))\
                    .then_inc(raw_loaded[j], 16)

            with sp_e.Fori(1, NCHUNKS // RAW) as t:
                for j in range(RAW):
                    load(t, j)
            for j in range(NCHUNKS % RAW):
                load(NCHUNKS // RAW, j)
            for n in range(KT):
                sp_e.wait_ge(updated, 16 + n + 1)
                sp_e.dma_start(out[n * P:n * P + P, :], xf[:, n, :]).then_inc(out_done, 16)
            sp_e.wait_ge(out_done, 16 * KT)

        @block.gpsimd
        def _(pool):
            def split(t, j):
                pool.wait_ge(high_ready, t * RAW + (j + 1))
                pool.tensor_tensor(wL[:, j % 2, :], raw[:, j, :], fp(wH[:, j % 2, :]),
                                   ALU.subtract).then_inc(low_ready, 1)

            for j in range(RAW):
                split(0, j)
            with pool.Fori(1, NCHUNKS // RAW) as t:
                for j in range(RAW):
                    split(t, j)
            for j in range(NCHUNKS % RAW):
                split(NCHUNKS // RAW, j)

        NORM = {n: i for i, n in enumerate(["conf", "mix0", "ffn0", "mix1", "ffn1", "ff1_pre", "ff1_post",
                                            "mix_pre", "mix_post", "ff2_pre", "ff2_post"])}
        LNORM = ["conf", "mix0", "ffn0", "mix1", "ffn1"]
        FULL = {n: i for i, n in enumerate(["pw2", "down0", "wo", "down1", "down2", "wout", "down3"])}
        XV = {n: i for i, n in enumerate(["in", "mix0", "ffn0", "mix1", "ff1_pre", "mix_pre", "mixer",
                                          "ff2_pre"])}
        XH = {n: i for i, n in enumerate(["in", "mix0", "ffn0", "mix1", "ff1_pre", "mix_pre", "mixer", "ff2_pre"])}
        NUNITS = DIFF_HEADS + NSA_HEADS
        SRC = {n: i for i, n in enumerate(["conf", "mix0", "ffn0", "mix1", "ffn1", "ff1_post", "mix_post",
                                           "ff2_post"])}

        @block.tensor
        def _(pe):
            def three(bank, w, rh, rl, start, stop, c=None):
                slot, cols = w
                pe.matmul(bank, wH[:, slot, cols], rh, start=start, stop=False)
                pe.matmul(bank, wH[:, slot, cols], rl, start=False, stop=False)
                return pe.matmul(bank, wL[:, slot, cols], rh, start=False, stop=stop)

            def tile_product(bank, c, slot, rH=xH, rL=xL):
                pe.wait_ge(low_ready, c + 1)
                for k in range(KT):
                    mm = three(bank, (slot, slice(k * P, k * P + P)), rH[:, k, :], rL[:, k, :],
                               k == 0, k == KT - 1)
                mm.then_inc(chunk_done, 1)

            def first_pair(b0, b1, c, xname):
                pe.wait_ge(low_ready, c + 2)
                for k in range(KT):
                    pe.wait_ge(x_ready, 8 * XV[xname] + k + 1)
                    cols = slice(k * P, k * P + P)
                    for i, b in enumerate((b0, b1)):
                        mm = three(b, ((c + i) % 2, cols), xH[:, k, :], xL[:, k, :], k == 0, k == KT - 1)
                        if k == KT - 1:
                            mm.then_inc(chunk_done, 1)

            def full_product(name, nk, rH, rL, ready, ready_base, banks_free):
                c0 = CHUNK[name]

                def one_k(k, j, first=False, last=False):
                    pe.wait_ge(low_ready, c0 + k + 1)
                    pe.wait_ge(ready, ready_base + k + 1)
                    slot = (c0 + j) % 2
                    rh = rH[:, bass.ds(k, 1), :].rearrange("p o t -> p (o t)")
                    rl = rL[:, bass.ds(k, 1), :].rearrange("p o t -> p (o t)")
                    for n in range(8):
                        if first:
                            banks_free(n)
                        mm = three(ps[n][:], (slot, slice(n * P, n * P + P)), rh, rl, first, last)
                        if last and n < 7:
                            mm.then_inc(bank_done, 1)
                    mm.then_inc(chunk_done, 1)

                one_k(0, 0, first=True, last=nk == 1)
                if nk > 2:
                    one_k(1, 1)
                    if nk > 4:
                        with pe.Fori(1, nk // 2 - 1) as t:
                            for j in range(2):
                                one_k(t * 2 + j, j)
                    one_k(nk - 2, 0)
                one_k(nk - 1, 1, last=True)

            def mean_product(name, src):
                i = SRC[name]
                for n in range(KT):
                    pe.wait_ge(src_ready, 8 * i + n + 1)
                    mm = pe.matmul(ps[0][:], cc("mean"), src[:, n, :], start=n == 0, stop=n == KT - 1)
                mm.then_inc(mean_ready, 1)

            def sumsq_product(name, bank):
                i = NORM[name]
                if name.endswith("post"):
                    pe.wait_ge(src_ready, 8 * SRC[name] + 2)
                for n in range(KT):
                    pe.wait_ge(squared, 8 * i + n + 1)
                    pe.matmul(ps[bank][:], cc("mean"), sq[n % 2], start=n == 0, stop=n == KT - 1)\
                        .then_inc(sumsq, 1)

            def x_wait(name):
                pe.wait_ge(x_ready, 8 * XV[name] + 8)

            def ffn(inst, xname, ple_tiles=0):
                c0 = CHUNK[f"gateup{inst}"]

                def gate_and_up(f, j, c):
                    pe.wait_ge(h_made, f + (24 * inst + 1))
                    tile_product(ps[2 * j][:], c, c0 % 2)
                    tile_product(ps[2 * j + 1][:], c + 1, (c0 + 1) % 2)

                pe.wait_ge(h_made, 24 * inst + 1)
                if ple_tiles:
                    pe.wait_ge(ple_sig, ple_tiles - 2)
                first_pair(ps[0][:], ps[1][:], c0, xname)
                if ple_tiles:
                    pe.wait_ge(ple_sig, ple_tiles)
                gate_and_up(1, 1, c0 + 2)
                with pe.Fori(1, FT // 2) as t:
                    for j in range(2):
                        gate_and_up(t * 2 + j, j, t * 4 + (c0 + 2 * j))

                def banks_free(n):
                    if n == 0:
                        pe.wait_ge(h_made, 24 * inst + 24)
                full_product(f"down{inst}", FT, hH, hL, h_ready, FT * inst, banks_free)

            def ple(layer, xname):
                pe.wait_ge(p_ready, layer + 1)
                pe.wait_ge(rstd_ready, NORM[xname] + 1)
                c0 = CHUNK[f"ple{layer}"]
                first_pair(ps[0][:], ps[1][:], c0, xname)
                for i, (kind, n) in enumerate(PLE_ORDER[2:]):
                    c = c0 + 2 + i
                    if kind == "gate":
                        if n >= 4:
                            pe.wait_ge(ple_sig, KT * layer + n - 3)
                        tile_product(ps[n % 4][:], c, c % 2)
                        continue
                    pe.wait_ge(low_ready, c + 1)
                    if n:
                        pe.wait_ge(ple_mul, KT * layer + 4)
                    for m in range(4):
                        for k in range(2):
                            cols = slice((2 * m + k) * P, (2 * m + k) * P + P)
                            mm = three(ps[4 + m][:], (c % 2, cols), pH[:, k, :], pL[:, k, :], k == 0, k == 1)
                    mm.then_inc(chunk_done, 1)

            def glu_products(n, j):
                pe.wait_ge(glu_banks_free, n + 1)
                tile_product(ps[2 * j][:], n * 2, 0)
                tile_product(ps[2 * j + 1][:], n * 2 + 1, 1)

            def conv_taps(n, j):
                pe.wait_ge(glu_banks_free, n + 3)
                pe.wait_ge(diag_ready, n * PE_TAPS + PE_TAPS)
                pe.wait_ge(conv_free, n + 1)
                for tap in range(PE_TAPS):
                    mm = pe.matmul(ps[4 + j][:], diag[:, j, tap, :], gpad[:, j, tap:tap + S], start=tap == 0,
                                   stop=tap == PE_TAPS - 1)
                mm.then_inc(conv_done, 1)

            pe.sem_inc(conv_done, 2)
            first_pair(ps[0][:], ps[1][:], 0, "in")
            with pe.Fori(0, KT // 2 - 1) as t:
                glu_products(t * 2 + 1, 1)
                conv_taps(t * 2, 0)
                glu_products(t * 2 + 2, 0)
                conv_taps(t * 2 + 1, 1)
            glu_products(KT - 1, 1)
            conv_taps(KT - 2, 0)
            conv_taps(KT - 1, 1)
            mean_product("conf", tmp)
            sumsq_product("conf", 1)
            full_product("pw2", KT, cH, cL, c_ready, 0, lambda n: None)
            mean_product("mix0", xf)
            sumsq_product("mix0", 1)
            ple(0, "mix0")
            ffn(0, "mix0", KT)
            mean_product("ffn0", xf)
            sumsq_product("ffn0", 1)

            c0 = CHUNK["qkv"]

            def project(p, j, which):
                pe.wait_ge(q_free, p * 4 + (which + 1))
                tile_product(ps[7][:], p * 3 + (c0 + which), (c0 + 3 * j + which) % 2)

            def turn_values(p, j):
                pe.wait_ge(qkv_copied, p * 4 + 3)
                for kt in range(QT):
                    mm = pe.transpose(ps[7][:, kt * P:kt * P + P], vT[:, kt * P:kt * P + P], cc("ident"))
                mm.then_inc(vt_ready, 1)

            def scores(p, j, h):
                pe.wait_ge(qkv_copied, p * 4 + 2)
                r = slice(DH * h, DH * h + DH)
                for kt in range(QT):
                    b = ps[3 * h + TILE_BANK[kt]]
                    o = TILE_COL[kt]
                    pe.matmul(b[:, o:o + TILE_W[kt]], kT[r, j, kt * P:kt * P + P], qT[r, j, kt * P:S],
                              start=kt != 3, stop=False, skip_group_check=True)
                    mm = pe.matmul(b[:, o:o + P], identB, maskSB, start=False, stop=False, skip_group_check=True)
                mm.then_inc(z_ready, 1)

            def cumulate(p, h):
                pe.wait_ge(sp_ready, p * 6 + (3 * h + 3))
                for kt in range(QT):
                    b = ps[3 * h + TILE_BANK[kt]]
                    o = TILE_COL[kt]
                    for k2 in range(kt, QT):
                        m = pe.matmul(b[:, o + (k2 - kt) * P:o + TILE_W[kt]], cc("negtri" if k2 == kt else "negone"),
                                      sp[:, h, TILE_OFF[k2]:TILE_OFF[k2] + TILE_W[k2]],
                                      start=False, stop=False, skip_group_check=True)
                m.then_inc(cum_ready, 1)

            def values(p, j, h):
                pe.wait_ge(a_ready, p * 6 + (3 * h + 3))
                r = slice(DH * h, DH * h + DH)
                for kt in range(QT):
                    m = pe.matmul(ps[6][r, kt * P:S], vN[:, j, kt, r], aT[:, h, TILE_OFF[kt]:TILE_OFF[kt] + TILE_W[kt]],
                                  start=kt == 0, stop=kt == QT - 1, skip_group_check=True)
                m.then_inc(av_ready, 1)

            def pair(p, j, more, first=False):
                if not first:
                    pe.wait_ge(a_ready, p * 6)
                scores(p, j, 0)
                scores(p, j, 1)
                if more:
                    project(p + 1, 1 - j, 0)
                cumulate(p, 0)
                if more:
                    project(p + 1, 1 - j, 1)
                cumulate(p, 1)
                if more:
                    project(p + 1, 1 - j, 2)
                if not first:
                    pe.wait_ge(m_ready, p)
                pe.wait_ge(qkv_copied, p * 4 + 4)
                values(p, j, 0)
                values(p, j, 1)
                if more:
                    turn_values(p + 1, 1 - j)

            first_pair(ps[7][:], ps[6][:], c0, "ffn0")
            project(0, 0, 2)
            turn_values(0, 0)
            pair(0, 0, True, first=True)
            pair(1, 1, True)
            with pe.Fori(1, KT // 2 - 1) as t:
                pair(t * 2, 0, True)
                pair(t * 2 + 1, 1, True)
            pair(KT - 2, 0, True)
            pair(KT - 1, 1, False)
            pe.wait_ge(a_ready, 6 * KT)
            pe.wait_ge(qkv_copied, 4 * KT)

            def wo_free(n):
                if n == 6:
                    pe.wait_ge(m_ready, KT)
            full_product("wo", KT, mH, mL, m_ready, 0, wo_free)
            mean_product("mix1", xf)
            sumsq_product("mix1", 1)
            ple(1, "mix1")
            ffn(1, "mix1", 2 * KT)
            mean_product("ffn1", xf)
            sumsq_product("ffn1", 1)

            sumsq_product("ff1_pre", 2)
            ffn(2, "ff1_pre")
            sumsq_product("ff1_post", 1)
            sumsq_product("mix_pre", 2)

            c0 = CHUNK["hybrid"]
            q_of = {"dq": dqT, "nq": nqT}

            def project_item(i):
                pe.wait_ge(b7_read, USE["item", i])
                tile_product(ps[7][:], c0 + i, (c0 + i) % 2)

            def second_step(i):
                kind = ITEMS[i][0]
                pe.wait_ge(b7_read, USE["second", i])
                if kind == "rope":
                    mm = pe.matmul(ps[7][:], cc("perm"), pre[:, ROPES.index(i) % 2, :], start=True, stop=True)
                else:
                    for t in range(QT):
                        mm = pe.transpose(ps[7][:, t * P:t * P + P], vturn0[:, t * P:t * P + P], cc("ident"))
                mm.then_inc(second_done, 1)

            def item(i):
                project_item(i)
                second_step(i)

            first_pair(ps[7][:], ps[6][:], c0, "mix_pre")
            item(2)
            for i in range(2):
                pe.wait_ge(b7_read, USE["item", i] + 1)
                pe.matmul(ps[3 + i][:], cc("swap"), kcvc[:, i, :], start=True, stop=True).then_inc(swapped, 1)
            for i in range(3, 7):
                item(i)

            pe.wait_ge(blocks_ready, 2)
            pe.wait_ge(w1_loaded, 32)
            for kv, blk in ((0, blk_k), (1, blk_v)):
                for pair_ in range(PAIRS):
                    mm = pe.matmul(ps[5][0:2 * NC, kv * CMP_HID:(kv + 1) * CMP_HID],
                                   blk[:, pair_, :, :].rearrange("p g c -> p (g c)"),
                                   w1b[:, kv, pair_ * CMP_HID:(pair_ + 1) * CMP_HID], start=pair_ == 0,
                                   stop=pair_ == PAIRS - 1, skip_group_check=True)
            mm.then_inc(hid_psum, 1)

            def turn_hidden():
                pe.wait_ge(hid_ready, 1)
                for k in range(4):
                    mm = pe.transpose(ps[3][:, k * 2 * NC:(k + 1) * 2 * NC], hid[0:2 * NC, k * P:k * P + P],
                                      con[0:2 * NC, CCOL["ident"]:CCOL["ident"] + 2 * NC])
                mm.then_inc(hid_psum, 1)

            def second_layer():
                pe.wait_ge(hid_ready, 2)
                for g in range(2):
                    for m in range(2):
                        pe.matmul(ps[4][DH * g:DH * g + DH, 0:NC], pc("w2_k", DH * m, DH),
                                  hidT[:, m, g * NC:(g + 1) * NC], start=m == 0, stop=m == 1, skip_group_check=True)
                for g in range(2):
                    for m in range(2):
                        mm = pe.matmul(ps[5][0:NC, DH * g:DH * g + DH], hidT[:, 2 + m, g * NC:(g + 1) * NC],
                                       pc("w2_v", DH * m, DH), start=m == 0, stop=m == 1, skip_group_check=True)
                mm.then_inc(hid_psum, 1)

            def scores2(m, q, k, r):
                for t in range(QT):
                    qt = QT - 1 - t
                    b = ps[3 * (m % 2) + TILE_BANK[t]]
                    o = TILE_COL[t]
                    pe.matmul(b[:, o:o + TILE_W[t]], q[r, qt * P:qt * P + P], k[r, 0:TILE_W[t]],
                              start=t != 3, stop=False, skip_group_check=True)
                    mm = pe.matmul(b[:, o + qt * P:o + qt * P + P], identB, maskCB, start=False, stop=False,
                                   skip_group_check=True)
                mm.then_inc(s_ready, 1)

            def turn_map(m, src):
                for kt in range(QT):
                    b = ps[3 * (m % 2) + TILE_BANK[kt]]
                    for qt in range(kt, QT):
                        o = TILE_COL[kt] + (qt - kt) * P
                        f = TILE_OFF[QT - 1 - qt] + kt * P
                        mm = pe.transpose(b[:, o:o + P], prob[:, src, f:f + P], cc("ident"))
                mm.then_inc(turned, 1)

            def weigh(m, v, w, first):
                for qt in range(QT):
                    for kt in range(qt + 1):
                        f = TILE_OFF[kt] + (qt - kt) * P
                        mm = pe.matmul(ps[6][:, qt * w:qt * w + w], AT[:, m % 2, f:f + P], v[:, kt, :],
                                       start=first and qt == 0 and kt == 0, stop=False, skip_group_check=True)
                return mm

            item(7)
            turn_hidden()
            item(8)
            second_layer()
            item(9)
            pe.wait_ge(hid_ready, 4)
            def weigh_head(h):
                pe.wait_ge(at_ready, 3 * (h + 1))
                if h:
                    pe.wait_ge(o_copied, h)
                if h == DIFF_HEADS - 1:
                    pe.wait_ge(cmp_steps, 1)
                weigh(0, dvN[:, h % 2, :, :], P, True).then_inc(o_ready, 1)

            def compressed_scores(j):
                pe.wait_ge(roped, 10 + j + 1)
                pe.wait_ge(b7_read, USE["cmp_scores", j])
                pe.wait_ge(o_copied, DIFF_HEADS + 2 * j - 1)
                for g in range(2):
                    for qt in range(QT):
                        r = slice(DH * g, DH * g + DH)
                        mm = pe.matmul(ps[7 - g][:, qt * NC:qt * NC + NC], nqT[r, j % 2, qt * P:qt * P + P],
                                       kcC[r, 0:NC], start=qt == 0, stop=False, skip_group_check=True)
                mm.then_inc(second_done, 1)

            def weigh_branches(u):
                v = u - DIFF_HEADS
                j, g = v // 2, v % 2
                r = slice(DH * g, DH * g + DH)
                pe.wait_ge(o_copied, u)
                if g == 1 and j < 3:
                    pe.wait_ge(cmp_steps, 4 * (j + 1) + 1)
                pe.wait_ge(b7_read, USE["cmp_turn", j, g] + 1)
                for qt in range(QT):
                    pe.matmul(ps[6][:, qt * DH:qt * DH + DH], pcT[0:NC, qt, :], vcC[0:NC, r],
                              start=qt == 0, stop=False, skip_group_check=True)
                pe.wait_ge(at_ready, 3 * u + 3)
                weigh(0, vsN[:, :, r], DH, False)
                pe.wait_ge(at2_ready, 3 * v + 3)
                weigh(1, vwN[:, :, r], DH, False).then_inc(o_ready, 1)

            for h in range(DIFF_HEADS):
                j = h % 2
                beside = BESIDE[h]
                project_item(beside[0])
                pe.wait_ge(b7_read, USE["second", 9 + 3 * h] + 1)
                pe.wait_ge(roped, 2 + 2 * h + 2)
                if h:
                    pe.wait_ge(at_ready, 3 * h)
                scores2(2 * h, dqT[:, j, :], dkT[:, j, :], slice(0, DH))
                second_step(beside[0])
                if h:
                    pe.wait_ge(p_exp, 8 * h)
                scores2(2 * h + 1, dqT[:, j, :], dkT[:, j, :], slice(DH, P))
                project_item(beside[1])
                if h:
                    weigh_head(h - 1)
                second_step(beside[1])
                for i in beside[2:]:
                    project_item(i)
                pe.wait_ge(p_ready2, QT * (h + 1))
                turn_map(0, 0)
                for i in beside[2:]:
                    second_step(i)
            compressed_scores(0)

            for j in range(4):
                for g in range(2):
                    u = DIFF_HEADS + 2 * j + g
                    v = u - DIFF_HEADS
                    r = slice(DH * g, DH * g + DH)
                    pe.wait_ge(at_ready, 3 * u)
                    pe.wait_ge(p_exp, 8 * u)
                    scores2(0, nqT[:, j % 2, :], ksT, r)
                    if v:
                        pe.wait_ge(at2_ready, 3 * v)
                    scores2(1, nqT[:, j % 2, :], kwT, r)
                    if v:
                        weigh_branches(u - 1)
                    else:
                        weigh_head(DIFF_HEADS - 1)
                    if g == 0 and j in (1, 2):
                        item(20 + j)
                    pe.wait_ge(cmp_ready, j + 1)
                    pe.wait_ge(b7_read, USE["cmp_turn", j, g])
                    for qt in range(QT):
                        mm = pe.transpose(ps[7][0:NC, qt * P:qt * P + P], pc_n[:, g, qt, :], cc("ident"))
                    mm.then_inc(second_done, 1)
                    n0 = QT * DIFF_HEADS + 8 * v
                    pe.wait_ge(p_ready2, n0 + QT)
                    turn_map(0, 0)
                    pe.wait_ge(p_ready2, n0 + 2 * QT)
                    turn_map(1, 1)
                    if g == 1 and j < 3:
                        compressed_scores(j + 1)
            weigh_branches(NUNITS - 1)

            pe.wait_ge(o_copied, NUNITS)
            pe.wait_ge(head_done, QT * DIFF_HEADS)
            for n in range(KT):
                for qt in range(QT):
                    mm = pe.transpose(ps[n][:, qt * P:qt * P + P], oN[:, qt, n * P:n * P + P], cc("ident"))
                mm.then_inc(o_turned, 1)
            full_product("wout", KT, xH, xL, x_ready, 8 * XV["mixer"],
                         lambda n: pe.wait_ge(x_ready, 8 * XV["mixer"] + n + 1))
            sumsq_product("mix_post", 1)
            sumsq_product("ff2_pre", 2)
            ffn(3, "ff2_pre")
            sumsq_product("ff2_post", 1)

        @block.scalar
        def _(act):
            def load_p(layer):
                act.dma_start(pf[:], pT[layer].rearrange("(k p) t -> p k t", p=P)).then_inc(p_loaded, 16)

            act.dma_start(par[:], params).then_inc(in_loaded, 16)
            act.dma_start(con[:], consts).then_inc(in_loaded, 16)
            load_p(0)

            def high(c, t=0):
                act.wait_ge(raw_loaded[c % RAW], t * 16 + 16 * (c // RAW + 1))
                act.activation(wH[:, c % 2, :], raw[:, c % RAW, :], ACT.Copy).then_inc(high_ready, 1)

            def high_after(c, t=0):
                act.wait_ge(chunk_done, t * 4 + (c + 1))
                high(c + 2, t)

            def highs(name, upto=None):
                c0, n = CHUNK[name], upto or dict(COUNTS)[name]
                if n >= 8:
                    with act.Fori(0, n // 4) as t:
                        for j in range(4):
                            high_after(c0 + j, t)
                for j in range(n // 4 * 4 if n >= 8 else 0, n):
                    if c0 + j + 2 < NCHUNKS:
                        high_after(c0 + j)

            high(0)
            high(1)
            for n in range(KT):
                act.wait_ge(x_loaded[n], 16)
                act.activation(xH[:, n, :], xf[:, n, :], ACT.Copy).then_inc(x_high, 1)
            act.wait_ge(in_loaded, 32)
            act.activation(identB, cc("ident"), ACT.Copy).then_inc(const_ready, 1)
            act.activation(maskSB, cc("maskS"), ACT.Copy).then_inc(const_ready, 1)
            act.activation(maskCB, cc("maskC"), ACT.Copy).then_inc(const_ready, 1)
            for n, f in (("ff1_post", 0.5), ("ff2_post", 0.5), ("subln", 1.0 - LAMBDA_INIT)):
                w = dict(PARAMS)[n]
                act.activation(pc(n, 0, w), pc(n, 0, w), ACT.Copy, scale=f).then_inc(const_ready, 1)

            def squares(name, src, ready, base, step=1):
                i = NORM[name]
                for n in range(KT):
                    act.wait_ge(ready, base + step * (n + 1))
                    if 8 * i + n - 1 > 0:
                        act.wait_ge(sumsq, 8 * i + n - 1)
                    act.activation(sq[n % 2], src[:, n, :], ACT.Square).then_inc(squared, 1)

            def inverse_std(name, bank, eps):
                i = NORM[name]
                act.wait_ge(sumsq, 8 * i + 8)
                if i:
                    act.wait_ge(normed, 8 * i)
                act.activation(rstd[:], ps[bank][:], ACT.Ln, bias=cc("eps", 2)[:, eps:eps + 1]).then_inc(log_ready, 1)
                act.wait_ge(log_ready, i + 1)
                act.activation(rstd[:], rstd[:], ACT.Exp, scale=-0.5).then_inc(rstd_ready, 1)

            def layer_norm(name, src, g, b):
                li = LNORM.index(name)
                if name == "mix0":
                    p_parts(0)
                if name == "mix1":
                    p_parts(1)
                act.preload_act_table_set("natural_log_exp_and_others")
                squares(name, src, centered, 8 * li)
                inverse_std(name, 1, 0)
                if name == "conf":
                    act.preload_act_table(ACT.Silu)
                for n in range(KT + 2):
                    if name[:4] == "conf" or name == "ffn1":
                        if n >= KT:
                            continue
                    else:
                        if n < KT:
                            act.wait_ge(normed, 8 * NORM[name] + n + 1)
                            act.activation(xH[:, n, :], src[:, n, :], ACT.Identity, bias=pc(b, n)).then_inc(x_high, 1)
                        if n >= 2:
                            act.wait_ge(x_ready, 8 * XV[name] + n - 1)
                            act.activation(src[:, n - 2, :], src[:, n - 2, :], ACT.Identity, bias=pc(b, n - 2))\
                                .then_inc(affine, 2)
                        continue
                    act.wait_ge(normed, 8 * NORM[name] + n + 1)
                    if name == "conf":
                        act.activation(src[:, n, :], src[:, n, :], ACT.Silu, scale=pc(g, n), bias=pc(b, n))\
                            .then_inc(affine, 1)
                        act.wait_ge(affine, 2 * n + 1)
                        act.activation(cH[:, n, :], src[:, n, :], ACT.Copy).then_inc(affine, 1)
                    elif name == "ffn1":
                        act.activation(src[:, n, :], src[:, n, :], ACT.Identity, scale=pc(g, n), bias=pc(b, n))\
                            .then_inc(affine, 2)

            def ple(layer):
                c0 = CHUNK[f"ple{layer}"]
                act.preload_act_table(ACT.Sigmoid)
                for i, (kind, n) in enumerate(PLE_ORDER):
                    act.wait_ge(chunk_done, c0 + i + 1)
                    if kind == "gate":
                        if n >= 4:
                            act.wait_ge(ple_free, KT * layer + n - 3)
                        act.activation(tmp[:, n % 4, :], ps[n % 4][:], ACT.Sigmoid).then_inc(ple_sig, 1)
                    high_after(c0 + i)

            def p_parts(layer):
                act.wait_ge(p_loaded, 16 * layer + 16)
                for k in range(2):
                    act.activation(pH[:, k, :], pf[:, k, :], ACT.Copy).then_inc(p_high, 1)

            def ffn(inst):
                c0 = CHUNK[f"gateup{inst}"]
                act.preload_act_table(ACT.Silu)
                with act.Fori(0, FT // 2) as t:
                    for j in range(2):
                        f = t * 2 + j
                        high_after(c0 + 2 * j, t)
                        act.wait_ge(h_made, t * 2 + (24 * inst + j + 1))
                        if inst < 2:
                            act.activation(tmp[:, j, :], ps[2 * j][:], ACT.Identity,
                                           scale=pc(f"fcw{inst}", f * FCONV_W + 2), bias=pc(f"fcb{inst}", f))\
                                .then_inc(tap2, 1)
                            act.wait_ge(tap10, t * 4 + (2 * FT * inst + 2 * j + 2))
                            act.activation(tmp[:, j, :], tmp[:, j, :], ACT.Silu).then_inc(gate_act, 1)
                        else:
                            act.activation(tmp[:, j, :], ps[2 * j][:], ACT.Silu).then_inc(gate_act, 1)
                        high_after(c0 + 2 * j + 1, t)
                        act.wait_ge(h_made, t * 2 + (24 * inst + 2 + j + 1))
                        act.activation(hH[:, bass.ds(f, 1), :].rearrange("p o t -> p (o t)"), tmp[:, 2 + j, :],
                                       ACT.Copy).then_inc(h_high, 1)
                highs(f"down{inst}")

            act.preload_act_table(ACT.Sigmoid)
            with act.Fori(0, KT // 2) as t:
                for j in range(2):
                    act.wait_ge(conv_done, t * 2 + (j + 1))
                    for tap in range(PE_TAPS):
                        act.activation(diag[:, j, tap, :], cc("ident"), ACT.Copy,
                                       scale=pc("dw_w", t * (2 * CONV_W) + (CONV_W * j + tap))).then_inc(diag_ready, 1)
                    high_after(2 * j, t)
                    act.wait_ge(glu_banks_free, t * 2 + (j + 1))
                    act.activation(sq[j], ps[2 * j][:], ACT.Sigmoid, bias=pc("pw1_bg", t * 2 + j)).then_inc(glu_sig, 1)
                    high_after(2 * j + 1, t)
            layer_norm("conf", tmp, "aln_g", "aln_b")
            highs("pw2")
            layer_norm("mix0", xf, "mix_g0", "mix_b0")
            ple(0)
            ffn(0)
            layer_norm("ffn0", xf, "ffn_g0", "ffn_b0")

            def copy_qkv(p, j, which):
                act.wait_ge(chunk_done, CHUNK["qkv"] + 3 * p + which + 1)
                b = 6 if p == 0 and which == 1 else 7
                if which == 0:
                    act.activation(qT[:, j, :], ps[7][:], ACT.Copy, scale=DH ** -0.5).then_inc(qkv_copied, 1)
                elif which == 1:
                    act.activation(kT[:, j, :], ps[b][:], ACT.Copy).then_inc(qkv_copied, 1)
                else:
                    act.activation(vT[:], ps[7][:], ACT.Copy).then_inc(qkv_copied, 1)
                high_after(CHUNK["qkv"] + 3 * p + which)
                act.wait_ge(qkv_copied, p * 4 + (which + 1))
                act.sem_inc(q_free, 1)

            def copy_values(p, j):
                act.wait_ge(vt_ready, p + 1)
                act.activation(vN[:, j, :, :].rearrange("p a b -> p (a b)"), ps[7][:], ACT.Copy).then_inc(qkv_copied, 1)
                act.wait_ge(qkv_copied, p * 4 + 4)
                act.sem_inc(q_free, 1)

            def softplus_log(p, h, first):
                act.wait_ge(z_ready, p * 2 + (h + 1))
                if not first:
                    act.wait_ge(sp_ready, p * 6 + (3 * h - 3))
                for b, off, w in BANKS3:
                    act.activation(lg[:, h, off:off + w], ps[3 * h + b][:, 0:w], ACT.Abs).then_inc(abs_ready, 1)
                act.wait_ge(abs_ready, p * 6 + (3 * h + 3))
                act.activation(lg[:, h, :], lg[:, h, :], ACT.Exp, scale=-1.0).then_inc(e_ready, 1)
                act.wait_ge(e_ready, p * 2 + (h + 1))
                act.activation(lg[:, h, :], lg[:, h, :], ACT.Ln, bias=1.0).then_inc(ln_ready, 1)

            def probabilities(p, h, first):
                act.wait_ge(cum_ready, p * 2 + (h + 1))
                if not first:
                    act.wait_ge(av_ready, p * 2 + (h - 1))
                for b, off, w in BANKS3:
                    act.activation(aT[:, h, off:off + w], ps[3 * h + b][:, 0:w], ACT.Exp).then_inc(a_ready, 1)

            def pair(p, j, more, first=False):
                softplus_log(p, 0, first)
                softplus_log(p, 1, first)
                if more:
                    copy_qkv(p + 1, 1 - j, 0)
                probabilities(p, 0, first)
                if more:
                    copy_qkv(p + 1, 1 - j, 1)
                probabilities(p, 1, first)
                if more:
                    copy_qkv(p + 1, 1 - j, 2)
                act.wait_ge(av_ready, p * 2 + 2)
                act.activation(mH[:, bass.ds(p, 1), :].rearrange("p o t -> p (o t)"), ps[6][:], ACT.Copy)\
                    .then_inc(m_high, 1)
                if more:
                    copy_values(p + 1, 1 - j)

            act.sem_inc(q_free, 1)
            for which in range(3):
                copy_qkv(0, 0, which)
            copy_values(0, 0)
            for p in range(KT):
                pair(p, p % 2, p < KT - 1, first=p == 0)

            highs("wo")
            act.wait_ge(m_ready, KT)
            load_p(1)
            layer_norm("mix1", xf, "mix_g1", "mix_b1")
            ple(1)
            ffn(1)
            layer_norm("ffn1", xf, "ffn_g1", "ffn_b1")

            def pre_norm(name, ready, base, step=1):
                act.preload_act_table_set("natural_log_exp_and_others")
                squares(name, xf, ready, base, step)
                inverse_std(name, 2, 1)
                for n in range(KT):
                    act.wait_ge(normed, 8 * NORM[name] + n + 1)
                    act.activation(xH[:, n, :], tmp[:, n, :], ACT.Copy, scale=pc(name, n)).then_inc(x_high, 1)

            def post_norm(name):
                act.preload_act_table_set("natural_log_exp_and_others")
                squares(name, tmp, src_ready, 8 * SRC[name])
                inverse_std(name, 1, 1)

            pre_norm("ff1_pre", affine, 64, 2)
            ffn(2)
            act.wait_ge(chunk_done, CHUNK["down2"] + FT)
            act.dma_start(ropeT[:].rearrange("p a t -> p (a t)"), rope).then_inc(rope_loaded, 16)
            for kv in range(2):
                act.dma_start(w1b[:, kv, :], w1[kv]).then_inc(w1_loaded, 16)
            post_norm("ff1_post")
            pre_norm("mix_pre", updated, 0)

            c0 = CHUNK["hybrid"]

            def take_item(i):
                kind, name, h = ITEMS[i]
                act.wait_ge(chunk_done, c0 + i + 1)
                if kind == "copy":
                    act.activation(kcvc[:, i, :], ps[7 - i][:], ACT.Copy).then_inc(b7_read, 1)
                elif kind == "rope":
                    r = ROPES.index(i)
                    if r >= 2:
                        act.wait_ge(roped, r - 1)
                    act.activation(pre[:, r % 2, :], ps[7][:], ACT.Copy,
                                   scale=DH ** -0.5 if name in ("dq", "nq") else 1.0).then_inc(b7_read, 1)
                else:
                    act.activation(vturn0[:], ps[7][:], ACT.Sigmoid if kind == "gate" else ACT.Copy)\
                        .then_inc(b7_read, 1)
                high_after(c0 + i)

            def take_second(i):
                kind, name, h = ITEMS[i]
                if kind in ("turn", "gate"):
                    act.wait_ge(second_done, SECONDS.index(("second", i)) + 1)
                    if kind == "gate":
                        act.activation(gN[:], ps[7][:].rearrange("p (q g) -> p q g", q=QT)[:, :, 0:24], ACT.Copy)\
                            .then_inc(b7_read, 1)
                    else:
                        dst = {"vs": vsN[:], "vw": vwN[:], "dv": dvN[:, h % 2, :, :]}[name]
                        act.activation(dst, ps[7][:].rearrange("p (q g) -> p q g", q=QT), ACT.Copy)\
                            .then_inc(b7_read, 1)

            def item(i):
                take_item(i)
                take_second(i)

            for i in range(7):
                item(i)
            act.wait_ge(lam_steps, 2)
            act.activation(st[:, 130:132], st[:, 128:130], ACT.Exp).then_inc(lam_steps, 1)
            act.wait_ge(hid_psum, 1)
            act.activation(hid[0:2 * NC, :], ps[5][0:2 * NC, :], ACT.Gelu_apprx_tanh).then_inc(hid_ready, 1)
            item(7)
            act.wait_ge(hid_psum, 2)
            act.activation(hidT[:].rearrange("p k c -> p (k c)"), ps[3][:, 0:8 * NC], ACT.Copy).then_inc(hid_ready, 1)
            item(8)
            act.wait_ge(hid_psum, 3)
            act.activation(vcC[0:NC, :], ps[5][0:NC, 0:P], ACT.Copy).then_inc(hid_ready, 1)
            act.activation(kcC[:, 0:NC], ps[4][:, 0:NC], ACT.Copy).then_inc(hid_ready, 1)
            item(9)

            def exps(u, m):
                act.wait_ge(max_ready, 8 * u + 4 * m + 4)
                for t in range(QT):
                    qt = QT - 1 - t
                    o, f = TILE_COL[t], TILE_OFF[t]
                    act.activation(prob[:, m, f:f + TILE_W[t]], ps[3 * m + TILE_BANK[t]][:, o:o + TILE_W[t]], ACT.Exp,
                                   bias=st[:, 4 * m + qt:4 * m + qt + 1],
                                   accum_out=st[:, 8 + 4 * m + qt:9 + 4 * m + qt]).then_inc(p_exp, 1)

            def copy_turned(m, n):
                act.wait_ge(turned, n)
                for b, off, w in BANKS3:
                    act.activation(AT[:, m, off:off + w], ps[3 * m + b][:, 0:w], ACT.Copy).then_inc(at_ready, 1)

            def copy_output(u):
                act.wait_ge(o_ready, u + 1)
                if u < DIFF_HEADS:
                    act.activation(oN[:, :, u * P:u * P + P], ps[6][:].rearrange("p (q d) -> p q d", q=QT), ACT.Copy)\
                        .then_inc(o_copied, 1)
                else:
                    c = DIFF_HEADS * P + (u - DIFF_HEADS) * DH
                    act.activation(oN[:, :, c:c + DH], ps[6][:, 0:QT * DH].rearrange("p (q d) -> p q d", q=QT),
                                   ACT.Copy).then_inc(o_copied, 1)

            for h in range(DIFF_HEADS):
                beside = BESIDE[h]
                take_item(beside[0])
                if h:
                    act.wait_ge(turned, h)
                exps(h, 0)
                exps(h, 1)
                take_item(beside[1])
                if h:
                    copy_output(h - 1)
                for i in beside[2:]:
                    take_item(i)
                copy_turned(0, h + 1)
                for i in beside[2:]:
                    take_second(i)
            for j in range(4):
                act.wait_ge(cmp_steps, 4 * j + 3)
                act.activation(pc_n[:], pc_n[:], ACT.Exp).then_inc(cmp_exp, 1)
                for g in range(2):
                    u = DIFF_HEADS + 2 * j + g
                    v = u - DIFF_HEADS
                    act.wait_ge(turned, DIFF_HEADS + 2 * v)
                    exps(u, 0)
                    exps(u, 1)
                    copy_output(u - 1)
                    if g == 0 and j in (1, 2):
                        item(20 + j)
                    act.wait_ge(second_done, SECONDS.index(("cmp_turn", j, g)) + 1)
                    act.activation(pcT[0:NC, :, :].rearrange("p q d -> p (q d)"), ps[7][0:NC, :], ACT.Copy)\
                        .then_inc(b7_read, 1)
                    copy_turned(0, DIFF_HEADS + 2 * v + 1)
            copy_output(NUNITS - 1)
            act.wait_ge(head_sq, 2)
            act.activation(st[:, 48:64], st[:, 32:48], ACT.Sqrt, scale=1.0 / P, bias=cc("eps", 2)[:, 1:2])\
                .then_inc(head_std, 1)
            for n in range(KT):
                act.wait_ge(o_turned, n + 1)
                act.activation(xH[:, n, :], ps[n][:], ACT.Copy, scale=pc("subln") if n < DIFF_HEADS else 1.0)\
                    .then_inc(x_high, 1)
            highs("wout")
            post_norm("mix_post")
            pre_norm("ff2_pre", updated, 8)
            ffn(3)
            post_norm("ff2_post")

        @block.vector
        def _(dve):
            def low_part(n):
                dve.tensor_tensor(xL[:, n, :], xf[:, n, :], fp(xH[:, n, :]), ALU.subtract).then_inc(x_ready, 1)

            dve.memset(gpad[:, :, 0:CONV_W - 1], 0.0).then_inc(glu_pad, 1)
            dve.wait_ge(in_loaded, 32)
            for n in range(KT):
                dve.wait_ge(x_high, n + 1)
                low_part(n)
            dve.sem_inc(glu_banks_free, 2)

            def take_banks(name, fn):
                for n in range(KT):
                    if n < 7:
                        dve.wait_ge(bank_done, 7 * FULL[name] + n + 1)
                    else:
                        dve.wait_ge(chunk_done, CHUNK[name] + dict(COUNTS)[name])
                    fn(n)

            def add_residual(n):
                dve.tensor_tensor(xf[:, n, :], ps[n][:], xf[:, n, :], ALU.add).then_inc(src_ready, 1)

            def normalise(name, dst, src, finish, lag=1, g=None):
                dve.wait_ge(rstd_ready, NORM[name] + 1)
                for n in range(KT + lag):
                    if n < KT and g:
                        dve.scalar_tensor_tensor(dst[:, n, :], src[:, n, :], pc(g, n), rstd[:], ALU.mult,
                                                 ALU.mult).then_inc(normed, 1)
                    elif n < KT:
                        dve.tensor_tensor(dst[:, n, :], src[:, n, :], rstd[:], ALU.mult).then_inc(normed, 1)
                    if n >= lag:
                        finish(n - lag)

            def layer_norm(name, src, g=None, b=None):
                if name != "conf":
                    g, b = f"{name[:3]}_g{name[3]}", f"{name[:3]}_b{name[3]}"
                li = LNORM.index(name)
                dve.wait_ge(mean_ready, li + 1)
                for n in range(KT):
                    dve.tensor_tensor(src[:, n, :], src[:, n, :], ps[0][:], ALU.subtract).then_inc(centered, 1)

                def finish(n):
                    if name == "ffn1":
                        return
                    if name == "conf":
                        dve.wait_ge(affine, 2 * n + 2)
                        dve.tensor_tensor(cL[:, n, :], src[:, n, :], fp(cH[:, n, :]), ALU.subtract).then_inc(c_ready, 1)
                    else:
                        dve.wait_ge(x_high, 8 * XH[name] + n + 1)
                        dve.scalar_tensor_tensor(xL[:, n, :], src[:, n, :], pc(b, n), fp(xH[:, n, :]), ALU.add,
                                                 ALU.subtract).then_inc(x_ready, 1)
                normalise(name, src, src, finish, 2, g if name not in ("conf", "ffn1") else None)

            def ple(layer):
                for k in range(2):
                    dve.wait_ge(p_high, 2 * layer + k + 1)
                    i = dve.tensor_tensor(pL[:, k, :], pf[:, k, :], fp(pH[:, k, :]), ALU.subtract)
                    if k == 1:
                        i.then_inc(p_ready, 1)

            def ple_tiles(layer):
                for n in range(KT):
                    dve.wait_ge(ple_sig, KT * layer + n + 1)
                    dve.wait_ge(chunk_done, CHUNK[f"ple{layer}"] + PLE_ORDER.index(("proj", n // 4)) + 1)
                    g_n = tmp[:, n % 4, :]
                    dve.tensor_tensor(g_n, ps[4 + n % 4][:], g_n, ALU.mult).then_inc(ple_mul, 1)
                    if n == 0:
                        dve.wait_ge(affine, 16 * LNORM.index(f"mix{layer}") + 16)
                    dve.wait_ge(ple_mul, KT * layer + n + 1)
                    dve.scalar_tensor_tensor(xf[:, n, :], xf[:, n, :], ALPHA, g_n, ALU.mult, ALU.add)\
                        .then_inc(ple_free, 1)
                dve.wait_ge(ple_free, KT * layer + KT)

            def ffn(inst):
                c0 = CHUNK[f"gateup{inst}"]
                dve.sem_inc(h_made, 2)
                with dve.Fori(0, FT // 2) as t:
                    for j in range(2):
                        f = t * 2 + j
                        if inst < 2:
                            dve.wait_ge(tap2, t * 2 + (FT * inst + j + 1))
                            for tap in (1, 0):
                                back = FCONV_W - 1 - tap
                                dve.scalar_tensor_tensor(tmp[:, j, back:S], ps[2 * j][:, 0:S - back],
                                                         pc(f"fcw{inst}", f * FCONV_W + tap), tmp[:, j, back:S],
                                                         ALU.mult, ALU.add).then_inc(tap10, 1)
                                if tap == 1:
                                    dve.wait_ge(tap10, t * 4 + (2 * FT * inst + 2 * j + 1))
                        dve.wait_ge(gate_act, t * 2 + (FT * inst + j + 1))
                        dve.wait_ge(chunk_done, t * 4 + (c0 + 2 * j + 2))
                        dve.tensor_tensor(tmp[:, 2 + j, :], ps[2 * j + 1][:], tmp[:, j, :], ALU.mult).then_inc(h_made, 1)
                        dve.wait_ge(h_high, t * 2 + (FT * inst + j + 1))
                        dve.tensor_tensor(hL[:, bass.ds(f, 1), :].rearrange("p o t -> p (o t)"), tmp[:, 2 + j, :],
                                          fp(hH[:, bass.ds(f, 1), :].rearrange("p o t -> p (o t)")), ALU.subtract)\
                            .then_inc(h_ready, 1)

            dve.wait_ge(glu_pad, 1)
            dve.sem_inc(conv_free, 2)
            with dve.Fori(0, KT // 2) as t:
                for j in range(2):
                    n = t * 2 + j
                    conv = tmp[:, bass.ds(n, 1), :].rearrange("p o t -> p (o t)")
                    dve.wait_ge(glu_sig, t * 2 + (j + 1))
                    dve.wait_ge(chunk_done, t * 4 + (2 * j + 2))
                    dve.scalar_tensor_tensor(gpad[:, j, CONV_W - 1:], ps[2 * j + 1][:], pc("pw1_ba", n), sq[j],
                                             ALU.add, ALU.mult).then_inc(glu_banks_free, 1)
                    dve.wait_ge(glu_banks_free, t * 2 + (j + 3))
                    for tap in range(PE_TAPS, CONV_W):
                        i = tap - PE_TAPS
                        w = pc("dw_w", n * CONV_W + tap)
                        dst = (conv, rstd[:])[i % 2]
                        if i >= 2:
                            dve.wait_ge(taps, t * (2 * DVE_STEPS) + (DVE_STEPS * j + i - 1))
                        elif i == 1:
                            dve.wait_ge(taps, t * (2 * DVE_STEPS) + (DVE_STEPS * j + 1))
                        if i == 0:
                            ins = dve.tensor_scalar(dst, gpad[:, j, tap:tap + S], w, pc("dw_b", n), ALU.mult, ALU.add)
                        elif i == 1:
                            ins = dve.tensor_scalar(dst, gpad[:, j, tap:tap + S], w, None, ALU.mult)
                        else:
                            ins = dve.scalar_tensor_tensor(dst, gpad[:, j, tap:tap + S], w, dst, ALU.mult, ALU.add)
                        ins.then_inc(taps, 1)
                    dve.wait_ge(taps, t * (2 * DVE_STEPS) + (DVE_STEPS * j + DVE_STEPS - 1))
                    dve.tensor_tensor(conv, conv, rstd[:], ALU.add).then_inc(taps, 1)
                    dve.wait_ge(taps, t * (2 * DVE_STEPS) + (DVE_STEPS * j + DVE_STEPS))
                    dve.wait_ge(conv_done, n + 3)
                    dve.tensor_tensor(conv, conv, ps[4 + j][:], ALU.add).then_inc(conv_free, 1)
                    dve.wait_ge(conv_free, n + 3)
                    dve.sem_inc(src_ready, 1)
            layer_norm("conf", tmp)
            for n in range(KT):
                dve.tensor_scalar(xf[:, n, :], xf[:, n, :], ALPHA, pc("pw2_b", n), ALU.mult, ALU.add).then_inc(res_scaled, 1)
            dve.wait_ge(res_scaled, KT)
            take_banks("pw2", add_residual)
            ple(0)
            layer_norm("mix0", xf)
            ple_tiles(0)
            ffn(0)
            take_banks("down0", add_residual)
            layer_norm("ffn0", xf)

            dve.wait_ge(affine, 16 * LNORM.index("ffn0") + 16)
            for n in range(KT):
                dve.tensor_scalar(xf[:, n, :], xf[:, n, :], ALPHA, None, ALU.mult).then_inc(res_scaled, 1)

            def softplus(p, h):
                dve.wait_ge(ln_ready, p * 2 + (h + 1))
                for b, off, w in BANKS3:
                    dve.scalar_tensor_tensor(sp[:, h, off:off + w], ps[3 * h + b][:, 0:w], 0.0, lg[:, h, off:off + w],
                                             ALU.max, ALU.add).then_inc(sp_ready, 1)

            def pair(p):
                softplus(p, 0)
                softplus(p, 1)
                dve.wait_ge(m_high, p + 1)
                m = bass.ds(p, 1)
                dve.tensor_tensor(mL[:, m, :].rearrange("p o t -> p (o t)"), ps[6][:],
                                  fp(mH[:, m, :].rearrange("p o t -> p (o t)")), ALU.subtract).then_inc(m_ready, 1)

            with dve.Fori(0, KT) as p:
                pair(p)
            dve.wait_ge(res_scaled, 2 * KT)
            take_banks("wo", add_residual)
            ple(1)
            layer_norm("mix1", xf)
            ple_tiles(1)
            ffn(1)
            take_banks("down1", add_residual)
            layer_norm("ffn1", xf)

            def copy_product(n):
                dve.tensor_copy(tmp[:, n, :], ps[n][:]).then_inc(src_ready, 1)

            def pre_norm(name):
                def finish(n):
                    dve.wait_ge(x_high, 8 * XH[name] + n + 1)
                    dve.scalar_tensor_tensor(xL[:, n, :], tmp[:, n, :], pc(name, n), fp(xH[:, n, :]), ALU.mult,
                                             ALU.subtract).then_inc(x_ready, 1)
                normalise(name, tmp, xf, finish, 2)

            def post_norm(name):
                def finish(n):
                    dve.wait_ge(normed, 8 * NORM[name] + n + 1)
                    dve.scalar_tensor_tensor(xf[:, n, :], tmp[:, n, :], pc(name, n), xf[:, n, :], ALU.mult, ALU.add)\
                        .then_inc(updated, 1)
                normalise(name, tmp, tmp, finish, 1)

            dve.wait_ge(affine, 80)
            pre_norm("ff1_pre")
            ffn(2)
            take_banks("down2", copy_product)
            post_norm("ff1_post")
            dve.wait_ge(updated, 8)
            pre_norm("mix_pre")

            lam = pc("lams", 0, 4 * DH).rearrange("p (a b d) -> p a b d", a=2, b=2)
            dve.tensor_tensor(st[:, 0:2 * DH].rearrange("p (a d) -> p a d", a=2), lam[:, :, 0, :], lam[:, :, 1, :],
                              ALU.mult).then_inc(lam_steps, 1)
            dve.wait_ge(lam_steps, 1)
            dve.tensor_reduce(st[:, 128:130], st[:, 0:2 * DH].rearrange("p (a d) -> p a d", a=2), AX_X, ALU.add)\
                .then_inc(lam_steps, 1)

            def item(i):
                kind, name, h = ITEMS[i]
                if kind == "copy":
                    dve.wait_ge(swapped, i + 1)
                    blk = (blk_k, blk_v)[i]
                    for odd in range(2):
                        r = slice(DH * odd, DH * odd + DH)
                        for g in range(2):
                            src = kcvc[r, i, :] if g == odd else ps[3 + i][r, :]
                            src = src.rearrange("p (c s two) -> p s c two", s=8, two=2)
                            for half in range(2):
                                pe_ = par[r, PCOL[("pe_k", "pe_v")[i]] + 8 * half:][:, 0:8]\
                                    .unsqueeze(2).broadcast_to([DH, 8, NC])
                                ins = dve.tensor_tensor(blk[r, 8 * half:8 * half + 8, g, :],
                                                        src[:, :, half:half + NC, odd], pe_, ALU.add)
                    ins.then_inc(blocks_ready, 1)
                elif kind == "rope":
                    r = ROPES.index(i)
                    dst = {"ks": ksT[:], "kw": kwT[:], "dq": dqT[:, h % 2, :], "dk": dkT[:, h % 2, :],
                           "nq": nqT[:, h % 2, :]}[name]
                    if r == 0:
                        dve.wait_ge(rope_loaded, 16)
                    else:
                        dve.wait_ge(roped, r)
                    dve.wait_ge(second_done, SECONDS.index(("second", i)) + 1)
                    dve.tensor_tensor(rot, ps[7][:], ropeT[:, 1, :], ALU.mult).then_inc(b7_read, 1)
                    dve.tensor_tensor(pre[:, r % 2, :], pre[:, r % 2, :], ropeT[:, 0, :], ALU.mult)\
                        .then_inc(rot_ready, 1)
                    dve.wait_ge(rot_ready, r + 1)
                    dve.wait_ge(b7_read, USE["second", i] + 1)
                    dve.tensor_tensor(dst, pre[:, r % 2, :], rot, ALU.add).then_inc(roped, 1)

            for i in (2, 0, 1, 3, 4, 5, 6):
                item(i)
            dve.wait_ge(lam_steps, 3)
            dve.scalar_tensor_tensor(st[:, 132:133], st[:, 131:132], -LAMBDA_INIT, st[:, 130:131], ALU.add,
                                     ALU.subtract).then_inc(lam_steps, 1)
            for i in range(7, 10):
                item(i)

            def maxima(u, m):
                dve.wait_ge(s_ready, 2 * u + m + 1)
                for t in range(QT):
                    qt = QT - 1 - t
                    o = TILE_COL[t]
                    dve.tensor_reduce(st[:, 4 * m + qt:4 * m + qt + 1], ps[3 * m + TILE_BANK[t]][:, o:o + TILE_W[t]],
                                      AX_X, ALU.max, negate=True).then_inc(max_ready, 1)

            for h in range(DIFF_HEADS):
                item(BESIDE[h][0])
                if h:
                    dve.wait_ge(p_exp, 8 * h)
                maxima(h, 0)
                maxima(h, 1)
                item(BESIDE[h][1])
                dve.wait_ge(p_exp, 8 * h + 8)
                if h:
                    dve.wait_ge(p_ready2, QT * h)
                dve.reciprocal(st[:, 16:24], st[:, 8:16]).then_inc(coef_ready, 1)
                if h == 0:
                    dve.wait_ge(lam_steps, 4)
                dve.wait_ge(coef_ready, 2 * h + 1)
                dve.tensor_scalar(st[:, 24:28], st[:, 20:24], st[:, 132:133], None, ALU.mult).then_inc(coef_ready, 1)
                dve.wait_ge(coef_ready, 2 * h + 2)
                for t in range(QT):
                    qt = QT - 1 - t
                    f = slice(TILE_OFF[t], TILE_OFF[t] + TILE_W[t])
                    dve.tensor_scalar(prob[:, 1, f], prob[:, 1, f], st[:, 24 + qt:25 + qt], None, ALU.mult)\
                        .then_inc(scaled, 1)
                for t in range(QT):
                    qt = QT - 1 - t
                    f = slice(TILE_OFF[t], TILE_OFF[t] + TILE_W[t])
                    dve.wait_ge(scaled, QT * h + t + 1)
                    dve.scalar_tensor_tensor(prob[:, 0, f], prob[:, 0, f], st[:, 16 + qt:17 + qt], prob[:, 1, f],
                                             ALU.mult, ALU.add).then_inc(p_ready2, 1)
                for i in BESIDE[h][2:]:
                    item(i)
            def compressed_maxima(j):
                dve.wait_ge(second_done, SECONDS.index(("cmp_scores", j)) + 1)
                cadd = cc("cadd", QT * NC).rearrange("p (q c) -> p q c", q=QT)
                base = 4 * j
                for g in range(2):
                    i = dve.tensor_tensor(pc_n[:, g, :, :], ps[7 - g][:, 0:QT * NC]
                                          .rearrange("p (q c) -> p q c", q=QT), cadd, ALU.add)
                    i.then_inc(b7_read if g == 0 else cmp_steps, 1)
                dve.wait_ge(b7_read, USE["cmp_scores", j] + 1)
                dve.wait_ge(cmp_steps, base + 1)
                flatc = pc_n[:].rearrange("p g q c -> p (g q) c")
                dve.tensor_reduce(st[:, 64:72], flatc, AX_X, ALU.max).then_inc(cmp_steps, 1)
                dve.wait_ge(cmp_steps, base + 2)
                dve.tensor_tensor(flatc, flatc, st[:, 64:72].unsqueeze(2).broadcast_to([P, 8, NC]), ALU.subtract)\
                    .then_inc(cmp_steps, 1)

            def compressed_weights(j):
                cmul = cc("cmul", QT * NC).rearrange("p (q c) -> p q c", q=QT)
                flatc = pc_n[:].rearrange("p g q c -> p (g q) c")
                dve.wait_ge(cmp_exp, j + 1)
                dve.tensor_reduce(st[:, 72:80], flatc, AX_X, ALU.add).then_inc(cmp_sum, 1)
                dve.wait_ge(cmp_sum, 3 * j + 1)
                dve.reciprocal(st[:, 80:88], st[:, 72:80]).then_inc(cmp_sum, 1)
                dve.wait_ge(cmp_sum, 3 * j + 2)
                for g in range(2):
                    gate = gN[:, :, 3 * (4 * g + j)]
                    i = dve.tensor_tensor(st[:, 88 + 4 * g:92 + 4 * g], gate, st[:, 80 + 4 * g:84 + 4 * g], ALU.mult)
                    if g == 1:
                        i.then_inc(cmp_sum, 1)
                dve.wait_ge(cmp_sum, 3 * j + 3)
                for g in range(2):
                    i = dve.tensor_tensor(pc_n[:, g, :, :], pc_n[:, g, :, :], cmul, ALU.mult)
                    if g == 1:
                        i.then_inc(cmp_steps, 1)
                dve.wait_ge(cmp_steps, 4 * j + 4)
                dve.tensor_tensor(flatc, flatc, st[:, 88:96].unsqueeze(2).broadcast_to([P, 8, NC]), ALU.mult)\
                    .then_inc(cmp_ready, 1)

            compressed_maxima(0)
            for j in range(4):
                for g in range(2):
                    u = DIFF_HEADS + 2 * j + g
                    v = u - DIFF_HEADS
                    dve.wait_ge(p_exp, 8 * u)
                    maxima(u, 0)
                    maxima(u, 1)
                    if g == 0:
                        compressed_weights(j)
                    dve.wait_ge(p_exp, 8 * u + 8)
                    dve.wait_ge(p_ready2, QT * DIFF_HEADS + 8 * v)
                    dve.reciprocal(st[:, 16:24], st[:, 8:16]).then_inc(coef_ready, 1)
                    c = 2 * DIFF_HEADS + 2 * v
                    dve.wait_ge(coef_ready, c + 1)
                    for m in range(2):
                        i = dve.tensor_tensor(st[:, 24 + 4 * m:28 + 4 * m], gN[:, :, 3 * (4 * g + j) + 1 + m],
                                              st[:, 16 + 4 * m:20 + 4 * m], ALU.mult)
                    i.then_inc(coef_ready, 1)
                    dve.wait_ge(coef_ready, c + 2)
                    for m in range(2):
                        for t in range(QT):
                            qt = QT - 1 - t
                            f = slice(TILE_OFF[t], TILE_OFF[t] + TILE_W[t])
                            dve.tensor_scalar(prob[:, m, f], prob[:, m, f], st[:, 24 + 4 * m + qt:25 + 4 * m + qt],
                                              None, ALU.mult).then_inc(p_ready2, 1)
                    if g == 0 and j in (1, 2):
                        item(20 + j)
                    dve.wait_ge(turned, DIFF_HEADS + 2 * v + 2)
                    if v:
                        dve.wait_ge(o_ready, u)
                    for b, off, w in BANKS3:
                        dve.tensor_copy(AT[:, 1, off:off + w], ps[3 + b][:, 0:w]).then_inc(at2_ready, 1)
                    if g == 1 and j < 3:
                        compressed_maxima(j + 1)
            heads = oN[:, :, 0:DIFF_HEADS * P].rearrange("p q (h d) -> p q h d", h=DIFF_HEADS)
            sqs = flat[:, 0:QT * DIFF_HEADS * P].rearrange("p (q h d) -> p q h d", q=QT, h=DIFF_HEADS)
            dve.wait_ge(turned, DIFF_HEADS + 16)
            for q in range(QT):
                i = dve.tensor_tensor(sqs[:, q], heads[:, q], heads[:, q], ALU.mult)
            i.then_inc(head_sq, 1)
            dve.wait_ge(head_sq, 1)
            dve.tensor_reduce(st[:, 32:48], flat[:, 0:QT * DIFF_HEADS * P].rearrange("p (a d) -> p a d", d=P), AX_X,
                              ALU.add).then_inc(head_sq, 1)
            dve.wait_ge(head_std, 1)
            dve.reciprocal(st[:, 96:112], st[:, 48:64]).then_inc(head_sq, 1)
            dve.wait_ge(head_sq, 3)
            for q in range(QT):
                for h in range(DIFF_HEADS):
                    k = 96 + q * DIFF_HEADS + h
                    dve.tensor_scalar(heads[:, q, h, :], heads[:, q, h, :], st[:, k:k + 1], None, ALU.mult)\
                        .then_inc(head_done, 1)
            for n in range(KT):
                dve.wait_ge(x_high, 8 * XH["mixer"] + n + 1)
                if n < DIFF_HEADS:
                    dve.scalar_tensor_tensor(xL[:, n, :], ps[n][:], pc("subln"), fp(xH[:, n, :]), ALU.mult,
                                             ALU.subtract).then_inc(x_ready, 1)
                else:
                    dve.tensor_tensor(xL[:, n, :], ps[n][:], fp(xH[:, n, :]), ALU.subtract).then_inc(x_ready, 1)
            take_banks("wout", copy_product)
            post_norm("mix_post")
            dve.wait_ge(updated, 16)
            pre_norm("ff2_pre")
            ffn(3)
            take_banks("down3", copy_product)
            post_norm("ff2_post")


def lay_out(inputs):
    import numpy as np
    a = {k: np.asarray(v) for k, v in inputs.items()}

    def by_output(w):
        n = w.shape[1] // P
        return w.reshape(KT, P, n, P).transpose(2, 1, 0, 3).reshape(n, P, KT * P)

    def by_k(w):
        return w.reshape(w.shape[0] // P, P, D)

    def mixed(*ws):
        return np.stack([by_output(w) for w in ws], axis=1).reshape(-1, P, KT * P)

    w_in = a["w_in_2"][0]
    sizes = [512, 512, 512, 512] + [128] * 6 + [24]
    at = np.concatenate([[0], np.cumsum(sizes)])
    dq, dk, dv, nq, kc, vc, ks, vs, kw, vw, gl = [w_in[:, at[i]:at[i + 1]] for i in range(11)]
    nq = nq.reshape(D, 2, 4, DH).transpose(0, 2, 1, 3).reshape(D, 512)
    gl = np.concatenate([gl, np.zeros((D, P - 24), np.float32)], axis=1)
    wo2 = a["w_out_2"][0]
    wo2 = np.concatenate([wo2[:512], wo2[512:].reshape(2, 4, DH, D).transpose(1, 0, 2, 3).reshape(512, D)], axis=0)
    parts = [mixed(a["a_pw1_w"][0][:, D:], a["a_pw1_w"][0][:, :D]), by_k(a["a_pw2_w"][0])]
    for l in range(2):
        if l == 1:
            parts += [mixed(a["b_wq"][0], a["kv_wk"], a["kv_wv"]), by_k(a["b_wo"][0])]
        gates = by_output(a["ple_w_gate"][l])
        proj = a["ple_w_proj"][l].reshape(2, P, 2, 4, P).transpose(2, 1, 3, 0, 4).reshape(2, P, 8 * P)
        parts += [np.stack([gates[n] if kind == "gate" else proj[n] for kind, n in PLE_ORDER]),
                  mixed(a["ffn_w_gate"][l], a["ffn_w_up"][l]), by_k(a["ffn_w_down"][l])]
    parts += [mixed(a["ff1_w_gate_2"][0], a["ff1_w_up_2"][0]), by_k(a["ff1_w_down_2"][0]), 
              *[by_output(w) for w in (kc, vc, ks, vs, kw, vw, gl)], mixed(dq, dk, dv), by_output(nq), by_k(wo2)]
    parts += [mixed(a["ff2_w_gate_2"][0], a["ff2_w_up_2"][0]), by_k(a["ff2_w_down_2"][0])]
    ws = np.concatenate(parts, axis=0)
    assert ws.shape[0] == NCHUNKS

    def col(v):
        return v.reshape(-1, P).T

    def taps(w):
        return w.reshape(w.shape[0], -1, P).transpose(2, 1, 0).reshape(P, -1)

    v = {"pw1_ba": col(a["a_pw1_b"][0][:D]), "pw1_bg": col(a["a_pw1_b"][0][D:]), "dw_w": taps(a["a_dw_w"][0]),
         "dw_b": col(a["a_dw_b"][0]), "aln_g": col(a["a_ln_g"][0]), "aln_b": col(a["a_ln_b"][0]),
         "pw2_b": col(a["a_pw2_b"][0])}
    for l in range(2):
        v[f"mix_g{l}"] = col(a["ln_mix_g"][l])
        v[f"mix_b{l}"] = col(a["ln_mix_b"][l])
        v[f"fcw{l}"] = taps(a["ffn_conv_w"][l])
        v[f"fcb{l}"] = col(a["ffn_conv_b"][l])
        v[f"ffn_g{l}"] = col(a["ln_ffn_g"][l])
        v[f"ffn_b{l}"] = col(a["ln_ffn_b"][l])
    for n, m in (("ff1_pre", "ff1_norm_pre_2"), ("ff1_post", "ff1_norm_post_2"), ("mix_pre", "mix_norm_pre_2"),
                 ("mix_post", "mix_norm_post_2"), ("ff2_pre", "ff2_norm_pre_2"), ("ff2_post", "ff2_norm_post_2")):
        v[n] = col(a[m][0])
    v["subln"] = col(a["diff_subln_2"][0])
    for n in "kv":
        v[f"pe_{n}"] = a[f"cmp_pe_{n}_2"][0].reshape(PAIRS, 2 * DH).T
    v["w2_k"] = a["cmp_k_w2_2"][0].reshape(2, P, DH).transpose(1, 0, 2).reshape(P, 2 * DH)
    v["w2_v"] = a["cmp_v_w2_2"][0].reshape(2, P, DH).transpose(1, 0, 2).reshape(P, 2 * DH)
    v["lams"] = np.tile(np.concatenate([a[f"lambda_{n}_2"][0] for n in ("q1", "k1", "q2", "k2")])[None], (P, 1))
    params = np.concatenate([v[n] for n, _ in PARAMS], axis=1)
    w1 = np.stack([a[f"cmp_{n}_w1_2"][0].reshape(PAIRS, P, CMP_HID).transpose(1, 0, 2).reshape(P, PAIRS * CMP_HID)
                   for n in "kv"])
    return {"ws": ws, "xT": np.ascontiguousarray(a["x"][0].T),
            "pT": np.ascontiguousarray(a["p"][:, 0].transpose(0, 2, 1)), "params": params, "w1": w1}


def constants():
    import numpy as np
    i = np.arange(P)
    later = i[None, :] > i[:, None]
    c = {"ident": np.eye(P), "mean": np.full((P, P), 1.0 / D), "negtri": -(i[:, None] >= i[None, :]).astype(float),
         "negone": -np.ones((P, P)), "maskS": np.where(later, 0.0, NEG), "maskC": np.where(later, NEG, 0.0),
         "eps": np.tile(np.array([[LN_EPS, RMS_EPS]]), (P, 1))}
    d = i % DH
    partner = np.where(d < 8, i + 8, np.where(d < 16, i - 8, i))
    c["perm"] = (i[:, None] == partner[None, :]).astype(float)
    c["swap"] = (i[:, None] == (i[None, :] + DH) % P).astype(float)
    t = np.arange(S).reshape(QT, P)
    cend = np.arange(NC) * CMP_STRIDE + CMP_BLOCK - 1
    valid = cend[None, None, :] <= t.T[:, :, None]
    c["cadd"] = np.where(valid, 0.0, NEG).reshape(P, -1)
    c["cmul"] = valid.astype(float).reshape(P, -1)
    consts = np.concatenate([c[n] for n, _ in CONSTS], axis=1).astype(np.float32)
    inv = (500000.0 ** (-np.arange(0, 16, 2) / 16.0)).astype(np.float32)
    ang = (np.arange(S, dtype=np.float32)[None, :] * inv[:, None]).astype(np.float64)
    cos, sin = np.cos(ang), np.sin(ang)
    table = np.zeros((P, 2, S))
    table[:, 0] = 1.0
    for base in (0, DH):
        table[base:base + 8, 0] = cos
        table[base + 8:base + 16, 0] = cos
        table[base:base + 8, 1] = -sin
        table[base + 8:base + 16, 1] = sin
    return consts, table.reshape(P, 2 * S).astype(np.float32)


def kernel(**inputs):
    import numpy as np
    import concourse.bacc as bacc
    from concourse.bass_utils import run_bass_kernel_spmd as run

    arrays = lay_out(inputs)
    arrays["consts"], arrays["rope"] = constants()
    nc = bacc.Bacc("TRN2", target_bir_lowering=False, num_devices=1)
    names = ["ws", "xT", "pT", "params", "consts", "rope", "w1"]
    arrays = {n: np.ascontiguousarray(arrays[n]) for n in names}
    args = [nc.dram_tensor(n, arrays[n].shape, mybir.dt.from_np(arrays[n].dtype), kind="ExternalInput").ap()
            for n in names]
    out = nc.dram_tensor("out", (D, S), F32, kind="ExternalOutput").ap()
    build_block(nc, *args, out)
    r = run(nc, [arrays], core_ids=[0])
    return np.ascontiguousarray(r.results[0]["out"].T)[None]
```

```python
from contextlib import ExitStack

import concourse.bass as bass
from concourse import mybir

F32 = mybir.dt.float32
F32R = mybir.dt.float32r
BF16 = mybir.dt.bfloat16
ACT = mybir.ActivationFunctionType
ALU = mybir.AluOpType
AX_X = mybir.AxisListType.X

P = 128
S = 512
D = 1024
KT = D // P
F = 2816
FT = F // P
CONV_W = 31
PE_TAPS = 9
DVE_STEPS = CONV_W - PE_TAPS + 1
FCONV_W = 3
QT = S // P
DH = 64
LN_EPS = 1e-5
RMS_EPS = 1e-6
ALPHA = 4.0 ** 0.25
NEG = -1e30
SLOTS = 4
LEAD = SLOTS - 1
CMP_BLOCK = 32
CMP_STRIDE = 16
NC = S // CMP_STRIDE - 1
CMP_HID = 256
PAIRS = CMP_BLOCK // 2
NSA_HEADS = 8
DIFF_HEADS = 4

COUNTS = [("pw1", 2 * KT), ("pw2", KT)]
for _l in range(2):
    if _l == 1:
        COUNTS += [("qkv", 3 * KT), ("wo", KT)]
    COUNTS += [(f"ple{_l}", KT + 2), (f"gateup{_l}", 2 * FT), (f"down{_l}", FT)]
COUNTS += [("gateup2", 2 * FT), ("down2", FT), ("hybrid", 7 + 3 * DIFF_HEADS + 4), ("wout", KT), ("gateup3", 2 * FT),
           ("down3", FT)]
PLE_ORDER = [("gate", 0), ("gate", 1), ("proj", 0), ("gate", 2), ("gate", 3), ("gate", 4), ("gate", 5), ("proj", 1),
             ("gate", 6), ("gate", 7)]
CHUNK = {}
NCHUNKS = 0
for _n, _k in COUNTS:
    CHUNK[_n] = NCHUNKS
    NCHUNKS += _k

PARAMS = [("pw1_ba", KT), ("pw1_bg", KT), ("dw_w", KT * CONV_W), ("dw_b", KT), ("aln_g", KT), ("aln_b", KT),
          ("pw2_b", KT), ("mix_g0", KT), ("mix_b0", KT), ("mix_g1", KT), ("mix_b1", KT),
          ("fcw0", FT * FCONV_W), ("fcb0", FT), ("fcw1", FT * FCONV_W), ("fcb1", FT),
          ("ffn_g0", KT), ("ffn_b0", KT), ("ffn_g1", KT), ("ffn_b1", KT),
          ("ff1_pre", KT), ("ff1_post", KT), ("mix_pre", KT), ("mix_post", KT), ("ff2_pre", KT), ("ff2_post", KT),
          ("subln", 1), ("pe_k", PAIRS), ("pe_v", PAIRS), ("w2_k", 2 * DH), ("w2_v", 2 * DH),
          ("lams", 4 * DH)]
PCOL = {}
NPAR = 0
for _n, _k in PARAMS:
    PCOL[_n] = NPAR
    NPAR += _k

CONSTS = [("ident", P), ("mean", P), ("negtri", P), ("negone", P), ("perm", P), ("swap", P), ("maskS", P), ("maskC", P),
          ("eps", 2), ("cadd", QT * NC), ("cmul", QT * NC)]
CCOL = {}
NCON = 0
for _n, _k in CONSTS:
    CCOL[_n] = NCON
    NCON += _k

TILE_W = [512, 384, 256, 128]
TILE_BANK = [0, 1, 2, 1]
TILE_COL = [0, 0, 0, 384]
TILE_OFF = [0, 512, 1024, 896]
SCORE_COLS = 1280
BANKS3 = [(0, 0, 512), (1, 512, 512), (2, 1024, 256)]

ITEMS = [("copy", "kc", 0), ("copy", "vc", 0), ("rope", "ks", 0), ("turn", "vs", 0), ("rope", "kw", 0),
         ("turn", "vw", 0), ("gate", "gates", 0)]
for _h in range(DIFF_HEADS):
    ITEMS += [("rope", "dq", _h), ("rope", "dk", _h), ("turn", "dv", _h)]
ITEMS += [("rope", "nq", _j) for _j in range(4)]
USE = {}


def _use(*key):
    USE[key] = len(USE)


def _use_item(i):
    _use("item", i)
    if ITEMS[i][0] != "copy":
        _use("second", i)


for _i in range(7):
    _use_item(_i)
for _i in range(7, 10):
    _use_item(_i)
BESIDE = [list(range(10 + 3 * _h, 13 + 3 * _h)) if _h < 3 else [19, 20] for _h in range(DIFF_HEADS)]
for _h in range(DIFF_HEADS):
    for _i in BESIDE[_h]:
        _use_item(_i)
for _j in range(4):
    _use("cmp_scores", _j)
    if _j in (1, 2):
        _use_item(20 + _j)
    _use("cmp_turn", _j, 0)
    _use("cmp_turn", _j, 1)
ROPES = [i for i, it in enumerate(ITEMS) if it[0] == "rope"]
SECONDS = [k for k in USE if k[0] not in ("item",)]
LAMBDA_INIT = 0.2


def build_block(nc, ws, xT, pT, params, consts, rope, w1, out, stop=None):
    with ExitStack() as ctx:
        def sb(name, shape, dt=F32):
            return ctx.enter_context(nc.sbuf_tensor(name, shape, dt))

        def sem(name):
            return ctx.enter_context(nc.semaphore(name))

        def overlay(specs):
            with ExitStack() as sub:
                return [sub.enter_context(nc.sbuf_tensor(n, s, d)) for n, s, d in specs]

        raw, = overlay([("raw", [P, SLOTS, 1024], F32)])
        wL = sb("wL", [P, SLOTS, 1024], F32R)
        wH = sb("wH", [P, SLOTS, 1024], F32R)
        xf = sb("xf", [P, KT, S])
        xH = sb("xH", [P, KT, S], F32R)
        xL = sb("xL", [P, KT, S], F32R)
        tmp = sb("tmp", [P, 10, S])
        rstd = sb("rstd", [P, S])
        par = sb("par", [P, NPAR])
        con = sb("con", [P, NCON])
        bcon = sb("bcon", [P, 3 * P], BF16)
        tri = sb("tri", [P, 2, P], F32R)
        vturn0 = sb("vturn0", [P, S])
        st = sb("st", [P, 160])
        sq = [tmp[:, 8, :], tmp[:, 9, :]]

        hH, hL = overlay([("hH", [P, FT, S], F32R), ("hL", [P, FT, S], F32R)])
        cH, cL, gpad, diag = overlay([("cH", [P, KT, S], F32R), ("cL", [P, KT, S], F32R),
                                      ("gpad", [P, 2, CONV_W - 1 + S], F32),
                                      ("diag", [P, 2, PE_TAPS, P], F32)])
        (mH, mL, qT, kT, vT, vN, lg, spH, spL, aT) = overlay([
            ("mH", [P, KT, S], F32R), ("mL", [P, KT, S], F32R), ("qT", [P, 2, S], F32), ("kT", [P, 2, S], F32),
            ("vT", [P, S], F32), ("vN", [P, 2, QT, P], F32),
            ("lg", [P, 2, SCORE_COLS], F32), ("spH", [P, 2, SCORE_COLS], F32R),
            ("spL", [P, 2, SCORE_COLS], F32R), ("aT", [P, 2, SCORE_COLS], F32)])
        _, pf, pH, pL = overlay([("pgap", [P, 18944], F32), ("pf", [P, 2, S], F32), ("pH", [P, 2, S], F32R),
                                 ("pL", [P, 2, S], F32R)])

        common = [("ropeT", [P, 2, S], F32), ("ksT", [P, S], F32), ("kwT", [P, S], F32), ("vsN", [P, QT, P], F32),
                  ("vwN", [P, QT, P], F32), ("gN", [P, QT, 24], F32), ("kcC", [P, 32], F32), ("vcC", [P, P], F32)]
        (ropeT, ksT, kwT, vsN, vwN, gN, kcC, vcC, w1b, kcvc, blk_v, hid, hidT) = overlay(common + [
            ("w1b", [P, 2, PAIRS * CMP_HID], F32), ("kcvc", [P, 2, S], F32), ("blk_v", [P, PAIRS, 2, NC], F32),
            ("hid", [P, 2 * CMP_HID], F32), ("hidT", [P, 4, 2 * NC], F32)])
        (dqT, dkT, dvN, AT, pcT, pc_n, oN, nqT) = overlay(
            [(n + "_", s, d) for n, s, d in common] + [
                ("dqT", [P, 2, S], F32), ("dkT", [P, 2, S], F32), ("dvN", [P, 2, QT, P], F32), ("AT", [P, 2, SCORE_COLS], F32), ("pcT", [P, QT, P], F32), ("pc_n", [P, 2, QT, NC], F32),
                ("oN", [P, QT, D], F32), ("nqT", [P, 2, S], F32)])[8:]
        flat = tmp[:].rearrange("p a b -> p (a b)")
        prob = flat[:, 0:2 * SCORE_COLS].rearrange("p (m c) -> p m c", m=2)
        pre = flat[:, 2560:3584].rearrange("p (a b) -> p a b", a=2)
        rot = flat[:, 3584:4096]
        blk_k = flat[:, 4096:4096 + NC * CMP_BLOCK].rearrange("p (s g c) -> p s g c", s=PAIRS, g=2)

        ps = [ctx.enter_context(nc.psum_tensor(f"ps{i}", [P, 512], F32)) for i in range(8)]

        def pc(name, n=0, w=1):
            return par[:, bass.ds(PCOL[name] + n, w)]

        def cc(name, w=P):
            return con[:, CCOL[name]:CCOL[name] + w]

        identB, maskSB, maskCB = bcon[:, 0:P], bcon[:, P:2 * P], bcon[:, 2 * P:3 * P]

        in_loaded = sem("in_loaded")
        x_loaded = [sem(f"x_loaded{k}") for k in range(KT)]
        raw_loaded = [sem(f"raw_loaded{j}") for j in range(SLOTS)]
        high_ready = sem("high_ready")
        low_ready = sem("low_ready")
        chunk_done = sem("chunk_done")
        bank_done = sem("bank_done")
        const_ready = sem("const_ready")
        x_high = sem("x_high")
        x_ready = sem("x_ready")
        src_ready = sem("src_ready")
        mean_ready = sem("mean_ready")
        centered = sem("centered")
        squared = sem("squared")
        sumsq = sem("sumsq")
        log_ready = sem("log_ready")
        rstd_ready = sem("rstd_ready")
        normed = sem("normed")
        affine = sem("affine")
        glu_sig = sem("glu_sig")
        glu_pad = sem("glu_pad")
        glu_banks_free = sem("glu_banks_free")
        taps = sem("taps")
        diag_ready = sem("diag_ready")
        conv_done = sem("conv_done")
        conv_free = sem("conv_free")
        c_act = sem("c_act")
        c_ready = sem("c_ready")
        res_scaled = sem("res_scaled")
        p_loaded = sem("p_loaded")
        p_high = sem("p_high")
        p_ready = sem("p_ready")
        ple_sig = sem("ple_sig")
        ple_mul = sem("ple_mul")
        ple_free = sem("ple_free")
        tap2 = sem("tap2")
        tap10 = sem("tap10")
        gate_scaled = sem("gate_scaled")
        gate_act = sem("gate_act")
        h_made = sem("h_made")
        h_high = sem("h_high")
        h_ready = sem("h_ready")
        q_free = sem("q_free")
        qkv_copied = sem("qkv_copied")
        z_ready = sem("z_ready")
        abs_ready = sem("abs_ready")
        e_ready = sem("e_ready")
        ln_ready = sem("ln_ready")
        sp_ready = sem("sp_ready")
        sp_high = sem("sp_high")
        sp_low = sem("sp_low")
        cum_ready = sem("cum_ready")
        a_ready = sem("a_ready")
        av_ready = sem("av_ready")
        vt_ready = sem("vt_ready")
        m_high = sem("m_high")
        m_ready = sem("m_ready")
        updated = sem("updated")
        w1_loaded = sem("w1_loaded")
        rope_loaded = sem("rope_loaded")
        b7_read = sem("b7_read")
        second_done = sem("second_done")
        roped = sem("roped")
        rot_ready = sem("rot_ready")
        blocks_ready = sem("blocks_ready")
        swapped = sem("swapped")
        hid_psum = sem("hid_psum")
        hid_ready = sem("hid_ready")
        lam_steps = sem("lam_steps")
        s_ready = sem("s_ready")
        max_ready = sem("max_ready")
        p_exp = sem("p_exp")
        coef_ready = sem("coef_ready")
        scaled = sem("scaled")
        p_ready2 = sem("p_ready2")
        turned = sem("turned")
        at_ready = sem("at_ready")
        at2_ready = sem("at2_ready")
        o_ready = sem("o_ready")
        o_copied = sem("o_copied")
        cmp_steps = sem("cmp_steps")
        cmp_sum = sem("cmp_sum")
        cmp_exp = sem("cmp_exp")
        cmp_ready = sem("cmp_ready")
        head_sq = sem("head_sq")
        head_std = sem("head_std")
        head_done = sem("head_done")
        o_turned = sem("o_turned")
        out_done = sem("out_done")

        block = ctx.enter_context(nc.Block())

        def fp(ap):
            return ap.bitcast(F32)

        @block.sync
        def _(sp_e):
            for c in range(2):
                sp_e.dma_start(raw[:, c, :], ws[c]).then_inc(raw_loaded[c], 16)
            for k in range(KT):
                sp_e.dma_start(xf[:, k, :], xT[k * P:k * P + P, :]).then_inc(x_loaded[k], 16)
            for c in range(2, SLOTS):
                sp_e.dma_start(raw[:, c, :], ws[c]).then_inc(raw_loaded[c], 16)

            def load(t, j):
                c = t * SLOTS + j
                sp_e.wait_ge(chunk_done, c - SLOTS + 1)
                sp_e.dma_start(raw[:, j, :], ws[bass.ds(c, 1)].rearrange("o p n -> (o p) n"))\
                    .then_inc(raw_loaded[j], 16)

            with sp_e.Fori(1, NCHUNKS // SLOTS) as t:
                for j in range(SLOTS):
                    load(t, j)
            for j in range(NCHUNKS % SLOTS):
                load(NCHUNKS // SLOTS, j)
            for n in range(KT):
                sp_e.wait_ge(updated, 16 + n + 1)
                sp_e.dma_start(out[n * P:n * P + P, :], xf[:, n, :]).then_inc(out_done, 16)
            sp_e.wait_ge(out_done, 16 * KT)

        @block.gpsimd
        def _(pool):
            def split(t, j):
                pool.wait_ge(high_ready, t * SLOTS + (j + 1))
                pool.tensor_tensor(wL[:, j, :], raw[:, j, :], fp(wH[:, j, :]), ALU.subtract).then_inc(low_ready, 1)

            for j in range(SLOTS):
                split(0, j)
            with pool.Fori(1, NCHUNKS // SLOTS) as t:
                for j in range(SLOTS):
                    split(t, j)
            for j in range(NCHUNKS % SLOTS):
                split(NCHUNKS // SLOTS, j)

        NORM = {n: i for i, n in enumerate(["conf", "mix0", "ffn0", "mix1", "ffn1", "ff1_pre", "ff1_post",
                                            "mix_pre", "mix_post", "ff2_pre", "ff2_post"])}
        DIVIDING = {n: len([m for m in list(NORM)[:i] if not m.endswith("pre")]) for n, i in NORM.items()}
        LNORM = ["conf", "mix0", "ffn0", "mix1", "ffn1"]
        FULL = {n: i for i, n in enumerate(["pw2", "down0", "wo", "down1", "down2", "wout", "down3"])}
        XV = {n: i for i, n in enumerate(["in", "mix0", "ffn0", "mix1", "ff1_pre", "mix_pre", "mixer",
                                          "ff2_pre"])}
        XH = {n: i for i, n in enumerate(["in", "mix0", "ffn0", "mix1", "ff1_pre", "mix_pre", "mixer", "ff2_pre"])}
        NUNITS = DIFF_HEADS + NSA_HEADS
        SRC = {n: i for i, n in enumerate(["conf", "mix0", "ffn0", "mix1", "ffn1", "ff1_post", "mix_post",
                                           "ff2_post"])}

        @block.tensor
        def _(pe):
            def three(bank, w, rh, rl, start, stop, c=None):
                slot, cols = w
                pe.matmul(bank, wH[:, slot, cols], rh, start=start, stop=False)
                pe.matmul(bank, wH[:, slot, cols], rl, start=False, stop=False)
                return pe.matmul(bank, wL[:, slot, cols], rh, start=False, stop=stop)

            def tile_product(bank, c, slot, rH=xH, rL=xL):
                pe.wait_ge(low_ready, c + 1)
                for k in range(KT):
                    mm = three(bank, (slot, slice(k * P, k * P + P)), rH[:, k, :], rL[:, k, :],
                               k == 0, k == KT - 1)
                mm.then_inc(chunk_done, 1)

            def first_pair(b0, b1, c, xname, norm=None):
                pe.wait_ge(low_ready, c + 2)
                for k in range(KT):
                    pe.wait_ge(x_ready, 8 * XV[xname] + k + 1)
                    cols = slice(k * P, k * P + P)
                    for i, b in enumerate((b0, b1)):
                        mm = three(b, ((c + i) % SLOTS, cols), xH[:, k, :], xL[:, k, :], k == 0, k == KT - 1)
                        if k == KT - 1:
                            mm.then_inc(chunk_done, 1)
                    if norm:
                        one_square(norm, k, 5)

            def full_product(name, nk, rH, rL, ready, ready_base, banks_free):
                c0 = CHUNK[name]

                def one_k(k, j, first=False, last=False):
                    pe.wait_ge(low_ready, c0 + k + 1)
                    pe.wait_ge(ready, ready_base + k + 1)
                    slot = (c0 + j) % SLOTS
                    rh = rH[:, bass.ds(k, 1), :].rearrange("p o t -> p (o t)")
                    rl = rL[:, bass.ds(k, 1), :].rearrange("p o t -> p (o t)")
                    for n in range(8):
                        if first:
                            banks_free(n)
                        mm = three(ps[n][:], (slot, slice(n * P, n * P + P)), rh, rl, first, last)
                        if last and n < 7:
                            mm.then_inc(bank_done, 1)
                    mm.then_inc(chunk_done, 1)

                before = 1 + (nk - 2) % SLOTS
                steps = (nk - 1 - before) // SLOTS
                for k in range(before):
                    one_k(k, k, first=k == 0)
                with pe.Fori(0, steps) as t:
                    for j in range(SLOTS):
                        one_k(t * SLOTS + (before + j), before + j)
                for k in range(before + steps * SLOTS, nk):
                    one_k(k, k, last=k == nk - 1)

            def mean_product(name, src):
                i = SRC[name]
                for n in range(KT):
                    pe.wait_ge(src_ready, 8 * i + n + 1)
                    mm = pe.matmul(ps[0][:], cc("mean"), src[:, n, :], start=n == 0, stop=n == KT - 1)
                mm.then_inc(mean_ready, 1)

            def keep_warm(bank, steps):
                for _ in range(steps):
                    pe.matmul(ps[bank][:, 0:3 * P], identB, bcon[:], start=True, stop=True)

            def one_square(name, n, bank):
                pe.wait_ge(squared, 8 * NORM[name] + n + 1)
                pe.matmul(ps[bank][:], cc("mean"), sq[n % 2], start=n == 0, stop=n == KT - 1).then_inc(sumsq, 1)

            def sumsq_product(name, bank):
                if name.endswith("post"):
                    pe.wait_ge(src_ready, 8 * SRC[name] + 2)
                for n in range(KT):
                    one_square(name, n, bank)
                if name != "ff2_post":
                    keep_warm(7, 30 if name.endswith("post") else 18)

            def ffn(inst, xname, ple_tiles=0):
                c0 = CHUNK[f"gateup{inst}"]

                def gate_and_up(f, j, c):
                    pe.wait_ge(h_made, f + (24 * inst + 1))
                    tile_product(ps[2 * j][:], c, (c0 + 2 * j) % SLOTS)
                    tile_product(ps[2 * j + 1][:], c + 1, (c0 + 2 * j + 1) % SLOTS)

                if ple_tiles:
                    pe.wait_ge(h_made, 24 * inst + 1)
                    pe.wait_ge(ple_sig, ple_tiles - 2)
                first_pair(ps[0][:], ps[1][:], c0, xname, xname if inst >= 2 else None)
                if ple_tiles:
                    pe.wait_ge(ple_sig, ple_tiles)
                gate_and_up(1, 1, c0 + 2)
                with pe.Fori(1, FT // 2) as t:
                    for j in range(2):
                        gate_and_up(t * 2 + j, j, t * 4 + (c0 + 2 * j))

                def banks_free(n):
                    if n == 0:
                        pe.wait_ge(h_made, 24 * inst + 24)
                full_product(f"down{inst}", FT, hH, hL, h_ready, FT * inst, banks_free)

            def ple(layer, xname):
                pe.wait_ge(p_ready, layer + 1)
                pe.wait_ge(rstd_ready, NORM[xname] + 1)
                c0 = CHUNK[f"ple{layer}"]
                first_pair(ps[0][:], ps[1][:], c0, xname)
                for i, (kind, n) in enumerate(PLE_ORDER[2:]):
                    c = c0 + 2 + i
                    if kind == "gate":
                        if n >= 4:
                            pe.wait_ge(ple_sig, KT * layer + n - 3)
                        tile_product(ps[n % 4][:], c, c % SLOTS)
                        continue
                    pe.wait_ge(low_ready, c + 1)
                    if n:
                        pe.wait_ge(ple_mul, KT * layer + 4)
                    for m in range(4):
                        for k in range(2):
                            cols = slice((2 * m + k) * P, (2 * m + k) * P + P)
                            mm = three(ps[4 + m][:], (c % SLOTS, cols), pH[:, k, :], pL[:, k, :], k == 0, k == 1)
                    mm.then_inc(chunk_done, 1)

            def glu_products(n, j):
                pe.wait_ge(glu_banks_free, n + 1)
                tile_product(ps[2 * j][:], n * 2, 2 * j)
                tile_product(ps[2 * j + 1][:], n * 2 + 1, 2 * j + 1)

            def conv_taps(n, j):
                pe.wait_ge(glu_banks_free, n + 3)
                pe.wait_ge(diag_ready, n * PE_TAPS + PE_TAPS)
                pe.wait_ge(conv_free, n + 1)
                for tap in range(PE_TAPS):
                    mm = pe.matmul(ps[4 + j][:], diag[:, j, tap, :], gpad[:, j, tap:tap + S], start=tap == 0,
                                   stop=tap == PE_TAPS - 1)
                mm.then_inc(conv_done, 1)

            pe.sem_inc(conv_done, 2)
            first_pair(ps[0][:], ps[1][:], 0, "in")
            with pe.Fori(0, KT // 2 - 1) as t:
                glu_products(t * 2 + 1, 1)
                conv_taps(t * 2, 0)
                glu_products(t * 2 + 2, 0)
                conv_taps(t * 2 + 1, 1)
            glu_products(KT - 1, 1)
            conv_taps(KT - 2, 0)
            conv_taps(KT - 1, 1)
            mean_product("conf", tmp)
            sumsq_product("conf", 1)
            full_product("pw2", KT, cH, cL, c_ready, 0, lambda n: None)
            mean_product("mix0", xf)
            sumsq_product("mix0", 1)
            ple(0, "mix0")
            ffn(0, "mix0", KT)
            mean_product("ffn0", xf)
            sumsq_product("ffn0", 1)

            c0 = CHUNK["qkv"]

            def project(p, j, which):
                if which != 1:
                    pe.wait_ge(q_free, p * 4 + (which + 1))
                elif p > 1:
                    pe.wait_ge(m_ready, p - 1)
                tile_product(ps[7 - which % 2][:], p * 3 + (c0 + which), (c0 + 3 * p + which) % SLOTS)

            def turn_values(p, j):
                pe.wait_ge(qkv_copied, p * 4 + 3)
                for kt in range(QT):
                    mm = pe.transpose(ps[7][:, kt * P:kt * P + P], vT[:, kt * P:kt * P + P], cc("ident"))
                mm.then_inc(vt_ready, 1)

            def scores(p, j, h):
                pe.wait_ge(qkv_copied, p * 4 + 2)
                r = slice(DH * h, DH * h + DH)
                for kt in range(QT):
                    b = ps[3 * h + TILE_BANK[kt]]
                    o = TILE_COL[kt]
                    pe.matmul(b[:, o:o + TILE_W[kt]], kT[r, j, kt * P:kt * P + P], qT[r, j, kt * P:S],
                              start=kt != 3, stop=False, skip_group_check=True)
                    mm = pe.matmul(b[:, o:o + P], identB, maskSB, start=False, stop=False, skip_group_check=True)
                mm.then_inc(z_ready, 1)

            def cumulate(p, h):
                pe.wait_ge(sp_low, p * 2 + (h + 1))
                for kt in range(QT):
                    b = ps[3 * h + TILE_BANK[kt]]
                    o = TILE_COL[kt]
                    for k2 in range(kt, QT):
                        for part in (spH, spL):
                            m = pe.matmul(b[:, o + (k2 - kt) * P:o + TILE_W[kt]], tri[:, int(k2 > kt), :],
                                          part[:, h, TILE_OFF[k2]:TILE_OFF[k2] + TILE_W[k2]],
                                          start=False, stop=False, skip_group_check=True)
                m.then_inc(cum_ready, 1)

            def values(p, j, h):
                pe.wait_ge(a_ready, p * 6 + (3 * h + 3))
                r = slice(DH * h, DH * h + DH)
                for kt in range(QT):
                    m = pe.matmul(ps[6][r, kt * P:S], vN[:, j, kt, r], aT[:, h, TILE_OFF[kt]:TILE_OFF[kt] + TILE_W[kt]],
                                  start=kt == 0, stop=kt == QT - 1, skip_group_check=True)
                m.then_inc(av_ready, 1)

            def pair(p, j, more, first=False):
                if not first:
                    pe.wait_ge(a_ready, p * 6)
                scores(p, j, 0)
                scores(p, j, 1)
                if more:
                    project(p + 1, 1 - j, 0)
                    project(p + 1, 1 - j, 1)
                cumulate(p, 0)
                cumulate(p, 1)
                if more:
                    project(p + 1, 1 - j, 2)
                if not first:
                    pe.wait_ge(m_ready, p)
                pe.wait_ge(qkv_copied, p * 4 + 4)
                if not more:
                    keep_warm(7, 10)
                values(p, j, 0)
                values(p, j, 1)
                if more:
                    turn_values(p + 1, 1 - j)

            first_pair(ps[7][:], ps[6][:], c0, "ffn0")
            project(0, 0, 2)
            turn_values(0, 0)
            for p in range(KT):
                pair(p, p % 2, p < KT - 1, first=p == 0)
            pe.wait_ge(a_ready, 6 * KT)
            pe.wait_ge(qkv_copied, 4 * KT)

            def wo_free(n):
                if n == 6:
                    pe.wait_ge(m_ready, KT)
            full_product("wo", KT, mH, mL, m_ready, 0, wo_free)
            mean_product("mix1", xf)
            sumsq_product("mix1", 1)
            ple(1, "mix1")
            ffn(1, "mix1", 2 * KT)
            mean_product("ffn1", xf)
            sumsq_product("ffn1", 1)

            ffn(2, "ff1_pre")
            sumsq_product("ff1_post", 1)

            c0 = CHUNK["hybrid"]
            q_of = {"dq": dqT, "nq": nqT}

            def project_item(i):
                pe.wait_ge(b7_read, USE["item", i])
                tile_product(ps[7][:], c0 + i, (c0 + i) % SLOTS)

            def second_step(i):
                kind = ITEMS[i][0]
                pe.wait_ge(b7_read, USE["second", i])
                if kind == "rope":
                    mm = pe.matmul(ps[7][:], cc("perm"), pre[:, ROPES.index(i) % 2, :], start=True, stop=True)
                else:
                    for t in range(QT):
                        mm = pe.transpose(ps[7][:, t * P:t * P + P], vturn0[:, t * P:t * P + P], cc("ident"))
                mm.then_inc(second_done, 1)

            def item(i):
                project_item(i)
                second_step(i)

            first_pair(ps[7][:], ps[6][:], c0, "mix_pre", "mix_pre")
            item(2)
            for i in range(2):
                pe.wait_ge(b7_read, USE["item", i] + 1)
                pe.matmul(ps[3 + i][:], cc("swap"), kcvc[:, i, :], start=True, stop=True).then_inc(swapped, 1)
            for i in range(3, 7):
                item(i)

            pe.wait_ge(blocks_ready, 2)
            pe.wait_ge(w1_loaded, 32)
            for kv, blk in ((0, blk_k), (1, blk_v)):
                for pair_ in range(PAIRS):
                    mm = pe.matmul(ps[5][0:2 * NC, kv * CMP_HID:(kv + 1) * CMP_HID],
                                   blk[:, pair_, :, :].rearrange("p g c -> p (g c)"),
                                   w1b[:, kv, pair_ * CMP_HID:(pair_ + 1) * CMP_HID], start=pair_ == 0,
                                   stop=pair_ == PAIRS - 1, skip_group_check=True)
            mm.then_inc(hid_psum, 1)

            def turn_hidden():
                pe.wait_ge(hid_ready, 1)
                for k in range(4):
                    mm = pe.transpose(ps[3][:, k * 2 * NC:(k + 1) * 2 * NC], hid[0:2 * NC, k * P:k * P + P],
                                      con[0:2 * NC, CCOL["ident"]:CCOL["ident"] + 2 * NC])
                mm.then_inc(hid_psum, 1)

            def second_layer():
                pe.wait_ge(hid_ready, 2)
                for g in range(2):
                    for m in range(2):
                        pe.matmul(ps[4][DH * g:DH * g + DH, 0:NC], pc("w2_k", DH * m, DH),
                                  hidT[:, m, g * NC:(g + 1) * NC], start=m == 0, stop=m == 1, skip_group_check=True)
                for g in range(2):
                    for m in range(2):
                        mm = pe.matmul(ps[5][0:NC, DH * g:DH * g + DH], hidT[:, 2 + m, g * NC:(g + 1) * NC],
                                       pc("w2_v", DH * m, DH), start=m == 0, stop=m == 1, skip_group_check=True)
                mm.then_inc(hid_psum, 1)

            def scores2(m, q, k, r):
                for t in range(QT):
                    qt = QT - 1 - t
                    b = ps[3 * (m % 2) + TILE_BANK[t]]
                    o = TILE_COL[t]
                    pe.matmul(b[:, o:o + TILE_W[t]], q[r, qt * P:qt * P + P], k[r, 0:TILE_W[t]],
                              start=t != 3, stop=False, skip_group_check=True)
                    mm = pe.matmul(b[:, o + qt * P:o + qt * P + P], identB, maskCB, start=False, stop=False,
                                   skip_group_check=True)
                mm.then_inc(s_ready, 1)

            def turn_map(m, src):
                for kt in range(QT):
                    b = ps[3 * (m % 2) + TILE_BANK[kt]]
                    for qt in range(kt, QT):
                        o = TILE_COL[kt] + (qt - kt) * P
                        f = TILE_OFF[QT - 1 - qt] + kt * P
                        mm = pe.transpose(b[:, o:o + P], prob[:, src, f:f + P], cc("ident"))
                mm.then_inc(turned, 1)

            def weigh(m, v, w, first):
                for qt in range(QT):
                    for kt in range(qt + 1):
                        f = TILE_OFF[kt] + (qt - kt) * P
                        mm = pe.matmul(ps[6][:, qt * w:qt * w + w], AT[:, m % 2, f:f + P], v[:, kt, :],
                                       start=first and qt == 0 and kt == 0, stop=False, skip_group_check=True)
                return mm

            item(7)
            turn_hidden()
            item(8)
            second_layer()
            item(9)
            pe.wait_ge(hid_ready, 4)
            def weigh_head(h):
                pe.wait_ge(at_ready, 3 * (h + 1))
                if h:
                    pe.wait_ge(o_copied, h)
                if h == DIFF_HEADS - 1:
                    pe.wait_ge(cmp_steps, 1)
                weigh(0, dvN[:, h % 2, :, :], P, True).then_inc(o_ready, 1)

            def compressed_scores(j):
                pe.wait_ge(roped, 10 + j + 1)
                pe.wait_ge(b7_read, USE["cmp_scores", j])
                pe.wait_ge(o_copied, DIFF_HEADS + 2 * j - 1)
                for g in range(2):
                    for qt in range(QT):
                        r = slice(DH * g, DH * g + DH)
                        mm = pe.matmul(ps[7 - g][:, qt * NC:qt * NC + NC], nqT[r, j % 2, qt * P:qt * P + P],
                                       kcC[r, 0:NC], start=qt == 0, stop=False, skip_group_check=True)
                mm.then_inc(second_done, 1)

            def weigh_branches(u):
                v = u - DIFF_HEADS
                j, g = v // 2, v % 2
                r = slice(DH * g, DH * g + DH)
                pe.wait_ge(o_copied, u)
                if g == 1 and j < 3:
                    pe.wait_ge(cmp_steps, 4 * (j + 1) + 1)
                pe.wait_ge(b7_read, USE["cmp_turn", j, g] + 1)
                for qt in range(QT):
                    pe.matmul(ps[6][:, qt * DH:qt * DH + DH], pcT[0:NC, qt, :], vcC[0:NC, r],
                              start=qt == 0, stop=False, skip_group_check=True)
                pe.wait_ge(at_ready, 3 * u + 3)
                weigh(0, vsN[:, :, r], DH, False)
                pe.wait_ge(at2_ready, 3 * v + 3)
                weigh(1, vwN[:, :, r], DH, False).then_inc(o_ready, 1)

            for h in range(DIFF_HEADS):
                j = h % 2
                beside = BESIDE[h]
                project_item(beside[0])
                pe.wait_ge(b7_read, USE["second", 9 + 3 * h] + 1)
                pe.wait_ge(roped, 2 + 2 * h + 2)
                if h:
                    pe.wait_ge(at_ready, 3 * h)
                scores2(2 * h, dqT[:, j, :], dkT[:, j, :], slice(0, DH))
                second_step(beside[0])
                if h:
                    pe.wait_ge(p_exp, 8 * h)
                scores2(2 * h + 1, dqT[:, j, :], dkT[:, j, :], slice(DH, P))
                project_item(beside[1])
                if h:
                    weigh_head(h - 1)
                second_step(beside[1])
                for i in beside[2:]:
                    project_item(i)
                pe.wait_ge(p_ready2, QT * (h + 1))
                turn_map(0, 0)
                for i in beside[2:]:
                    second_step(i)
            compressed_scores(0)

            for j in range(4):
                for g in range(2):
                    u = DIFF_HEADS + 2 * j + g
                    v = u - DIFF_HEADS
                    r = slice(DH * g, DH * g + DH)
                    pe.wait_ge(at_ready, 3 * u)
                    pe.wait_ge(p_exp, 8 * u)
                    scores2(0, nqT[:, j % 2, :], ksT, r)
                    if v:
                        pe.wait_ge(at2_ready, 3 * v)
                    scores2(1, nqT[:, j % 2, :], kwT, r)
                    if v:
                        weigh_branches(u - 1)
                    else:
                        weigh_head(DIFF_HEADS - 1)
                    if g == 0 and j in (1, 2):
                        item(20 + j)
                    pe.wait_ge(cmp_ready, j + 1)
                    pe.wait_ge(b7_read, USE["cmp_turn", j, g])
                    for qt in range(QT):
                        mm = pe.transpose(ps[7][0:NC, qt * P:qt * P + P], pc_n[:, g, qt, :], cc("ident"))
                    mm.then_inc(second_done, 1)
                    n0 = QT * DIFF_HEADS + 8 * v
                    pe.wait_ge(p_ready2, n0 + QT)
                    turn_map(0, 0)
                    pe.wait_ge(p_ready2, n0 + 2 * QT)
                    turn_map(1, 1)
                    if g == 1 and j < 3:
                        compressed_scores(j + 1)
            weigh_branches(NUNITS - 1)

            pe.wait_ge(o_copied, NUNITS)
            pe.wait_ge(head_done, QT * DIFF_HEADS)
            for n in range(KT):
                for qt in range(QT):
                    mm = pe.transpose(ps[n][:, qt * P:qt * P + P], oN[:, qt, n * P:n * P + P], cc("ident"))
                mm.then_inc(o_turned, 1)
            full_product("wout", KT, xH, xL, x_ready, 8 * XV["mixer"],
                         lambda n: pe.wait_ge(x_ready, 8 * XV["mixer"] + n + 1))
            sumsq_product("mix_post", 1)
            ffn(3, "ff2_pre")
            sumsq_product("ff2_post", 1)

        @block.scalar
        def _(act):
            def load_p(layer):
                act.dma_start(pf[:], pT[layer].rearrange("(k p) t -> p k t", p=P)).then_inc(p_loaded, 16)

            act.dma_start(par[:], params).then_inc(in_loaded, 16)
            act.dma_start(con[:], consts).then_inc(in_loaded, 16)
            load_p(0)

            def high(c, t=0):
                act.wait_ge(raw_loaded[c % SLOTS], t * 16 + 16 * (c // SLOTS + 1))
                act.activation(wH[:, c % SLOTS, :], raw[:, c % SLOTS, :], ACT.Copy).then_inc(high_ready, 1)

            def high_after(c, t=0):
                act.wait_ge(chunk_done, t * SLOTS + (c + 1))
                high(c + LEAD, t)

            def highs(name, upto=None):
                c0, n = CHUNK[name], upto or dict(COUNTS)[name]
                n = min(n, NCHUNKS - LEAD - c0)
                with act.Fori(0, n // SLOTS) as t:
                    for j in range(SLOTS):
                        high_after(c0 + j, t)
                for j in range(n // SLOTS * SLOTS, n):
                    high_after(c0 + j)

            for c in range(2):
                high(c)
            for n in range(KT):
                act.wait_ge(x_loaded[n], 16)
                act.activation(xH[:, n, :], xf[:, n, :], ACT.Copy).then_inc(x_high, 1)
            for c in range(2, LEAD):
                high(c)
            act.wait_ge(in_loaded, 32)
            act.activation(identB, cc("ident"), ACT.Copy).then_inc(const_ready, 1)
            act.activation(tri[:, 0, :], cc("negtri"), ACT.Copy).then_inc(const_ready, 1)
            act.activation(tri[:, 1, :], cc("negone"), ACT.Copy).then_inc(const_ready, 1)
            act.activation(maskSB, cc("maskS"), ACT.Copy).then_inc(const_ready, 1)
            act.activation(maskCB, cc("maskC"), ACT.Copy).then_inc(const_ready, 1)
            for n, f in (("ff1_post", 0.5), ("ff2_post", 0.5), ("subln", 1.0 - LAMBDA_INIT)):
                w = dict(PARAMS)[n]
                act.activation(pc(n, 0, w), pc(n, 0, w), ACT.Copy, scale=f).then_inc(const_ready, 1)

            def one_square(name, n, src):
                i = NORM[name]
                if 8 * i + n - 1 > 0:
                    act.wait_ge(sumsq, 8 * i + n - 1)
                act.activation(sq[n % 2], src[:, n, :], ACT.Square).then_inc(squared, 1)

            def squares(name, src, ready, base):
                for n in range(KT):
                    act.wait_ge(ready, base + (n + 1))
                    one_square(name, n, src)

            def square_and_high(name, n):
                one_square(name, n, xf)
                act.activation(xH[:, n, :], xf[:, n, :], ACT.Copy, scale=pc(name, n)).then_inc(x_high, 1)

            def inverse_std(name, bank, eps):
                i = NORM[name]
                act.wait_ge(sumsq, 8 * i + 8)
                if DIVIDING[name]:
                    act.wait_ge(normed, 8 * DIVIDING[name])
                act.activation(rstd[:], ps[bank][:], ACT.Ln, bias=cc("eps", 2)[:, eps:eps + 1]).then_inc(log_ready, 1)
                act.wait_ge(log_ready, i + 1)
                act.activation(rstd[:], rstd[:], ACT.Exp, scale=-0.5).then_inc(rstd_ready, 1)

            def layer_norm(name, src, g, b):
                li = LNORM.index(name)
                if name == "mix0":
                    p_parts(0)
                if name == "mix1":
                    p_parts(1)
                act.preload_act_table_set("natural_log_exp_and_others")
                squares(name, src, centered, 8 * li)
                inverse_std(name, 1, 0)
                if name == "conf":
                    act.preload_act_table(ACT.Silu)
                for n in range(KT + 2):
                    if name == "ffn1":
                        if n < KT:
                            act.wait_ge(normed, 8 * DIVIDING[name] + n + 1)
                            act.activation(src[:, n, :], src[:, n, :], ACT.Identity, bias=pc(b, n))\
                                .then_inc(affine, 2)
                        if 1 <= n <= KT:
                            act.wait_ge(affine, 16 * li + 2 * n)
                            square_and_high("ff1_pre", n - 1)
                        continue
                    if name != "conf":
                        if n < KT:
                            act.wait_ge(normed, 8 * DIVIDING[name] + n + 1)
                            act.activation(xH[:, n, :], src[:, n, :], ACT.Identity, bias=pc(b, n)).then_inc(x_high, 1)
                        if n >= 2:
                            act.wait_ge(x_ready, 8 * XV[name] + n - 1)
                            act.activation(src[:, n - 2, :], src[:, n - 2, :], ACT.Identity, bias=pc(b, n - 2))\
                                .then_inc(affine, 2)
                        continue
                    if n < KT:
                        act.wait_ge(normed, n + 1)
                        act.activation(src[:, n, :], src[:, n, :], ACT.Silu, scale=pc(g, n), bias=pc(b, n))\
                            .then_inc(affine, 1)
                        act.wait_ge(affine, 2 * n + 1)
                        act.activation(cH[:, n, :], src[:, n, :], ACT.Copy).then_inc(affine, 1)

            def ple(layer):
                c0 = CHUNK[f"ple{layer}"]
                act.preload_act_table(ACT.Sigmoid)
                for i, (kind, n) in enumerate(PLE_ORDER):
                    act.wait_ge(chunk_done, c0 + i + 1)
                    if kind == "gate":
                        if n >= 4:
                            act.wait_ge(ple_free, KT * layer + n - 3)
                        act.activation(tmp[:, n % 4, :], ps[n % 4][:], ACT.Sigmoid).then_inc(ple_sig, 1)
                    high_after(c0 + i)

            def p_parts(layer):
                act.wait_ge(p_loaded, 16 * layer + 16)
                for k in range(2):
                    act.activation(pH[:, k, :], pf[:, k, :], ACT.Copy).then_inc(p_high, 1)

            def ffn(inst):
                c0 = CHUNK[f"gateup{inst}"]
                act.preload_act_table(ACT.Silu)
                with act.Fori(0, FT // 2) as t:
                    for j in range(2):
                        f = t * 2 + j
                        high_after(c0 + 2 * j, t)
                        if inst < 2:
                            act.wait_ge(h_made, t * 2 + (24 * inst + j + 1))
                            act.activation(tmp[:, j, :], ps[2 * j][:], ACT.Identity,
                                           scale=pc(f"fcw{inst}", f * FCONV_W + 2), bias=pc(f"fcb{inst}", f))\
                                .then_inc(tap2, 1)
                            act.wait_ge(tap10, t * 4 + (2 * FT * inst + 2 * j + 2))
                            act.activation(tmp[:, j, :], tmp[:, j, :], ACT.Silu).then_inc(gate_act, 1)
                        else:
                            act.wait_ge(gate_scaled, t * 2 + (FT * (inst - 2) + j + 1))
                            act.activation(tmp[:, j, :], tmp[:, j, :], ACT.Silu).then_inc(gate_act, 1)
                        high_after(c0 + 2 * j + 1, t)
                        act.wait_ge(h_made, t * 2 + (24 * inst + 2 + j + 1))
                        act.activation(hH[:, bass.ds(f, 1), :].rearrange("p o t -> p (o t)"), tmp[:, 2 + j, :],
                                       ACT.Copy).then_inc(h_high, 1)
                highs(f"down{inst}")

            act.preload_act_table(ACT.Sigmoid)
            with act.Fori(0, KT // 2) as t:
                for j in range(2):
                    act.wait_ge(conv_done, t * 2 + (j + 1))
                    for tap in range(PE_TAPS):
                        act.activation(diag[:, j, tap, :], cc("ident"), ACT.Copy,
                                       scale=pc("dw_w", t * (2 * CONV_W) + (CONV_W * j + tap))).then_inc(diag_ready, 1)
                    high_after(2 * j, t)
                    act.wait_ge(glu_banks_free, t * 2 + (j + 1))
                    act.activation(sq[j], ps[2 * j][:], ACT.Sigmoid, bias=pc("pw1_bg", t * 2 + j)).then_inc(glu_sig, 1)
                    high_after(2 * j + 1, t)
            layer_norm("conf", tmp, "aln_g", "aln_b")
            highs("pw2")
            layer_norm("mix0", xf, "mix_g0", "mix_b0")
            ple(0)
            ffn(0)
            layer_norm("ffn0", xf, "ffn_g0", "ffn_b0")

            def copy_qkv(p, j, which):
                act.wait_ge(chunk_done, CHUNK["qkv"] + 3 * p + which + 1)
                if which == 0:
                    act.activation(qT[:, j, :], ps[7][:], ACT.Copy, scale=DH ** -0.5).then_inc(qkv_copied, 1)
                elif which == 1:
                    act.activation(kT[:, j, :], ps[6][:], ACT.Copy).then_inc(qkv_copied, 1)
                else:
                    act.activation(vT[:], ps[7][:], ACT.Copy).then_inc(qkv_copied, 1)
                high_after(CHUNK["qkv"] + 3 * p + which)
                act.wait_ge(qkv_copied, p * 4 + (which + 1))
                act.sem_inc(q_free, 1)

            def copy_values(p, j):
                act.wait_ge(vt_ready, p + 1)
                act.activation(vN[:, j, :, :].rearrange("p a b -> p (a b)"), ps[7][:], ACT.Copy).then_inc(qkv_copied, 1)
                act.wait_ge(qkv_copied, p * 4 + 4)
                act.sem_inc(q_free, 1)

            def softplus_log(p, h, first):
                act.wait_ge(z_ready, p * 2 + (h + 1))
                if not first:
                    act.wait_ge(sp_low, p * 2 + (h - 1))
                for b, off, w in BANKS3:
                    act.activation(lg[:, h, off:off + w], ps[3 * h + b][:, 0:w], ACT.Abs).then_inc(abs_ready, 1)
                act.wait_ge(abs_ready, p * 6 + (3 * h + 3))
                act.activation(lg[:, h, :], lg[:, h, :], ACT.Exp, scale=-1.0).then_inc(e_ready, 1)

            def softplus_end(p, h):
                act.wait_ge(e_ready, p * 2 + (h + 1))
                act.activation(lg[:, h, :], lg[:, h, :], ACT.Ln, bias=1.0).then_inc(ln_ready, 1)

            def softplus_high(p, h):
                act.wait_ge(sp_ready, p * 6 + (3 * h + 3))
                act.activation(spH[:, h, :], lg[:, h, :], ACT.Copy).then_inc(sp_high, 1)

            def probabilities(p, h, first):
                act.wait_ge(cum_ready, p * 2 + (h + 1))
                if not first:
                    act.wait_ge(av_ready, p * 2 + (h - 1))
                for b, off, w in BANKS3:
                    act.activation(aT[:, h, off:off + w], ps[3 * h + b][:, 0:w], ACT.Exp).then_inc(a_ready, 1)

            def pair(p, j, more, first=False):
                softplus_log(p, 0, first)
                softplus_end(p, 0)
                softplus_log(p, 1, first)
                softplus_high(p, 0)
                softplus_end(p, 1)
                if more:
                    copy_qkv(p + 1, 1 - j, 0)
                softplus_high(p, 1)
                if more:
                    copy_qkv(p + 1, 1 - j, 1)
                probabilities(p, 0, first)
                probabilities(p, 1, first)
                if more:
                    copy_qkv(p + 1, 1 - j, 2)
                act.wait_ge(av_ready, p * 2 + 2)
                act.activation(mH[:, bass.ds(p, 1), :].rearrange("p o t -> p (o t)"), ps[6][:], ACT.Copy)\
                    .then_inc(m_high, 1)
                if more:
                    copy_values(p + 1, 1 - j)

            act.sem_inc(q_free, 1)
            for which in range(3):
                copy_qkv(0, 0, which)
            copy_values(0, 0)
            for p in range(KT):
                pair(p, p % 2, p < KT - 1, first=p == 0)

            highs("wo")
            act.wait_ge(m_ready, KT)
            load_p(1)
            layer_norm("mix1", xf, "mix_g1", "mix_b1")
            ple(1)
            ffn(1)
            layer_norm("ffn1", xf, "ffn_g1", "ffn_b1")

            def pre_norm(name, base):
                for n in range(KT):
                    act.wait_ge(updated, base + n + 1)
                    square_and_high(name, n)
                inverse_std(name, 5, 1)

            def post_norm(name):
                act.preload_act_table_set("natural_log_exp_and_others")
                squares(name, tmp, src_ready, 8 * SRC[name])
                inverse_std(name, 1, 1)

            inverse_std("ff1_pre", 5, 1)
            ffn(2)
            act.wait_ge(chunk_done, CHUNK["down2"] + FT)
            act.dma_start(ropeT[:].rearrange("p a t -> p (a t)"), rope).then_inc(rope_loaded, 16)
            for kv in range(2):
                act.dma_start(w1b[:, kv, :], w1[kv]).then_inc(w1_loaded, 16)
            post_norm("ff1_post")
            pre_norm("mix_pre", 0)

            c0 = CHUNK["hybrid"]

            def take_second(i):
                kind, name, h = ITEMS[i]
                if kind in ("turn", "gate"):
                    act.wait_ge(second_done, SECONDS.index(("second", i)) + 1)
                    if kind == "gate":
                        act.activation(gN[:], ps[7][:].rearrange("p (q g) -> p q g", q=QT)[:, :, 0:24], ACT.Sigmoid)\
                            .then_inc(b7_read, 1)
                    else:
                        dst = {"vs": vsN[:], "vw": vwN[:], "dv": dvN[:, h % 2, :, :]}[name]
                        act.activation(dst, ps[7][:].rearrange("p (q g) -> p q g", q=QT), ACT.Copy)\
                            .then_inc(b7_read, 1)

            def item(i):
                high_after(c0 + i)
                take_second(i)

            for i in range(7):
                item(i)
            act.wait_ge(lam_steps, 2)
            act.activation(st[:, 130:132], st[:, 128:130], ACT.Exp).then_inc(lam_steps, 1)
            act.wait_ge(hid_psum, 1)
            act.activation(hid[0:2 * NC, :], ps[5][0:2 * NC, :], ACT.Gelu_apprx_tanh).then_inc(hid_ready, 1)
            item(7)
            act.wait_ge(hid_psum, 2)
            act.activation(hidT[:].rearrange("p k c -> p (k c)"), ps[3][:, 0:8 * NC], ACT.Copy).then_inc(hid_ready, 1)
            item(8)
            act.wait_ge(hid_psum, 3)
            act.activation(vcC[0:NC, :], ps[5][0:NC, 0:P], ACT.Copy).then_inc(hid_ready, 1)
            act.activation(kcC[:, 0:NC], ps[4][:, 0:NC], ACT.Copy).then_inc(hid_ready, 1)
            item(9)

            def exps(u, m):
                act.wait_ge(max_ready, 8 * u + 4 * m + 4)
                for t in range(QT):
                    qt = QT - 1 - t
                    o, f = TILE_COL[t], TILE_OFF[t]
                    act.activation(prob[:, m, f:f + TILE_W[t]], ps[3 * m + TILE_BANK[t]][:, o:o + TILE_W[t]], ACT.Exp,
                                   bias=st[:, 4 * m + qt:4 * m + qt + 1],
                                   accum_out=st[:, 8 + 4 * m + qt:9 + 4 * m + qt]).then_inc(p_exp, 1)

            def copy_turned(m, n):
                act.wait_ge(turned, n)
                for b, off, w in BANKS3:
                    act.activation(AT[:, m, off:off + w], ps[3 * m + b][:, 0:w], ACT.Copy).then_inc(at_ready, 1)

            def copy_output(u):
                act.wait_ge(o_ready, u + 1)
                if u < DIFF_HEADS:
                    act.activation(oN[:, :, u * P:u * P + P], ps[6][:].rearrange("p (q d) -> p q d", q=QT), ACT.Copy)\
                        .then_inc(o_copied, 1)
                else:
                    c = DIFF_HEADS * P + (u - DIFF_HEADS) * DH
                    act.activation(oN[:, :, c:c + DH], ps[6][:, 0:QT * DH].rearrange("p (q d) -> p q d", q=QT),
                                   ACT.Copy).then_inc(o_copied, 1)

            for h in range(DIFF_HEADS):
                beside = BESIDE[h]
                high_after(c0 + beside[0])
                if h:
                    act.wait_ge(turned, h)
                exps(h, 0)
                exps(h, 1)
                high_after(c0 + beside[1])
                if h:
                    copy_output(h - 1)
                for i in beside[2:]:
                    high_after(c0 + i)
                copy_turned(0, h + 1)
                for i in beside[2:]:
                    take_second(i)
            for j in range(4):
                act.wait_ge(cmp_steps, 4 * j + 3)
                act.activation(pc_n[:], pc_n[:], ACT.Exp).then_inc(cmp_exp, 1)
                for g in range(2):
                    u = DIFF_HEADS + 2 * j + g
                    v = u - DIFF_HEADS
                    act.wait_ge(turned, DIFF_HEADS + 2 * v)
                    exps(u, 0)
                    exps(u, 1)
                    copy_output(u - 1)
                    if g == 0 and j in (1, 2):
                        item(20 + j)
                    act.wait_ge(second_done, SECONDS.index(("cmp_turn", j, g)) + 1)
                    act.activation(pcT[0:NC, :, :].rearrange("p q d -> p (q d)"), ps[7][0:NC, :], ACT.Copy)\
                        .then_inc(b7_read, 1)
                    copy_turned(0, DIFF_HEADS + 2 * v + 1)
            copy_output(NUNITS - 1)
            act.wait_ge(head_sq, 2)
            act.activation(st[:, 48:64], st[:, 32:48], ACT.Sqrt, scale=1.0 / P, bias=cc("eps", 2)[:, 1:2])\
                .then_inc(head_std, 1)
            for n in range(KT):
                act.wait_ge(o_turned, n + 1)
                act.activation(xH[:, n, :], ps[n][:], ACT.Copy, scale=pc("subln") if n < DIFF_HEADS else 1.0)\
                    .then_inc(x_high, 1)
            highs("wout")
            post_norm("mix_post")
            pre_norm("ff2_pre", 8)
            ffn(3)
            post_norm("ff2_post")

        @block.vector
        def _(dve):
            def low_part(n):
                dve.tensor_tensor(xL[:, n, :], xf[:, n, :], fp(xH[:, n, :]), ALU.subtract).then_inc(x_ready, 1)

            dve.memset(gpad[:, :, 0:CONV_W - 1], 0.0).then_inc(glu_pad, 1)
            dve.wait_ge(in_loaded, 32)
            for n in range(KT):
                dve.wait_ge(x_high, n + 1)
                low_part(n)
            dve.sem_inc(glu_banks_free, 2)

            def take_banks(name, fn):
                for n in range(KT):
                    if n < 7:
                        dve.wait_ge(bank_done, 7 * FULL[name] + n + 1)
                    else:
                        dve.wait_ge(chunk_done, CHUNK[name] + dict(COUNTS)[name])
                    fn(n)

            def add_residual(n):
                dve.tensor_tensor(xf[:, n, :], ps[n][:], xf[:, n, :], ALU.add).then_inc(src_ready, 1)

            def normalise(name, dst, src, finish, lag, g=None):
                dve.wait_ge(rstd_ready, NORM[name] + 1)
                for n in range(KT + lag):
                    if n < KT and g:
                        dve.scalar_tensor_tensor(dst[:, n, :], src[:, n, :], pc(g, n), rstd[:], ALU.mult,
                                                 ALU.mult).then_inc(normed, 1)
                    elif n < KT:
                        dve.tensor_tensor(dst[:, n, :], src[:, n, :], rstd[:], ALU.mult).then_inc(normed, 1)
                    if n >= lag:
                        finish(n - lag)

            def pre_low(name, n):
                dve.wait_ge(x_high, 8 * XH[name] + n + 1)
                dve.scalar_tensor_tensor(xL[:, n, :], xf[:, n, :], pc(name, n), fp(xH[:, n, :]), ALU.mult,
                                         ALU.subtract).then_inc(x_ready, 1)

            def layer_norm(name, src, g=None, b=None):
                if name != "conf":
                    g, b = f"{name[:3]}_g{name[3]}", f"{name[:3]}_b{name[3]}"
                li = LNORM.index(name)
                dve.wait_ge(mean_ready, li + 1)
                for n in range(KT):
                    dve.tensor_tensor(src[:, n, :], src[:, n, :], ps[0][:], ALU.subtract).then_inc(centered, 1)

                def finish(n):
                    if name == "ffn1":
                        pre_low("ff1_pre", n)
                    elif name == "conf":
                        dve.wait_ge(affine, 2 * n + 2)
                        dve.tensor_tensor(cL[:, n, :], src[:, n, :], fp(cH[:, n, :]), ALU.subtract).then_inc(c_ready, 1)
                    else:
                        dve.wait_ge(x_high, 8 * XH[name] + n + 1)
                        dve.scalar_tensor_tensor(xL[:, n, :], src[:, n, :], pc(b, n), fp(xH[:, n, :]), ALU.add,
                                                 ALU.subtract).then_inc(x_ready, 1)
                normalise(name, src, src, finish, 3 if name == "ffn1" else 2, g)

            def ple(layer):
                for k in range(2):
                    dve.wait_ge(p_high, 2 * layer + k + 1)
                    i = dve.tensor_tensor(pL[:, k, :], pf[:, k, :], fp(pH[:, k, :]), ALU.subtract)
                    if k == 1:
                        i.then_inc(p_ready, 1)

            def ple_tiles(layer):
                for n in range(KT):
                    dve.wait_ge(ple_sig, KT * layer + n + 1)
                    dve.wait_ge(chunk_done, CHUNK[f"ple{layer}"] + PLE_ORDER.index(("proj", n // 4)) + 1)
                    g_n = tmp[:, n % 4, :]
                    dve.tensor_tensor(g_n, ps[4 + n % 4][:], g_n, ALU.mult).then_inc(ple_mul, 1)
                    if n == 0:
                        dve.wait_ge(affine, 16 * LNORM.index(f"mix{layer}") + 16)
                    dve.wait_ge(ple_mul, KT * layer + n + 1)
                    dve.scalar_tensor_tensor(xf[:, n, :], xf[:, n, :], ALPHA, g_n, ALU.mult, ALU.add)\
                        .then_inc(ple_free, 1)
                dve.wait_ge(ple_free, KT * layer + KT)

            def ffn(inst):
                c0 = CHUNK[f"gateup{inst}"]
                dve.sem_inc(h_made, 2)
                if inst >= 2:
                    dve.wait_ge(rstd_ready, NORM[("ff1_pre", "ff2_pre")[inst - 2]] + 1)
                with dve.Fori(0, FT // 2) as t:
                    for j in range(2):
                        f = t * 2 + j
                        if inst < 2:
                            dve.wait_ge(tap2, t * 2 + (FT * inst + j + 1))
                            for tap in (1, 0):
                                back = FCONV_W - 1 - tap
                                dve.scalar_tensor_tensor(tmp[:, j, back:S], ps[2 * j][:, 0:S - back],
                                                         pc(f"fcw{inst}", f * FCONV_W + tap), tmp[:, j, back:S],
                                                         ALU.mult, ALU.add).then_inc(tap10, 1)
                                if tap == 1:
                                    dve.wait_ge(tap10, t * 4 + (2 * FT * inst + 2 * j + 1))
                        else:
                            dve.wait_ge(chunk_done, t * 4 + (c0 + 2 * j + 1))
                            dve.wait_ge(h_made, t * 2 + (24 * inst + j + 1))
                            dve.tensor_tensor(tmp[:, j, :], ps[2 * j][:], rstd[:], ALU.mult).then_inc(gate_scaled, 1)
                        dve.wait_ge(gate_act, t * 2 + (FT * inst + j + 1))
                        dve.wait_ge(chunk_done, t * 4 + (c0 + 2 * j + 2))
                        dve.tensor_tensor(tmp[:, 2 + j, :], ps[2 * j + 1][:], tmp[:, j, :], ALU.mult).then_inc(h_made, 1)
                        dve.wait_ge(h_high, t * 2 + (FT * inst + j + 1))
                        dve.tensor_tensor(hL[:, bass.ds(f, 1), :].rearrange("p o t -> p (o t)"), tmp[:, 2 + j, :],
                                          fp(hH[:, bass.ds(f, 1), :].rearrange("p o t -> p (o t)")), ALU.subtract)\
                            .then_inc(h_ready, 1)

            dve.wait_ge(glu_pad, 1)
            dve.sem_inc(conv_free, 2)
            with dve.Fori(0, KT // 2) as t:
                for j in range(2):
                    n = t * 2 + j
                    conv = tmp[:, bass.ds(n, 1), :].rearrange("p o t -> p (o t)")
                    dve.wait_ge(glu_sig, t * 2 + (j + 1))
                    dve.wait_ge(chunk_done, t * 4 + (2 * j + 2))
                    dve.scalar_tensor_tensor(gpad[:, j, CONV_W - 1:], ps[2 * j + 1][:], pc("pw1_ba", n), sq[j],
                                             ALU.add, ALU.mult).then_inc(glu_banks_free, 1)
                    dve.wait_ge(glu_banks_free, t * 2 + (j + 3))
                    for tap in range(PE_TAPS, CONV_W):
                        i = tap - PE_TAPS
                        w = pc("dw_w", n * CONV_W + tap)
                        dst = (conv, rstd[:])[i % 2]
                        if i >= 2:
                            dve.wait_ge(taps, t * (2 * DVE_STEPS) + (DVE_STEPS * j + i - 1))
                        elif i == 1:
                            dve.wait_ge(taps, t * (2 * DVE_STEPS) + (DVE_STEPS * j + 1))
                        if i == 0:
                            ins = dve.tensor_scalar(dst, gpad[:, j, tap:tap + S], w, pc("dw_b", n), ALU.mult, ALU.add)
                        elif i == 1:
                            ins = dve.tensor_scalar(dst, gpad[:, j, tap:tap + S], w, None, ALU.mult)
                        else:
                            ins = dve.scalar_tensor_tensor(dst, gpad[:, j, tap:tap + S], w, dst, ALU.mult, ALU.add)
                        ins.then_inc(taps, 1)
                    dve.wait_ge(taps, t * (2 * DVE_STEPS) + (DVE_STEPS * j + DVE_STEPS - 1))
                    dve.tensor_tensor(conv, conv, rstd[:], ALU.add).then_inc(taps, 1)
                    dve.wait_ge(taps, t * (2 * DVE_STEPS) + (DVE_STEPS * j + DVE_STEPS))
                    dve.wait_ge(conv_done, n + 3)
                    dve.tensor_tensor(conv, conv, ps[4 + j][:], ALU.add).then_inc(conv_free, 1)
                    dve.wait_ge(conv_free, n + 3)
                    dve.sem_inc(src_ready, 1)
            layer_norm("conf", tmp)
            for n in range(KT):
                dve.tensor_scalar(xf[:, n, :], xf[:, n, :], ALPHA, pc("pw2_b", n), ALU.mult, ALU.add).then_inc(res_scaled, 1)
            dve.wait_ge(res_scaled, KT)
            take_banks("pw2", add_residual)
            ple(0)
            layer_norm("mix0", xf)
            ple_tiles(0)
            ffn(0)
            take_banks("down0", add_residual)
            layer_norm("ffn0", xf)

            dve.wait_ge(affine, 16 * LNORM.index("ffn0") + 16)
            for n in range(KT):
                dve.tensor_scalar(xf[:, n, :], xf[:, n, :], ALPHA, None, ALU.mult).then_inc(res_scaled, 1)

            def softplus(p, h):
                dve.wait_ge(ln_ready, p * 2 + (h + 1))
                for b, off, w in BANKS3:
                    dve.scalar_tensor_tensor(lg[:, h, off:off + w], ps[3 * h + b][:, 0:w], 0.0, lg[:, h, off:off + w],
                                             ALU.max, ALU.add).then_inc(sp_ready, 1)

            def softplus_low(p, h):
                dve.wait_ge(sp_high, p * 2 + (h + 1))
                dve.tensor_tensor(spL[:, h, :], lg[:, h, :], fp(spH[:, h, :]), ALU.subtract).then_inc(sp_low, 1)

            def pair(p):
                softplus(p, 0)
                softplus_low(p, 0)
                softplus(p, 1)
                softplus_low(p, 1)
                dve.wait_ge(m_high, p + 1)
                m = bass.ds(p, 1)
                dve.tensor_tensor(mL[:, m, :].rearrange("p o t -> p (o t)"), ps[6][:],
                                  fp(mH[:, m, :].rearrange("p o t -> p (o t)")), ALU.subtract).then_inc(m_ready, 1)

            with dve.Fori(0, KT) as p:
                pair(p)
            dve.wait_ge(res_scaled, 2 * KT)
            take_banks("wo", add_residual)
            ple(1)
            layer_norm("mix1", xf)
            ple_tiles(1)
            ffn(1)
            take_banks("down1", add_residual)
            layer_norm("ffn1", xf)

            def copy_product(n):
                dve.tensor_copy(tmp[:, n, :], ps[n][:]).then_inc(src_ready, 1)

            def scale_product(n):
                dve.tensor_tensor(tmp[:, n, :], ps[n][:], rstd[:], ALU.mult).then_inc(src_ready, 1)

            def post_norm(name, following=None):
                dve.wait_ge(rstd_ready, NORM[name] + 1)
                for n in range(KT + 3):
                    if n < KT:
                        dve.tensor_tensor(tmp[:, n, :], tmp[:, n, :], rstd[:], ALU.mult).then_inc(normed, 1)
                    if 1 <= n <= KT:
                        dve.wait_ge(normed, 8 * DIVIDING[name] + n)
                        dve.scalar_tensor_tensor(xf[:, n - 1, :], tmp[:, n - 1, :], pc(name, n - 1), xf[:, n - 1, :],
                                                 ALU.mult, ALU.add).then_inc(updated, 1)
                    if n >= 3 and following:
                        pre_low(following, n - 3)

            ffn(2)
            take_banks("down2", scale_product)
            post_norm("ff1_post", "mix_pre")
            dve.wait_ge(rstd_ready, NORM["mix_pre"] + 1)

            lam = pc("lams", 0, 4 * DH).rearrange("p (a b d) -> p a b d", a=2, b=2)
            dve.tensor_tensor(st[:, 0:2 * DH].rearrange("p (a d) -> p a d", a=2), lam[:, :, 0, :], lam[:, :, 1, :],
                              ALU.mult).then_inc(lam_steps, 1)
            dve.wait_ge(lam_steps, 1)
            dve.tensor_reduce(st[:, 128:130], st[:, 0:2 * DH].rearrange("p (a d) -> p a d", a=2), AX_X, ALU.add)\
                .then_inc(lam_steps, 1)

            hybrid0 = CHUNK["hybrid"]

            def take_item(i):
                kind, name, h = ITEMS[i]
                dve.wait_ge(chunk_done, hybrid0 + i + 1)
                if kind == "copy":
                    dve.tensor_tensor(kcvc[:, i, :], ps[7 - i][:], rstd[:], ALU.mult).then_inc(b7_read, 1)
                elif kind == "rope":
                    r = ROPES.index(i)
                    if r >= 2:
                        dve.wait_ge(roped, r - 1)
                    dve.scalar_tensor_tensor(pre[:, r % 2, :], ps[7][:], DH ** -0.5 if name in ("dq", "nq") else 1.0,
                                             rstd[:], ALU.mult, ALU.mult).then_inc(b7_read, 1)
                else:
                    dve.tensor_tensor(vturn0[:], ps[7][:], rstd[:], ALU.mult).then_inc(b7_read, 1)

            def finish_item(i):
                kind, name, h = ITEMS[i]
                if kind == "copy":
                    dve.wait_ge(swapped, i + 1)
                    blk = (blk_k, blk_v)[i]
                    for odd in range(2):
                        r = slice(DH * odd, DH * odd + DH)
                        for g in range(2):
                            src = kcvc[r, i, :] if g == odd else ps[3 + i][r, :]
                            src = src.rearrange("p (c s two) -> p s c two", s=8, two=2)
                            for half in range(2):
                                pe_ = par[r, PCOL[("pe_k", "pe_v")[i]] + 8 * half:][:, 0:8]\
                                    .unsqueeze(2).broadcast_to([DH, 8, NC])
                                ins = dve.tensor_tensor(blk[r, 8 * half:8 * half + 8, g, :],
                                                        src[:, :, half:half + NC, odd], pe_, ALU.add)
                    ins.then_inc(blocks_ready, 1)
                elif kind == "rope":
                    r = ROPES.index(i)
                    dst = {"ks": ksT[:], "kw": kwT[:], "dq": dqT[:, h % 2, :], "dk": dkT[:, h % 2, :],
                           "nq": nqT[:, h % 2, :]}[name]
                    if r == 0:
                        dve.wait_ge(rope_loaded, 16)
                    else:
                        dve.wait_ge(roped, r)
                    dve.wait_ge(second_done, SECONDS.index(("second", i)) + 1)
                    dve.tensor_tensor(rot, ps[7][:], ropeT[:, 1, :], ALU.mult).then_inc(b7_read, 1)
                    dve.tensor_tensor(pre[:, r % 2, :], pre[:, r % 2, :], ropeT[:, 0, :], ALU.mult)\
                        .then_inc(rot_ready, 1)
                    dve.wait_ge(rot_ready, r + 1)
                    dve.wait_ge(b7_read, USE["second", i] + 1)
                    dve.tensor_tensor(dst, pre[:, r % 2, :], rot, ALU.add).then_inc(roped, 1)

            def item(i):
                take_item(i)
                finish_item(i)

            take_item(0)
            take_item(1)
            item(2)
            finish_item(0)
            finish_item(1)
            for i in range(3, 7):
                item(i)
            dve.wait_ge(lam_steps, 3)
            dve.scalar_tensor_tensor(st[:, 132:133], st[:, 131:132], -LAMBDA_INIT, st[:, 130:131], ALU.add,
                                     ALU.subtract).then_inc(lam_steps, 1)
            for i in range(7, 10):
                item(i)

            def maxima(u, m):
                dve.wait_ge(s_ready, 2 * u + m + 1)
                for t in range(QT):
                    qt = QT - 1 - t
                    o = TILE_COL[t]
                    dve.tensor_reduce(st[:, 4 * m + qt:4 * m + qt + 1], ps[3 * m + TILE_BANK[t]][:, o:o + TILE_W[t]],
                                      AX_X, ALU.max, negate=True).then_inc(max_ready, 1)

            for h in range(DIFF_HEADS):
                item(BESIDE[h][0])
                if h:
                    dve.wait_ge(p_exp, 8 * h)
                maxima(h, 0)
                maxima(h, 1)
                item(BESIDE[h][1])
                dve.wait_ge(p_exp, 8 * h + 8)
                if h:
                    dve.wait_ge(p_ready2, QT * h)
                dve.reciprocal(st[:, 16:24], st[:, 8:16]).then_inc(coef_ready, 1)
                if h == 0:
                    dve.wait_ge(lam_steps, 4)
                dve.wait_ge(coef_ready, 2 * h + 1)
                dve.tensor_scalar(st[:, 24:28], st[:, 20:24], st[:, 132:133], None, ALU.mult).then_inc(coef_ready, 1)
                dve.wait_ge(coef_ready, 2 * h + 2)
                for t in range(QT):
                    qt = QT - 1 - t
                    f = slice(TILE_OFF[t], TILE_OFF[t] + TILE_W[t])
                    dve.tensor_scalar(prob[:, 1, f], prob[:, 1, f], st[:, 24 + qt:25 + qt], None, ALU.mult)\
                        .then_inc(scaled, 1)
                for t in range(QT):
                    qt = QT - 1 - t
                    f = slice(TILE_OFF[t], TILE_OFF[t] + TILE_W[t])
                    dve.wait_ge(scaled, QT * h + t + 1)
                    dve.scalar_tensor_tensor(prob[:, 0, f], prob[:, 0, f], st[:, 16 + qt:17 + qt], prob[:, 1, f],
                                             ALU.mult, ALU.add).then_inc(p_ready2, 1)
                for i in BESIDE[h][2:]:
                    item(i)
            def compressed_maxima(j):
                dve.wait_ge(second_done, SECONDS.index(("cmp_scores", j)) + 1)
                cadd = cc("cadd", QT * NC).rearrange("p (q c) -> p q c", q=QT)
                base = 4 * j
                for g in range(2):
                    i = dve.tensor_tensor(pc_n[:, g, :, :], ps[7 - g][:, 0:QT * NC]
                                          .rearrange("p (q c) -> p q c", q=QT), cadd, ALU.add)
                    i.then_inc(b7_read if g == 0 else cmp_steps, 1)
                dve.wait_ge(b7_read, USE["cmp_scores", j] + 1)
                dve.wait_ge(cmp_steps, base + 1)
                flatc = pc_n[:].rearrange("p g q c -> p (g q) c")
                dve.tensor_reduce(st[:, 64:72], flatc, AX_X, ALU.max).then_inc(cmp_steps, 1)
                dve.wait_ge(cmp_steps, base + 2)
                dve.tensor_tensor(flatc, flatc, st[:, 64:72].unsqueeze(2).broadcast_to([P, 8, NC]), ALU.subtract)\
                    .then_inc(cmp_steps, 1)

            def compressed_weights(j):
                cmul = cc("cmul", QT * NC).rearrange("p (q c) -> p q c", q=QT)
                flatc = pc_n[:].rearrange("p g q c -> p (g q) c")
                dve.wait_ge(cmp_exp, j + 1)
                dve.tensor_reduce(st[:, 72:80], flatc, AX_X, ALU.add).then_inc(cmp_sum, 1)
                dve.wait_ge(cmp_sum, 3 * j + 1)
                dve.reciprocal(st[:, 80:88], st[:, 72:80]).then_inc(cmp_sum, 1)
                dve.wait_ge(cmp_sum, 3 * j + 2)
                for g in range(2):
                    gate = gN[:, :, 3 * (4 * g + j)]
                    i = dve.tensor_tensor(st[:, 88 + 4 * g:92 + 4 * g], gate, st[:, 80 + 4 * g:84 + 4 * g], ALU.mult)
                    if g == 1:
                        i.then_inc(cmp_sum, 1)
                dve.wait_ge(cmp_sum, 3 * j + 3)
                for g in range(2):
                    i = dve.tensor_tensor(pc_n[:, g, :, :], pc_n[:, g, :, :], cmul, ALU.mult)
                    if g == 1:
                        i.then_inc(cmp_steps, 1)
                dve.wait_ge(cmp_steps, 4 * j + 4)
                dve.tensor_tensor(flatc, flatc, st[:, 88:96].unsqueeze(2).broadcast_to([P, 8, NC]), ALU.mult)\
                    .then_inc(cmp_ready, 1)

            compressed_maxima(0)
            for j in range(4):
                for g in range(2):
                    u = DIFF_HEADS + 2 * j + g
                    v = u - DIFF_HEADS
                    dve.wait_ge(p_exp, 8 * u)
                    maxima(u, 0)
                    maxima(u, 1)
                    if g == 0:
                        compressed_weights(j)
                    dve.wait_ge(p_exp, 8 * u + 8)
                    dve.wait_ge(p_ready2, QT * DIFF_HEADS + 8 * v)
                    dve.reciprocal(st[:, 16:24], st[:, 8:16]).then_inc(coef_ready, 1)
                    c = 2 * DIFF_HEADS + 2 * v
                    dve.wait_ge(coef_ready, c + 1)
                    for m in range(2):
                        i = dve.tensor_tensor(st[:, 24 + 4 * m:28 + 4 * m], gN[:, :, 3 * (4 * g + j) + 1 + m],
                                              st[:, 16 + 4 * m:20 + 4 * m], ALU.mult)
                    i.then_inc(coef_ready, 1)
                    dve.wait_ge(coef_ready, c + 2)
                    for m in range(2):
                        for t in range(QT):
                            qt = QT - 1 - t
                            f = slice(TILE_OFF[t], TILE_OFF[t] + TILE_W[t])
                            dve.tensor_scalar(prob[:, m, f], prob[:, m, f], st[:, 24 + 4 * m + qt:25 + 4 * m + qt],
                                              None, ALU.mult).then_inc(p_ready2, 1)
                    if g == 0 and j in (1, 2):
                        item(20 + j)
                    dve.wait_ge(turned, DIFF_HEADS + 2 * v + 2)
                    if v:
                        dve.wait_ge(o_ready, u)
                    for b, off, w in BANKS3:
                        dve.tensor_copy(AT[:, 1, off:off + w], ps[3 + b][:, 0:w]).then_inc(at2_ready, 1)
                    if g == 1 and j < 3:
                        compressed_maxima(j + 1)
            heads = oN[:, :, 0:DIFF_HEADS * P].rearrange("p q (h d) -> p q h d", h=DIFF_HEADS)
            sqs = flat[:, 0:QT * DIFF_HEADS * P].rearrange("p (q h d) -> p q h d", q=QT, h=DIFF_HEADS)
            dve.wait_ge(turned, DIFF_HEADS + 16)
            for q in range(QT):
                i = dve.tensor_tensor(sqs[:, q], heads[:, q], heads[:, q], ALU.mult)
            i.then_inc(head_sq, 1)
            dve.wait_ge(head_sq, 1)
            dve.tensor_reduce(st[:, 32:48], flat[:, 0:QT * DIFF_HEADS * P].rearrange("p (a d) -> p a d", d=P), AX_X,
                              ALU.add).then_inc(head_sq, 1)
            dve.wait_ge(head_std, 1)
            dve.reciprocal(st[:, 96:112], st[:, 48:64]).then_inc(head_sq, 1)
            dve.wait_ge(head_sq, 3)
            for q in range(QT):
                for h in range(DIFF_HEADS):
                    k = 96 + q * DIFF_HEADS + h
                    dve.tensor_scalar(heads[:, q, h, :], heads[:, q, h, :], st[:, k:k + 1], None, ALU.mult)\
                        .then_inc(head_done, 1)
            for n in range(KT):
                dve.wait_ge(x_high, 8 * XH["mixer"] + n + 1)
                if n < DIFF_HEADS:
                    dve.scalar_tensor_tensor(xL[:, n, :], ps[n][:], pc("subln"), fp(xH[:, n, :]), ALU.mult,
                                             ALU.subtract).then_inc(x_ready, 1)
                else:
                    dve.tensor_tensor(xL[:, n, :], ps[n][:], fp(xH[:, n, :]), ALU.subtract).then_inc(x_ready, 1)
            take_banks("wout", copy_product)
            post_norm("mix_post", "ff2_pre")
            ffn(3)
            take_banks("down3", scale_product)
            post_norm("ff2_post")


def lay_out(inputs):
    import numpy as np
    a = {k: np.asarray(v) for k, v in inputs.items()}

    def by_output(w):
        n = w.shape[1] // P
        return w.reshape(KT, P, n, P).transpose(2, 1, 0, 3).reshape(n, P, KT * P)

    def by_k(w):
        return w.reshape(w.shape[0] // P, P, D)

    def mixed(*ws):
        return np.stack([by_output(w) for w in ws], axis=1).reshape(-1, P, KT * P)

    w_in = a["w_in_2"][0]
    sizes = [512, 512, 512, 512] + [128] * 6 + [24]
    at = np.concatenate([[0], np.cumsum(sizes)])
    dq, dk, dv, nq, kc, vc, ks, vs, kw, vw, gl = [w_in[:, at[i]:at[i + 1]] for i in range(11)]
    nq = nq.reshape(D, 2, 4, DH).transpose(0, 2, 1, 3).reshape(D, 512)
    gl = np.concatenate([gl, np.zeros((D, P - 24), np.float32)], axis=1)
    wo2 = a["w_out_2"][0]
    wo2 = np.concatenate([wo2[:512], wo2[512:].reshape(2, 4, DH, D).transpose(1, 0, 2, 3).reshape(512, D)], axis=0)
    parts = [mixed(a["a_pw1_w"][0][:, D:], a["a_pw1_w"][0][:, :D]), by_k(a["a_pw2_w"][0])]
    for l in range(2):
        if l == 1:
            parts += [mixed(a["b_wq"][0], a["kv_wk"], a["kv_wv"]), by_k(a["b_wo"][0])]
        gates = by_output(a["ple_w_gate"][l])
        proj = a["ple_w_proj"][l].reshape(2, P, 2, 4, P).transpose(2, 1, 3, 0, 4).reshape(2, P, 8 * P)
        parts += [np.stack([gates[n] if kind == "gate" else proj[n] for kind, n in PLE_ORDER]),
                  mixed(a["ffn_w_gate"][l], a["ffn_w_up"][l]), by_k(a["ffn_w_down"][l])]
    parts += [mixed(a["ff1_w_gate_2"][0], a["ff1_w_up_2"][0]), by_k(a["ff1_w_down_2"][0]), 
              *[by_output(w) for w in (kc, vc, ks, vs, kw, vw, gl)], mixed(dq, dk, dv), by_output(nq), by_k(wo2)]
    parts += [mixed(a["ff2_w_gate_2"][0], a["ff2_w_up_2"][0]), by_k(a["ff2_w_down_2"][0])]
    ws = np.concatenate(parts, axis=0)
    assert ws.shape[0] == NCHUNKS

    def col(v):
        return v.reshape(-1, P).T

    def taps(w):
        return w.reshape(w.shape[0], -1, P).transpose(2, 1, 0).reshape(P, -1)

    v = {"pw1_ba": col(a["a_pw1_b"][0][:D]), "pw1_bg": col(a["a_pw1_b"][0][D:]), "dw_w": taps(a["a_dw_w"][0]),
         "dw_b": col(a["a_dw_b"][0]), "aln_g": col(a["a_ln_g"][0]), "aln_b": col(a["a_ln_b"][0]),
         "pw2_b": col(a["a_pw2_b"][0])}
    for l in range(2):
        v[f"mix_g{l}"] = col(a["ln_mix_g"][l])
        v[f"mix_b{l}"] = col(a["ln_mix_b"][l])
        v[f"fcw{l}"] = taps(a["ffn_conv_w"][l])
        v[f"fcb{l}"] = col(a["ffn_conv_b"][l])
        v[f"ffn_g{l}"] = col(a["ln_ffn_g"][l])
        v[f"ffn_b{l}"] = col(a["ln_ffn_b"][l])
    for n, m in (("ff1_pre", "ff1_norm_pre_2"), ("ff1_post", "ff1_norm_post_2"), ("mix_pre", "mix_norm_pre_2"),
                 ("mix_post", "mix_norm_post_2"), ("ff2_pre", "ff2_norm_pre_2"), ("ff2_post", "ff2_norm_post_2")):
        v[n] = col(a[m][0])
    v["subln"] = col(a["diff_subln_2"][0])
    for n in "kv":
        v[f"pe_{n}"] = a[f"cmp_pe_{n}_2"][0].reshape(PAIRS, 2 * DH).T
    v["w2_k"] = a["cmp_k_w2_2"][0].reshape(2, P, DH).transpose(1, 0, 2).reshape(P, 2 * DH)
    v["w2_v"] = a["cmp_v_w2_2"][0].reshape(2, P, DH).transpose(1, 0, 2).reshape(P, 2 * DH)
    v["lams"] = np.tile(np.concatenate([a[f"lambda_{n}_2"][0] for n in ("q1", "k1", "q2", "k2")])[None], (P, 1))
    params = np.concatenate([v[n] for n, _ in PARAMS], axis=1)
    w1 = np.stack([a[f"cmp_{n}_w1_2"][0].reshape(PAIRS, P, CMP_HID).transpose(1, 0, 2).reshape(P, PAIRS * CMP_HID)
                   for n in "kv"])
    return {"ws": ws, "xT": np.ascontiguousarray(a["x"][0].T),
            "pT": np.ascontiguousarray(a["p"][:, 0].transpose(0, 2, 1)), "params": params, "w1": w1}


def constants():
    import numpy as np
    i = np.arange(P)
    later = i[None, :] > i[:, None]
    c = {"ident": np.eye(P), "mean": np.full((P, P), 1.0 / D), "negtri": -(i[:, None] >= i[None, :]).astype(float),
         "negone": -np.ones((P, P)), "maskS": np.where(later, 0.0, NEG), "maskC": np.where(later, NEG, 0.0),
         "eps": np.tile(np.array([[LN_EPS, RMS_EPS]]), (P, 1))}
    d = i % DH
    partner = np.where(d < 8, i + 8, np.where(d < 16, i - 8, i))
    c["perm"] = (i[:, None] == partner[None, :]).astype(float)
    c["swap"] = (i[:, None] == (i[None, :] + DH) % P).astype(float)
    t = np.arange(S).reshape(QT, P)
    cend = np.arange(NC) * CMP_STRIDE + CMP_BLOCK - 1
    valid = cend[None, None, :] <= t.T[:, :, None]
    c["cadd"] = np.where(valid, 0.0, NEG).reshape(P, -1)
    c["cmul"] = valid.astype(float).reshape(P, -1)
    consts = np.concatenate([c[n] for n, _ in CONSTS], axis=1).astype(np.float32)
    inv = (500000.0 ** (-np.arange(0, 16, 2) / 16.0)).astype(np.float32)
    ang = (np.arange(S, dtype=np.float32)[None, :] * inv[:, None]).astype(np.float64)
    cos, sin = np.cos(ang), np.sin(ang)
    table = np.zeros((P, 2, S))
    table[:, 0] = 1.0
    for base in (0, DH):
        table[base:base + 8, 0] = cos
        table[base + 8:base + 16, 0] = cos
        table[base:base + 8, 1] = -sin
        table[base + 8:base + 16, 1] = sin
    return consts, table.reshape(P, 2 * S).astype(np.float32)


def kernel(**inputs):
    import numpy as np
    import concourse.bacc as bacc
    from concourse.bass_utils import run_bass_kernel_spmd as run

    arrays = lay_out(inputs)
    arrays["consts"], arrays["rope"] = constants()
    nc = bacc.Bacc("TRN2", target_bir_lowering=False, num_devices=1)
    names = ["ws", "xT", "pT", "params", "consts", "rope", "w1"]
    arrays = {n: np.ascontiguousarray(arrays[n]) for n in names}
    args = [nc.dram_tensor(n, arrays[n].shape, mybir.dt.from_np(arrays[n].dtype), kind="ExternalInput").ap()
            for n in names]
    out = nc.dram_tensor("out", (D, S), F32, kind="ExternalOutput").ap()
    build_block(nc, *args, out)
    r = run(nc, [arrays], core_ids=[0])
    return np.ascontiguousarray(r.results[0]["out"].T)[None]
```
